# Optimizing a Trainium2 kernel written in Bass

```python
import jax, jax.numpy as jnp
from jax import lax
import numpy as np

D_MODEL = 1024
BATCH = 1
SEQ = 256
DEPTH = 1
DEC_BATCH = 8
DEC_SEQ = 4
PAST_LEN = 2048
PAGE_SIZE = 128

D_MIX = D_MODEL
GLA_WIDTH = D_MIX // 2
GLA_HEADS = 4
GLA_DV = GLA_WIDTH // GLA_HEADS
GLA_KDIM = GLA_WIDTH // 2
GLA_DK = GLA_KDIM // GLA_HEADS
GLA_LOWRANK = 16
GLA_NORMALIZER = 16.0
HGRN_WIDTH = D_MIX - GLA_WIDTH
HGRN_EXPAND = 128
HGRN_HEADS = HGRN_WIDTH // HGRN_EXPAND
HGRN_DK = HGRN_EXPAND
HGRN_FDIM = HGRN_HEADS * HGRN_DK
HGRN_DV = HGRN_WIDTH // HGRN_HEADS
D_IN = 2 * GLA_KDIM + 2 * GLA_WIDTH + GLA_LOWRANK + 2 * HGRN_FDIM + 2 * HGRN_WIDTH
CHUNK = 64
N_EXPERTS = 32
TOP_K = 4
D_FF = D_MODEL
SWIGLU_LIMIT = 7.0
SWIGLU_ALPHA = 1.702
MOE_BLOCK = 128
PLE_DIM = 256
EPS = 1e-6

kernel_name = 'hymba_gla_hgrn2_moe_ple_step'

def rms_norm(x, g):
    xf = x.astype(jnp.float32)
    y = xf * lax.rsqrt(jnp.mean(xf * xf, axis=-1, keepdims=True) + EPS)
    return (y * g.astype(jnp.float32)).astype(x.dtype)

def head_rms_norm(o, g):
    return o * lax.rsqrt(jnp.mean(o * o, axis=-1, keepdims=True) + EPS) * g.astype(jnp.float32)

def chunk_gated_linear(q, k, v, log_a, s0, scale):
    B, L, H, DK = q.shape
    DV = v.shape[-1]
    C = CHUNK if L % CHUNK == 0 else L
    N = L // C
    f32 = jnp.float32
    q = q.astype(f32).reshape(B, N, C, H, DK) * scale
    k = k.astype(f32).reshape(B, N, C, H, DK)
    v = v.astype(f32).reshape(B, N, C, H, DV)
    b = lax.cumsum(log_a.astype(f32).reshape(B, N, C, H, DK), axis=2)
    b_last = b[:, :, -1]
    ref = b[:, :, C // 2][:, :, None]
    q_r = q * jnp.exp(b - ref)
    k_r = k * jnp.exp(ref - b)
    att = jnp.einsum('bnchk,bnshk->bnhcs', q_r, k_r)
    causal = jnp.tril(jnp.ones((C, C), dtype=bool))
    att = jnp.where(causal, att, 0.0)
    o_intra = jnp.einsum('bnhcs,bnshv->bnchv', att, v)
    k_end = k * jnp.exp(b_last[:, :, None] - b)
    u = jnp.einsum('bnchk,bnchv->bnhkv', k_end, v)

    def step(s, inp):
        decay, du = inp
        return decay[..., None] * s + du, s

    s_final, s_prev = lax.scan(step, s0.astype(f32),
                               (jnp.moveaxis(jnp.exp(b_last), 1, 0), jnp.moveaxis(u, 1, 0)))
    s_prev = jnp.moveaxis(s_prev, 0, 1)
    o_inter = jnp.einsum('bnchk,bnhkv->bnchv', q * jnp.exp(b), s_prev)
    return (o_inter + o_intra).reshape(B, L, H, DV), s_final

def parallel_mixers(a, s_gla, s_hgrn, lb, w_in, w_gk2, b_gk2, gn_gla, gn_hgrn, w_out):
    B, L, _ = a.shape
    f32 = jnp.float32
    z = a @ w_in
    splits = np.cumsum([GLA_KDIM, GLA_KDIM, GLA_WIDTH, GLA_WIDTH, GLA_LOWRANK,
                        HGRN_FDIM, HGRN_FDIM, HGRN_WIDTH]).tolist()
    q1, k1, v1, g1, r1, q2, f2, i2, g2 = jnp.split(z, splits, axis=-1)
    log_a = jax.nn.log_sigmoid((r1 @ w_gk2 + b_gk2).astype(f32)) / GLA_NORMALIZER
    o1, s1 = chunk_gated_linear(q1.reshape(B, L, GLA_HEADS, GLA_DK),
                                k1.reshape(B, L, GLA_HEADS, GLA_DK),
                                v1.reshape(B, L, GLA_HEADS, GLA_DV),
                                log_a.reshape(B, L, GLA_HEADS, GLA_DK),
                                s_gla, GLA_DK ** -0.5)
    o1 = head_rms_norm(o1, gn_gla) * jax.nn.silu(g1.astype(f32).reshape(B, L, GLA_HEADS, GLA_DV))
    forget = lb + (1.0 - lb) * jax.nn.sigmoid(f2.astype(f32))
    q2h = jax.nn.silu(q2.astype(f32))
    i2h = jax.nn.silu(i2.astype(f32))
    o2, s2 = chunk_gated_linear(q2h.reshape(B, L, HGRN_HEADS, HGRN_DK),
                                (1.0 - forget).reshape(B, L, HGRN_HEADS, HGRN_DK),
                                i2h.reshape(B, L, HGRN_HEADS, HGRN_DV),
                                jnp.log(forget).reshape(B, L, HGRN_HEADS, HGRN_DK),
                                s_hgrn, 1.0)
    o2 = head_rms_norm(o2, gn_hgrn) * jax.nn.sigmoid(g2.astype(f32).reshape(B, L, HGRN_HEADS, HGRN_DV))
    o = jnp.concatenate([o1.reshape(B, L, GLA_WIDTH), o2.reshape(B, L, HGRN_WIDTH)], axis=-1).astype(a.dtype)
    return o @ w_out, s1, s2

def moe(x, w_router, b_router, w_gu, b_gu, w_dn, b_dn):
    B, L, D = x.shape
    T = B * L
    TK = T * TOP_K
    f32 = jnp.float32
    xt = x.reshape(T, D)
    logits = (xt @ w_router + b_router).astype(f32)
    top_v, top_i = lax.top_k(logits, TOP_K)
    gates = jax.nn.softmax(top_v, axis=-1)
    flat_e = top_i.reshape(-1).astype(jnp.int32)
    order = jnp.argsort(flat_e).astype(jnp.int32)
    sorted_e = flat_e[order]
    counts = jnp.bincount(flat_e, length=N_EXPERTS).astype(jnp.int32)
    padded = (counts + MOE_BLOCK - 1) // MOE_BLOCK * MOE_BLOCK
    start = jnp.cumsum(counts) - counts
    pend = jnp.cumsum(padded)
    pstart = pend - padded
    rank = jnp.arange(TK, dtype=jnp.int32) - start[sorted_e]
    dest = pstart[sorted_e] + rank
    n_blocks = -(-TK // MOE_BLOCK) + N_EXPERTS
    R = n_blocks * MOE_BLOCK
    row_tok = jnp.full((R,), T, dtype=jnp.int32).at[dest].set(order // TOP_K)
    row_gate = jnp.zeros((R,), f32).at[dest].set(gates.reshape(-1)[order])
    block_rows = jnp.arange(n_blocks, dtype=jnp.int32) * MOE_BLOCK
    block_e = jnp.minimum(jnp.searchsorted(pend, block_rows, side='right'), N_EXPERTS - 1)
    x_pad = jnp.concatenate([xt, jnp.zeros((1, D), xt.dtype)], axis=0)
    xb = x_pad[row_tok].reshape(n_blocks, MOE_BLOCK, D)

    def expert_block(args):
        xblk, e = args
        gu = xblk @ w_gu[e] + b_gu[e]
        gate, up = jnp.split(gu, 2, axis=-1)
        gate = jnp.minimum(gate, SWIGLU_LIMIT)
        up = jnp.clip(up, -SWIGLU_LIMIT, SWIGLU_LIMIT)
        hid = (up + 1.0) * (gate * jax.nn.sigmoid(gate * SWIGLU_ALPHA))
        return hid @ w_dn[e] + b_dn[e]

    y = lax.map(expert_block, (xb, block_e)).reshape(R, D)
    out = jnp.zeros((T + 1, D), f32).at[row_tok].add(y.astype(f32) * row_gate[:, None])[:T]
    return out.reshape(B, L, D).astype(x.dtype)

def setup_inputs(seed: int = 0) -> dict:
    key = jax.random.key(seed)
    ks = jax.random.split(key, 25)
    f32 = jnp.float32

    def nrm(k, shape, scale):
        return jax.random.normal(k, shape, f32) * scale

    return {
        'x_prompt': nrm(ks[0], (BATCH, SEQ, D_MODEL), 1.0),
        'x_sample': nrm(ks[1], (DEC_BATCH, DEC_SEQ, D_MODEL), 1.0),
        'p_prompt': nrm(ks[2], (DEPTH, BATCH, SEQ, PLE_DIM), 1.0),
        'p_sample': nrm(ks[3], (DEPTH, DEC_BATCH, DEC_SEQ, PLE_DIM), 1.0),
        'state_gla': nrm(ks[4], (DEPTH, DEC_BATCH, GLA_HEADS, GLA_DK, GLA_DV), 0.5),
        'state_hgrn': nrm(ks[5], (DEPTH, DEC_BATCH, HGRN_HEADS, HGRN_DK, HGRN_DV), 0.5),
        'g_mix': 1.0 + nrm(ks[6], (DEPTH, D_MODEL), 0.1),
        'w_in': nrm(ks[7], (DEPTH, D_MODEL, D_IN), D_MODEL ** -0.5),
        'w_gk2': nrm(ks[8], (DEPTH, GLA_LOWRANK, GLA_KDIM), GLA_LOWRANK ** -0.5),
        'b_gk2': nrm(ks[9], (DEPTH, GLA_KDIM), 0.1),
        'gn_gla': 1.0 + nrm(ks[10], (DEPTH, GLA_DV), 0.1),
        'lb_logits': nrm(ks[11], (DEPTH + 1, HGRN_FDIM), 0.1),
        'gn_hgrn': 1.0 + nrm(ks[12], (DEPTH, HGRN_DV), 0.1),
        'w_out': nrm(ks[13], (DEPTH, D_MIX, D_MODEL), D_MIX ** -0.5),
        'g_ffn': 1.0 + nrm(ks[14], (DEPTH, D_MODEL), 0.1),
        'w_router': nrm(ks[15], (DEPTH, D_MODEL, N_EXPERTS), D_MODEL ** -0.5),
        'b_router': nrm(ks[16], (DEPTH, N_EXPERTS), 0.01),
        'w_gu': nrm(ks[17], (DEPTH, N_EXPERTS, D_MODEL, 2 * D_FF), D_MODEL ** -0.5),
        'b_gu': nrm(ks[18], (DEPTH, N_EXPERTS, 2 * D_FF), 0.02),
        'w_dn': nrm(ks[19], (DEPTH, N_EXPERTS, D_FF, D_MODEL), D_FF ** -0.5),
        'b_dn': nrm(ks[20], (DEPTH, N_EXPERTS, D_MODEL), 0.02),
        'g_ple': 1.0 + nrm(ks[21], (DEPTH, D_MODEL), 0.1),
        'w_ple_gate': nrm(ks[22], (DEPTH, D_MODEL, D_MODEL), D_MODEL ** -0.5),
        'w_ple_proj': nrm(ks[23], (DEPTH, PLE_DIM, D_MODEL), PLE_DIM ** -0.5),
        'g_final': 1.0 + nrm(ks[24], (D_MODEL,), 0.1),
    }

def reference(x_prompt, x_sample, p_prompt, p_sample, state_gla, state_hgrn,
              g_mix, w_in, w_gk2, b_gk2, gn_gla, lb_logits, gn_hgrn, w_out,
              g_ffn, w_router, b_router, w_gu, b_gu, w_dn, b_dn,
              g_ple, w_ple_gate, w_ple_proj, g_final):
    f32 = jnp.float32
    lb_all = jnp.cumsum(jax.nn.softmax(lb_logits.astype(f32), axis=0), axis=0)

    def trunk(x, p, init_gla, init_hgrn):
        h = x
        new_gla = []
        new_hgrn = []
        for i in range(DEPTH):
            a = rms_norm(h, g_mix[i])
            o, sg, sh = parallel_mixers(a, init_gla[i], init_hgrn[i], lb_all[i], w_in[i], w_gk2[i],
                                        b_gk2[i], gn_gla[i], gn_hgrn[i], w_out[i])
            h = h + o
            h = h + moe(rms_norm(h, g_ffn[i]), w_router[i], b_router[i], w_gu[i], b_gu[i], w_dn[i], b_dn[i])
            gate = jax.nn.sigmoid((rms_norm(h, g_ple[i]) @ w_ple_gate[i]).astype(f32))
            h = h + (gate * (p[i] @ w_ple_proj[i]).astype(f32)).astype(h.dtype)
            new_gla.append(sg.astype(x.dtype))
            new_hgrn.append(sh.astype(x.dtype))
        return rms_norm(h, g_final), jnp.stack(new_gla), jnp.stack(new_hgrn)

    b_p = x_prompt.shape[0]
    zero_gla = jnp.zeros((DEPTH, b_p, GLA_HEADS, GLA_DK, GLA_DV), f32)
    zero_hgrn = jnp.zeros((DEPTH, b_p, HGRN_HEADS, HGRN_DK, HGRN_DV), f32)
    y_prompt, new_gla_prompt, new_hgrn_prompt = trunk(x_prompt, p_prompt, zero_gla, zero_hgrn)
    y_sample, new_gla_sample, new_hgrn_sample = trunk(x_sample, p_sample, state_gla, state_hgrn)
    return (y_prompt, y_sample, new_gla_prompt, new_hgrn_prompt, new_gla_sample, new_hgrn_sample)


_drawn_inputs = setup_inputs


def setup_inputs(seed=0):
    import zlib

    import numpy as np

    out = dict(_drawn_inputs(seed))
    spreads = {}
    factors = {'b_gu': 6.013, 'b_dn': 6.925, 'g_ple': 3.56}
    for name, (base, spread) in spreads.items():
        noise = np.random.default_rng([zlib.crc32(name.encode()), seed]).standard_normal(out[name].shape)
        drawn = base * np.exp(spread * noise) if base else spread * noise
        out[name] = __import__('jax').numpy.asarray(drawn.astype(out[name].dtype))
    for name, factor in factors.items():
        out[name] = (out[name] * factor).astype(out[name].dtype)
    return out
```

```python
from contextlib import ExitStack

import concourse.bass as bass
from concourse import mybir

F32 = mybir.dt.float32
I32 = mybir.dt.int32
U32 = mybir.dt.uint32
ALU = mybir.AluOpType
ACT = mybir.ActivationFunctionType
AX_X = mybir.AxisListType.X

P = 128
BANK = 512
EPS = 1e-6
SLOTS = 64
SWIGLU_LIMIT = 7.0
SWIGLU_ALPHA = 1.702
GLA_NORMALIZER = 16.0
CHUNK = 64


class Links:

    def __init__(self, eng, sem, base=0):
        self.eng, self.sem, self.base, self.n = eng, sem, base, 0

    def add(self, ins):
        self.n += 1
        ins.then_inc(self.sem, 1)

    def wait(self):
        self.eng.wait_ge(self.sem, self.base + self.n)


def build(nc, io, out):
    D = io["x_prompt"].shape[2]
    L = io["x_prompt"].shape[1]
    SB, SL = io["x_sample"].shape[:2]
    S = SB * SL
    T = L + S
    E = io["w_router"].shape[2]
    FF = io["w_dn"].shape[2]
    PLE = io["w_ple_proj"].shape[1]
    GH, GK, GV = io["state_gla"].shape[2:]
    HH, HK, HV = io["state_hgrn"].shape[2:]
    RANK = io["w_gk2"].shape[1]
    KD = D // P
    KF = FF // P
    TT = L // P
    NT = TT + 1
    NCH = L // CHUNK
    PAIRS = GH * GK // P
    HEADS = GH + HH
    KU = PAIRS + HH
    TOPK = 4
    BLOCKS = -(-T // SLOTS)
    assert GV == HV == HK == P and GK * 2 == P and L == TT * P and S <= 32 and BANK >= T

    tiles = [(t * P, P) for t in range(TT)] + [(L, S)]

    G = 4
    c_q1 = 0
    c_v1 = 2 * GH * GK
    c_g1 = c_v1 + GH * GV
    c_r1 = c_g1 + GH * GV
    c_q2 = c_r1 + RANK
    c_f2 = c_q2 + HH * HK
    c_i2 = c_f2 + HH * HK
    c_g2 = c_i2 + HH * HV
    group_cols = [c_q1, c_q2, c_f2, c_v1, c_i2, c_g1, c_g2]
    NG = len(group_cols)
    Z_Q1, Z_K1, Z_Q2, Z_F2, Z_V, Z_I2, Z_G1, Z_G2 = 0, 2, 4, 8, 12, 16, 20, 24
    NZ = NG * G
    WSLOTS = 4

    UNITS = KD + KF // 2
    UCOLS = 2 * FF
    assert 2 * FF == 2 * D

    with ExitStack() as ctx:
        def sb(name, shape, dt=F32):
            return ctx.enter_context(nc.sbuf_tensor(name, shape, dt))

        def sem(name):
            return ctx.enter_context(nc.semaphore(name))

        ring = sb("ring", [P, UNITS * UCOLS])
        at = [0]

        def carve(*dims):
            n = 1
            for d in dims:
                n *= d
            v = ring[:, at[0]:at[0] + n]
            at[0] += n
            if len(dims) == 1:
                return v
            names = "abcd"[:len(dims)]
            return v.rearrange("p (" + " ".join(names) + ") -> p " + " ".join(names),
                               **{k: d for k, d in zip(names, dims)})

        z = carve(NZ, T)
        decay_start = at[0]
        lam = carve(KU, T)
        cum = carve(KU, T)
        at[0] = decay_start
        kend_tok = carve(TT, 2, KU * P)
        kend_smp = carve(KU * P)
        e_q = carve(KU, T)
        e_k = carve(KU, T)
        e_end = carve(KU, T)
        e_b = carve(KU, T)
        qr_pad = carve(PAIRS, 2, T)
        qb_pad = carve(PAIRS, 2, T)
        hist_start = at[0]
        s_hist = carve(KU, NCH, P)
        assert at[0] <= UNITS * UCOLS
        at[0] = hist_start
        gs = carve(3, PAIRS, T)
        assert at[0] <= UNITS * UCOLS
        att = z[:, 0:HEADS, :]
        o_raw = z[:, Z_V:Z_V + HEADS, :]

        wst = sb("wst", [P, WSLOTS, KD, P])
        blk = wst[:].rearrange("p a b c -> p (a b c)")
        bc = KD * SLOTS
        xsel, gbuf, ubuf, sbuf, hid, yT = (blk[:, i * bc:(i + 1) * bc].rearrange("p (c s) -> p c s", s=SLOTS) for i in range(6))
        yrow = blk[0:SLOTS, 6 * bc:6 * bc + D]
        assert 6 * bc + D <= WSLOTS * KD * P and KF == KD
        tok = sb("tok", [P, NT, D])
        hT = sb("hT", [P, KD, T])
        aT = sb("aT", [P, KD, T])
        acc = sb("acc", [P, KD, T])
        s0 = sb("s0", [P, 2, SB, P])
        vmask = sb("vmask", [32, 2, SB, P])
        rinv = sb("rinv", [P, T])
        lnbuf = sb("lnbuf", [P, T])
        ident = sb("ident", [P, P])
        ones = sb("ones", [P, P])
        upper = sb("upper", [P, P])
        reset = sb("reset", [P, T])
        maskf = sb("maskf", [P, P + 32])
        maski = sb("maski", [P, P + 32], I32)
        seqmask = sb("seqmask", [32, SB])
        iota_i = sb("iota_i", [P, BLOCKS * SLOTS], I32)
        iota1 = sb("iota1", [P, BLOCKS * SLOTS])
        eps = sb("eps", [P, 1])
        NV = 4 * KD + PAIRS + 2 * HH + 2
        vec_rows = sb("vec_rows", [NV, P])
        vecT = sb("vecT", [P, NV])
        V_MIX, V_FFN, V_PLE, V_FIN, V_BGK = 0, KD, 2 * KD, 3 * KD, 4 * KD
        V_LB = V_BGK + PAIRS
        V_GN = V_LB + 2 * HH
        lbt = sb("lbt", [P, 6, HH])
        r1w = sb("r1w", [P, KD, RANK])
        r1T = sb("r1T", [RANK, T])
        gk2 = sb("gk2", [RANK, GH * GK])
        dec = sb("dec", [P, KU, NCH + SB])
        w_rt = sb("w_rt", [P, KD, E])
        b_rt = sb("b_rt", [P, E])
        bgu_rows = sb("bgu_rows", [P, E * 2 * KF // P, P])
        bdn_rows = sb("bdn_rows", [P, E * KD // P, P])
        bguT = sb("bguT", [P, E, 2 * KF])
        bdnT = sb("bdnT", [P, E, KD])
        p_tok = sb("p_tok", [P, NT, PLE])
        pT = sb("pT", [P, PLE // P, T])
        w_pp = sb("w_pp", [P, PLE // P, D])
        logit = sb("logit", [P, NT, E])
        top8 = sb("top8", [P, NT, 8])
        idx8 = sb("idx8", [P, NT, 8], U32)
        idxf = sb("idxf", [P, NT, TOPK])
        pk = sb("pk", [P, NT, TOPK])
        psum_k = sb("psum_k", [P, NT, 2])
        onehot = sb("onehot", [P, NT, TOPK, E])
        gated = sb("gated", [P, NT, TOPK, E])
        gate_e = sb("gate_e", [P, NT, E])
        memb = sb("memb", [P, NT, E])
        rankp = sb("rankp", [P, NT, E])
        cnt_f = sb("cnt_f", [1, E + 1])
        cnt_i = sb("cnt_i", [1, E + 1], I32)
        sel = sb("sel", [P, NT, SLOTS])
        selg = sb("selg", [P, NT, SLOTS])
        selT = sb("selT", [SLOTS, T])

        ps = ctx.enter_context(nc.psum_tensor("ps", [P, 8, BANK], F32))

        x_loaded = sem("x_loaded")
        vec_loaded = sem("vec_loaded")
        small_loaded = sem("small_loaded")
        r1w_loaded = sem("r1w_loaded")
        ple_loaded = sem("ple_loaded")
        pool_link = sem("pool_link")
        consts_ready = sem("consts_ready")
        xT_done = sem("xT_done")
        xT_copied_a = sem("xT_copied_a")
        xT_copied_v = sem("xT_copied_v")
        vec_done = sem("vec_done")
        vec_copied = sem("vec_copied")
        bias_done = sem("bias_done")
        bias_copied = sem("bias_copied")
        sq_ready = sem("sq_ready")
        ss_ready = sem("ss_ready")
        act_link = sem("act_link")
        rinv_ready = sem("rinv_ready")
        norm_ready = sem("norm_ready")
        r1_done = sem("r1_done")
        r1_copied = sem("r1_copied")
        gs_done = sem("gs_done")
        gs_bias = sem("gs_bias")
        gs_exp = sem("gs_exp")
        w_loaded = [sem(f"w_loaded{i}") for i in range(WSLOTS)]
        z_done = sem("z_done")
        z_copied = sem("z_copied")
        sig_ready = sem("sig_ready")
        chain = sem("chain")
        forget_ready = sem("forget_ready")
        lnf_ready = sem("lnf_ready")
        d1_ready = sem("d1_ready")
        e_ready = sem("e_ready")
        d3_ready = sem("d3_ready")
        cum_ready = sem("cum_ready")
        qk_ready = sem("qk_ready")
        v_ready = sem("v_ready")
        vt_done = sem("vt_done")
        v_copied = sem("v_copied")
        ke_done = sem("ke_done")
        ke_copied = sem("ke_copied")
        att_zeroed = sem("att_zeroed")
        att_done = sem("att_done")
        att_masked = sem("att_masked")
        u_done = sem("u_done")
        s_ready = sem("s_ready")
        o_done = sem("o_done")
        o_copied = sem("o_copied")
        osq_ready = sem("osq_ready")
        oss_ready = sem("oss_ready")
        oln_ready = sem("oln_ready")
        orinv_ready = sem("orinv_ready")
        gates_ready = sem("gates_ready")
        o_ready = sem("o_ready")
        s0_loaded = [sem("s0_loaded0"), sem("s0_loaded1")]
        vm_ready = sem("vm_ready")
        su_done = sem("su_done")
        su_used = sem("su_used")
        s_copied_u = sem("s_copied_u")
        lb_ready = sem("lb_ready")
        lb_exp = sem("lb_exp")
        s0_stored = sem("s0_stored")
        sp_stored = sem("sp_stored")
        h_done = sem("h_done")
        h_ready = sem("h_ready")
        xn_done = sem("xn_done")
        xn_copied = sem("xn_copied")
        lg_done = sem("lg_done")
        pk_ready = sem("pk_ready")
        pk_exp = sem("pk_exp")
        memb_ready = sem("memb_ready")
        rank_done = sem("rank_done")
        cnt_ready = sem("cnt_ready")
        zero_ready = sem("zero_ready")
        p_done = sem("p_done")
        p_copied = sem("p_copied")
        u_loaded = [sem(f"u_loaded{i}") for i in range(UNITS)]
        u_used = sem("u_used")
        sel_ready = sem("sel_ready")
        xs_done = sem("xs_done")
        xs_copied = sem("xs_copied")
        gate_ready = sem("gate_ready")
        sigm_ready = sem("sigm_ready")
        hid_ready = sem("hid_ready")
        y_copied = sem("y_copied")
        yr_done = sem("yr_done")
        yr_copied = sem("yr_copied")
        st_done = sem("st_done")
        st_copied = sem("st_copied")
        cb_done = sem("cb_done")
        acc_added = sem("acc_added")
        moe_chain = sem("moe_chain")
        pg_loaded = sem("pg_loaded")
        pg_done = sem("pg_done")
        pg_sig = sem("pg_sig")
        pg_used = sem("pg_used")
        out_done = sem("out_done")
        out_copied = sem("out_copied")
        out_stored = sem("out_stored")

        block = ctx.enter_context(nc.Block())

        def unit_src(e, c):
            if c < KD:
                return io["w_gu"][0, e, c * P:(c + 1) * P, :]
            c = 2 * (c - KD)
            return io["w_dn"][0, e, c * P:(c + 2) * P, :].rearrange("(c p) n -> p c n", p=P)

        def unit_dst(c):
            v = ring[:, c * UCOLS:(c + 1) * UCOLS]
            return v if c < KD else v.rearrange("p (c n) -> p c n", c=2)

        def overflow_blocks(eng, body):
            n = eng.alloc_register(f"blocks_{eng.engine.name}")
            eng.reg_mov(n, E)
            eng.wait_ge(cnt_ready, 1)
            most = eng.value_load(cnt_i[0:1, E:E + 1], min_val=0, max_val=T)
            with eng.If(most > SLOTS):
                with eng.Fori(0, E) as e:
                    c = eng.value_load(cnt_i[0:1, bass.ds(e, 1)], min_val=0, max_val=T)
                    with eng.Fori(1, BLOCKS) as j:
                        with eng.If(c > j * SLOTS):
                            body(eng.snap(n, min_val=E, max_val=E * BLOCKS), e, j)
                            eng.reg_add(n, n, 1)
            return eng.snap(n, min_val=E, max_val=E * BLOCKS)

        @block.sync
        def _(sp):
            cols = [(io["w_in"], c0 + j * P) for c0 in group_cols for j in range(G)]
            cols += [(io["w_out"], j * P) for j in range(KD)]

            def load_cols(i):
                w, c0 = cols[i]
                if i >= WSLOTS:
                    last = i - WSLOTS
                    if last < NZ:
                        sp.wait_ge(z_done, last + 1)
                    else:
                        sp.wait_ge(h_done, last - NZ + 1)
                sp.dma_start(wst[:, i % WSLOTS], w[0, :, c0:c0 + P].rearrange("(c p) n -> p c n", p=P)) \
                    .then_inc(w_loaded[i % WSLOTS], 16)

            def state_dram(gla, hgrn, u):
                if u < PAIRS:
                    return gla[0][:, 2 * u:2 * u + 2].rearrange("b h k v -> (h k) b v")
                return hgrn[0][:, u - PAIRS].rearrange("b k v -> k b v")

            def load_state(u):
                sp.dma_start(s0[:, u % 2], state_dram(io["state_gla"], io["state_hgrn"], u)).then_inc(s0_loaded[u % 2], 16)

            for i in range(NZ + WSLOTS):
                load_cols(i)
                if i == NZ // 2:
                    load_state(0)
                    load_state(1)
            sp.wait_ge(s_ready, 1)
            sp.dma_start(out[2][0, 0].rearrange("(u h) k v -> (h k) u v", h=2), s_hist[:, 0:PAIRS, NCH - 1, :]) \
                .then_inc(sp_stored, 16)
            sp.dma_start(out[3][0, 0].rearrange("h k v -> k h v"), s_hist[:, PAIRS:KU, NCH - 1, :]).then_inc(sp_stored, 16)
            for u in range(KU):
                sp.wait_ge(su_used, 2 * u + 2 if u < PAIRS else GH + u - PAIRS + 1)
                sp.dma_start(state_dram(out[4], out[5], u), s0[:, u % 2]).then_inc(s0_stored, 16)
                if u + 2 < KU:
                    sp.wait_ge(s0_stored, 16 * (u + 1))
                    load_state(u + 2)
            sp.wait_ge(o_ready, HEADS)
            sp.wait_ge(sp_stored, 16 * 2)
            for c in range(UNITS):
                if c < KD - WSLOTS:
                    load_cols(NZ + WSLOTS + c)
                sp.dma_start(unit_dst(c), unit_src(0, c)).then_inc(u_loaded[c], 16)

            def load_block(n, e, j):
                for c in range(UNITS):
                    sp.wait_ge(u_used, n * UNITS + (c + 1 - UNITS))
                    sp.dma_start(unit_dst(c), unit_src(e, c)).then_inc(u_loaded[c], 16)

            with sp.Fori(1, E) as e:
                load_block(e, e, 0)
            n = overflow_blocks(sp, load_block)
            for c in range(KD // 2):
                sp.wait_ge(u_used, n * UNITS + (c + 1 - UNITS))
                sp.dma_start(ring[:, c * UCOLS:(c + 1) * UCOLS].rearrange("p (c n) -> p c n", c=2),
                             io["w_ple_gate"][0, 2 * c * P:(2 * c + 2) * P, :].rearrange("(c p) n -> p c n", p=P)) \
                    .then_inc(pg_loaded, 16)
            sp.wait_ge(out_copied, NT)
            sp.dma_start(out[0][0].rearrange("(t p) d -> p t d", p=P), tok[:, 0:TT, :]).then_inc(out_stored, 16)
            sp.dma_start(out[1].rearrange("b l d -> (b l) d"), tok[0:S, TT, :]).then_inc(out_stored, 16)
            sp.wait_ge(out_stored, 32)
            sp.wait_ge(s0_stored, 16 * KU)

        @block.gpsimd
        def _(pool):
            lk = Links(pool, pool_link)
            lk.add(pool.memset(ident[:], 0.0))
            lk.add(pool.memset(ones[:], 1.0))
            lk.add(pool.memset(reset[:], 1.0))
            lk.add(pool.memset(maskf[:], 1.0))
            lk.add(pool.memset(seqmask[:], 1.0))
            lk.add(pool.memset(eps[:], EPS))
            lk.add(pool.iota(iota_i[:], pattern=[[1, BLOCKS * SLOTS]], base=1, channel_multiplier=0))
            lk.wait()
            pool.affine_select(out=ident[:], in_=ident[:], compare_op=ALU.not_equal, fill=1.0, base=0,
                               pattern=[[-1, P]], channel_multiplier=1).then_inc(consts_ready, 1)
            pool.affine_select(out=upper[:], in_=ones[:], compare_op=ALU.is_gt, fill=0.0, base=0,
                               pattern=[[1, P]], channel_multiplier=-1).then_inc(consts_ready, 1)
            pool.memset(reset[:, 0:L].rearrange("p (n c) -> p n c", c=CHUNK)[:, :, 0:1], 0.0).then_inc(consts_ready, 1)
            pool.memset(reset[:, L:T].rearrange("p (n c) -> p n c", c=SL)[:, :, 0:1], 0.0).then_inc(consts_ready, 1)
            lk.add(pool.affine_select(out=maskf[:], in_=maskf[:], compare_op=ALU.is_ge, fill=0.0, base=0,
                                      pattern=[[1, P + 32]], channel_multiplier=-1))
            lk.wait()
            lk.add(pool.memset(maskf[0:CHUNK, CHUNK:P], 0.0))
            lk.add(pool.affine_select(out=maskf[0:32, P:P + 32], in_=ones[0:32, 0:32], compare_op=ALU.is_ge, fill=0.0,
                                      base=0, pattern=[[1, 32]], channel_multiplier=-1))
            lk.wait()
            lk.add(pool.affine_select(out=maskf[0:32, P:P + 32], in_=maskf[0:32, P:P + 32], compare_op=ALU.is_ge,
                                      fill=0.0, base=0, pattern=[[-SL, 32 // SL], [0, SL]], channel_multiplier=1))
            lk.add(pool.affine_select(out=seqmask[:], in_=seqmask[:], compare_op=ALU.is_ge, fill=0.0, base=0,
                                      pattern=[[-SL, SB]], channel_multiplier=1))
            lk.wait()
            pool.affine_select(out=seqmask[:], in_=seqmask[:], compare_op=ALU.is_ge, fill=0.0, base=SL - 1,
                               pattern=[[SL, SB]], channel_multiplier=-1).then_inc(consts_ready, 1)
            pool.tensor_copy(maski[:], maskf[:]).then_inc(consts_ready, 1)
            pool.tensor_copy(iota1[:], iota_i[:]).then_inc(consts_ready, 1)
            pool.memset(qr_pad, 0.0).then_inc(consts_ready, 1)
            pool.memset(qb_pad, 0.0).then_inc(consts_ready, 1)
            pool.memset(idx8[:], 0).then_inc(consts_ready, 1)
            pool.memset(top8[:], 0.0).then_inc(consts_ready, 1)
            pool.memset(selT[:], 0.0).then_inc(st_copied, 1)
            pool.wait_ge(qk_ready, 1)
            pool.memset(att, 0.0).then_inc(att_zeroed, 1)
            pool.memset(kend_tok, 0.0).then_inc(att_zeroed, 1)
            for h in range(HEADS):
                if h == 0:
                    pool.wait_ge(v_copied, NT)
                if h >= 2:
                    pool.wait_ge(su_done, h - 1)
                pool.tensor_tensor(vmask[0:S, h % 2], tok[0:S, TT, h * P:(h + 1) * P].unsqueeze(1).to_broadcast([S, SB, P]),
                                   seqmask[0:S, :].unsqueeze(2).to_broadcast([S, SB, P]), ALU.mult).then_inc(vm_ready, 1)
            pool.wait_ge(h_done, KD)
            pool.memset(acc[:], 0.0).then_inc(zero_ready, 1)
            pool.memset(yrow, 0.0).then_inc(yr_copied, 1)

        @block.scalar
        def _(act):
            lk = Links(act, act_link)
            act.dma_start(tok[:, 0:TT, :], io["x_prompt"][0].rearrange("(t p) d -> p t d", p=P)).then_inc(x_loaded, 16)
            act.dma_start(tok[0:S, TT, :], io["x_sample"].rearrange("b l d -> (b l) d")).then_inc(x_loaded, 16)
            row = 0
            for name, n in (("g_mix", KD), ("g_ffn", KD), ("g_ple", KD), ("g_final", KD), ("b_gk2", PAIRS),
                            ("lb_logits", 2 * HH), ("gn_gla", 1), ("gn_hgrn", 1)):
                a = io[name]
                src = a.rearrange("(r p) -> r p", p=P) if len(a.shape) == 1 else a.rearrange("a (r p) -> (a r) p", p=P)
                act.dma_start(vec_rows[row:row + n, :], src).then_inc(vec_loaded, 16)
                row += n
            act.dma_start(r1w[:], io["w_in"][0, :, c_r1:c_r1 + RANK].rearrange("(c p) n -> p c n", p=P)).then_inc(r1w_loaded, 16)
            act.dma_start(gk2[:], io["w_gk2"][0]).then_inc(r1w_loaded, 16)
            act.dma_start(w_rt[:], io["w_router"][0].rearrange("(c p) n -> p c n", p=P)).then_inc(small_loaded, 16)
            act.dma_start(b_rt[:], io["b_router"][0:1, :].to_broadcast([P, E])).then_inc(small_loaded, 16)
            act.dma_start(bgu_rows[:], io["b_gu"][0].rearrange("e (c f) -> (e c) f", f=P).rearrange("(a p) f -> p a f", p=P)) \
                .then_inc(small_loaded, 16)
            act.dma_start(bdn_rows[:], io["b_dn"][0].rearrange("e (c f) -> (e c) f", f=P).rearrange("(a p) f -> p a f", p=P)) \
                .then_inc(small_loaded, 16)
            act.dma_start(p_tok[:, 0:TT, :], io["p_prompt"][0, 0].rearrange("(t p) d -> p t d", p=P)).then_inc(ple_loaded, 16)
            act.dma_start(p_tok[0:S, TT, :], io["p_sample"][0].rearrange("b l d -> (b l) d")).then_inc(ple_loaded, 16)
            act.dma_start(w_pp[:], io["w_ple_proj"][0].rearrange("(c p) n -> p c n", p=P)).then_inc(ple_loaded, 16)

            for c in range(0, KD, 2):
                act.wait_ge(xT_done, c + 1)
                act.copy(hT[:, c, :], ps[:, c, 0:T]).then_inc(xT_copied_a, 1)

            def inv_rms(k, src, sqbuf):
                act.activation(sqbuf, src, ACT.Square).then_inc(sq_ready, 1)
                act.wait_ge(ss_ready, k + 1)
                lk.add(act.activation(lnbuf[:], ps[:, 7, 0:T], ACT.Ln, bias=eps[:, 0:1], scale=1.0 / D))
                lk.wait()
                act.activation(rinv[:], lnbuf[:], ACT.Exp, scale=-0.5).then_inc(rinv_ready, 1)

            act.wait_ge(xT_copied_v, KD // 2)
            act.wait_ge(xT_copied_a, KD // 2)
            act.wait_ge(consts_ready, 11)
            inv_rms(0, hT[:], acc[:])

            act.wait_ge(lb_ready, 1)
            act.activation(lbt[:, 1:3], lbt[:, 1:3], ACT.Exp).then_inc(lb_exp, 1)
            act.wait_ge(r1_done, 1)
            act.copy(r1T[:], ps[0:RANK, 7, 0:T]).then_inc(r1_copied, 1)
            act.wait_ge(gs_bias, 1)
            lk.add(act.activation(gs[:, 2], gs[:, 1], ACT.Exp, scale=-1.0))
            lk.wait()
            act.activation(gs[:, 2], gs[:, 2], ACT.Ln, bias=ones[:, 0:1], scale=1.0).then_inc(gs_exp, 1)

            def copy_groups(g0, g1):
                with act.Fori(g0, g1) as g:
                    for j in range(G):
                        act.wait_ge(z_done, g * G + (j + 1))
                        act.copy(z[:, bass.ds(g * G + j, 1), :], ps[:, j:j + 1, 0:T]).then_inc(z_copied, 1)

            copy_groups(0, 3)
            act.wait_ge(z_copied, 3 * G)
            act.activation(e_q[:, 2:6, :], z[:, Z_Q2:Z_Q2 + G, :], ACT.Sigmoid).then_inc(sig_ready, 1)
            act.activation(e_k[:, 2:6, :], z[:, Z_F2:Z_F2 + G, :], ACT.Sigmoid).then_inc(sig_ready, 1)
            copy_groups(3, 5)
            act.wait_ge(z_copied, 5 * G)
            act.activation(e_end[:, 2:6, :], z[:, Z_I2:Z_I2 + G, :], ACT.Sigmoid).then_inc(sig_ready, 1)
            act.wait_ge(forget_ready, 1)
            act.activation(lam[:, PAIRS:KU, :], lam[:, PAIRS:KU, :], ACT.Ln).then_inc(lnf_ready, 1)
            act.wait_ge(cum_ready, 1)
            act.activation(e_b, cum, ACT.Exp).then_inc(e_ready, 1)
            act.wait_ge(d1_ready, 1)
            act.activation(e_q, lam, ACT.Exp).then_inc(e_ready, 1)
            act.activation(e_k, lam, ACT.Exp, scale=-1.0).then_inc(e_ready, 1)
            act.wait_ge(v_ready, 1)
            act.wait_ge(d3_ready, 1)
            act.activation(e_end, lam, ACT.Exp).then_inc(e_ready, 1)
            copy_groups(5, 7)
            act.wait_ge(z_copied, 7 * G)
            act.activation(acc[:, 0:G, :], z[:, Z_G1:Z_G1 + G, :], ACT.Sigmoid).then_inc(sig_ready, 1)
            act.activation(z[:, Z_G2:Z_G2 + G, :], z[:, Z_G2:Z_G2 + G, :], ACT.Sigmoid).then_inc(sig_ready, 1)

            def head_rinv(h):
                act.wait_ge(oss_ready, h + 1)
                if h:
                    act.wait_ge(orinv_ready, h)
                lk.add(act.activation(lnbuf[:], ps[:, 2 + h % 2, 0:T], ACT.Ln, bias=eps[:, 0:1], scale=1.0 / P))
                lk.wait()
                act.activation(aT[:, h, :], lnbuf[:], ACT.Exp, scale=-0.5).then_inc(orinv_ready, 1)

            for h in range(HEADS):
                act.wait_ge(o_done, h + 1)
                act.copy(o_raw[:, h, :], ps[:, h % 2, 0:T]).then_inc(o_copied, 1)
                act.activation(aT[:, h, :], ps[:, h % 2, 0:T], ACT.Square).then_inc(osq_ready, 1)
                if h >= 2:
                    head_rinv(h - 2)
            for h in range(HEADS - 2, HEADS):
                head_rinv(h)

            act.wait_ge(h_ready, KD)
            inv_rms(1, hT[:], tok[:, :, :].rearrange("p t d -> p (t d)")[:, 0:KD * T].rearrange("p (c t) -> p c t", t=T))
            act.wait_ge(ss_ready, 2)
            for t, (t0, n) in enumerate(tiles):
                act.wait_ge(xn_done, t + 1)
                act.copy(tok[0:n, t, :], ps[0:n, 2 * t:2 * t + 2, :].rearrange("p b n -> p (b n)")).then_inc(xn_copied, 1)
            act.wait_ge(pk_ready, 1)
            act.activation(pk[:], pk[:], ACT.Exp).then_inc(pk_exp, 1)

            def expert(n, e, j):
                act.wait_ge(xs_done, n + 1)
                act.copy(xsel.rearrange("p c s -> p (c s)"), ps[:, 2, :]).then_inc(xs_copied, 1)
                act.wait_ge(gate_ready, n + 1)
                act.activation(sbuf, gbuf, ACT.Sigmoid, scale=SWIGLU_ALPHA).then_inc(sigm_ready, 1)
                act.wait_ge(st_done, n + 1)
                act.copy(selT[:], ps[0:SLOTS, 2, 0:T]).then_inc(st_copied, 1)
                act.wait_ge(yr_done, n + 1)
                act.copy(yrow, ps[0:SLOTS, 4:6, :].rearrange("p b n -> p (b n)")).then_inc(yr_copied, 1)

            act.wait_ge(st_copied, 1)
            act.wait_ge(yr_copied, 1)
            with act.Fori(0, E) as e:
                expert(e, e, 0)
            overflow_blocks(act, expert)

            act.wait_ge(h_ready, KD + 1)
            inv_rms(2, hT[:], acc[:])
            for c in range(KD):
                act.wait_ge(pg_done, c + 1)
                act.activation(acc[:, c, :], ps[:, c % 4, 0:T], ACT.Sigmoid).then_inc(pg_sig, 1)
            act.wait_ge(h_ready, KD + 2)
            inv_rms(3, hT[:], acc[:])
            for t, (t0, n) in enumerate(tiles):
                act.wait_ge(out_done, t + 1)
                act.copy(tok[0:n, t, :], ps[0:n, 2 * t:2 * t + 2, :].rearrange("p b n -> p (b n)")).then_inc(out_copied, 1)

        @block.tensor
        def _(pe):
            def mm(o, lhsT, rhs, start, stop):
                return pe.matmul(o, lhsT, rhs, start=start, stop=stop, skip_group_check=True)

            pe.wait_ge(consts_ready, 2)
            pe.wait_ge(x_loaded, 32)
            for c in range(KD):
                for t, (t0, n) in enumerate(tiles):
                    ins = pe.transpose(ps[:, c, t0:t0 + n], tok[0:n, t, c * P:(c + 1) * P], ident[0:n, 0:n])
                ins.then_inc(xT_done, 1)
            pe.wait_ge(vec_loaded, 16 * 8)
            pe.wait_ge(xT_copied_a, 1)
            pe.transpose(ps[:, 0, 0:NV], vec_rows[:], ident[0:NV, 0:NV]).then_inc(vec_done, 1)

            def sums(k, sqbuf):
                pe.wait_ge(sq_ready, k + 1)
                for c in range(KD):
                    ins = mm(ps[:, 7, 0:T], ones[:], sqbuf[:, c, :], c == 0, c == KD - 1)
                ins.then_inc(ss_ready, 1)

            sums(0, acc)
            pe.wait_ge(r1w_loaded, 32)
            pe.wait_ge(norm_ready, KD)
            pe.wait_ge(rinv_ready, 1)
            for c in range(KD):
                ins = mm(ps[0:RANK, 7, 0:T], r1w[:, c, :], aT[:, c, :], c == 0, c == KD - 1)
            ins.then_inc(r1_done, 1)
            pe.wait_ge(r1_copied, 1)
            pe.wait_ge(xT_copied_v, KD // 2)
            for u in range(PAIRS):
                ins = mm(ps[:, 5 + u, 0:T], gk2[:, u * P:(u + 1) * P], r1T[:], True, True)
            ins.then_inc(gs_done, 1)
            pe.wait_ge(vec_copied, 1)
            def project(g, first=False):
                for j in range(G):
                    pe.wait_ge(w_loaded[j], 16 * (g + 1))
                    if not first:
                        pe.wait_ge(z_copied, g * G + (j + 1 - G))
                    for c in range(KD):
                        ins = mm(ps[:, j, 0:T], wst[:, j, c, :], aT[:, c, :], c == 0, c == KD - 1)
                    ins.then_inc(z_done, 1)

            project(0, first=True)
            with pe.Fori(1, NG) as g:
                project(g)
            pe.wait_ge(small_loaded, 16 * 4)
            pe.wait_ge(ple_loaded, 16 * 3)
            pe.wait_ge(gs_bias, 1)
            for a in range(E * 2 * KF // P):
                pe.transpose(ps[:, 4, a * P:(a + 1) * P], bgu_rows[:, a, :], ident[:])
            for a in range(E * KD // P):
                pe.transpose(ps[:, 5, a * P:(a + 1) * P], bdn_rows[:, a, :], ident[:])
            for c in range(PLE // P):
                for t, (t0, n) in enumerate(tiles):
                    ins = pe.transpose(ps[:, 6 + c, t0:t0 + n], p_tok[0:n, t, c * P:(c + 1) * P], ident[0:n, 0:n])
            ins.then_inc(bias_done, 1)
            pe.wait_ge(v_ready, 1)
            pe.wait_ge(z_copied, NZ)
            pe.wait_ge(bias_copied, 1)
            for t, (t0, n) in enumerate(tiles):
                for c in range(HEADS):
                    ins = pe.transpose(ps[0:n, 2 * t + c // 4, (c % 4) * P:(c % 4 + 1) * P], z[:, Z_V + c, t0:t0 + n], ident[:])
                ins.then_inc(vt_done, 1)
            pe.wait_ge(qk_ready, 1)
            for t, (t0, n) in enumerate(tiles):
                pe.wait_ge(v_copied, t + 1)
                for u in range(KU):
                    ins = pe.transpose(ps[0:n, 2 * t + u // 4, (u % 4) * P:(u % 4 + 1) * P], e_end[:, u, t0:t0 + n], ident[:])
                ins.then_inc(ke_done, 1)
            pe.wait_ge(ke_copied, 1)
            for h in range(HEADS):
                b = h % 4
                if h >= 4:
                    pe.wait_ge(att_masked, h - 3)
                u = h // 2 if h < GH else h - GH + PAIRS
                q = qr_pad[:, u, h % 2, :] if h < GH else e_q[:, u, :]
                for t, (t0, n) in enumerate(tiles):
                    ins = mm(ps[0:n, b, t0:t0 + n], e_k[:, u, t0:t0 + n], q[:, t0:t0 + n], True, True)
                ins.then_inc(att_done, 1)
            k = 0
            for u in range(KU):
                heads = 2 if u < PAIRS else 1
                v0 = 2 * u * P if u < PAIRS else (GH + u - PAIRS) * P
                for n0 in range(0, NCH, 2):
                    if k >= 4:
                        pe.wait_ge(s_copied_u, k - 3)
                    for n in (n0, n0 + 1):
                        ins = mm(ps[:, 4 + k % 4, (n - n0) * 2 * P:(n - n0) * 2 * P + heads * P],
                                 kend_tok[:, n // 2, n % 2, u * P:(u + 1) * P], tok[:, n // 2, v0:v0 + heads * P], True, True)
                    ins.then_inc(u_done, 1)
                    k += 1
            def head_sums(h):
                pe.wait_ge(osq_ready, h + 1)
                if h >= 2:
                    pe.wait_ge(orinv_ready, h - 1)
                mm(ps[:, 2 + h % 2, 0:T], ones[:], aT[:, h, :], True, True).then_inc(oss_ready, 1)

            pe.wait_ge(s_ready, 1)
            for h in range(HEADS):
                b = h % 2
                pe.wait_ge(att_masked, HEADS)
                if h >= 2:
                    pe.wait_ge(osq_ready, h - 1)
                    pe.wait_ge(o_copied, h - 1)
                u = h // 2 if h < GH else h - GH + PAIRS
                qb = qb_pad[:, u, h % 2, :] if h < GH else e_b[:, u, :]
                if h < GH and h % 2 == 0 or h >= GH:
                    pe.wait_ge(s0_loaded[u % 2], 16 * (u // 2 + 1))
                for t, (t0, n) in enumerate(tiles):
                    mm(ps[:, b, t0:t0 + n], tok[0:n, t, h * P:(h + 1) * P], att[0:n, h, t0:t0 + n], t == 0, False)
                for n in range(1, NCH):
                    mm(ps[:, b, n * CHUNK:(n + 1) * CHUNK], s_hist[:, u, n - 1, :], qb[:, n * CHUNK:(n + 1) * CHUNK], False, False)
                for s in range(SB):
                    c0 = L + s * SL
                    ins = mm(ps[:, b, c0:c0 + SL], s0[:, u % 2, s, :], qb[:, c0:c0 + SL], False, s == SB - 1)
                ins.then_inc(o_done, 1)
                pe.wait_ge(vm_ready, h + 1)
                if h >= 2:
                    pe.wait_ge(su_used, h - 1)
                for half in range(2):
                    ins = mm(ps[:, 4 + 2 * (h % 2) + half, :], kend_smp[0:S, u * P:(u + 1) * P],
                             vmask[0:S, h % 2, half * 4:half * 4 + 4, :].rearrange("p b v -> p (b v)"), True, True)
                ins.then_inc(su_done, 1)
                if h >= 1:
                    head_sums(h - 1)
            head_sums(HEADS - 1)
            for c in range(KD):
                i = NZ + c
                pe.wait_ge(w_loaded[i % WSLOTS], 16 * (i // WSLOTS + 1))
                if c == 0:
                    pe.wait_ge(o_ready, HEADS)
                    pe.wait_ge(su_used, HEADS)
                if c >= 4:
                    pe.wait_ge(h_ready, c - 3)
                for h in range(HEADS):
                    ins = mm(ps[:, 4 + c % 4, 0:T], wst[:, i % WSLOTS, h, :], acc[:, h, :], h == 0, h == HEADS - 1)
                ins.then_inc(h_done, 1)
            pe.wait_ge(h_ready, KD)
            sums(1, tok[:, :, :].rearrange("p t d -> p (t d)")[:, 0:KD * T].rearrange("p (c t) -> p c t", t=T))
            pe.wait_ge(norm_ready, 2 * KD)
            for t, (t0, n) in enumerate(tiles):
                for c in range(KD):
                    ins = mm(ps[0:n, 6, t * E:(t + 1) * E], aT[:, c, t0:t0 + n], w_rt[:, c, :], c == 0, c == KD - 1)
            ins.then_inc(lg_done, 1)
            for t, (t0, n) in enumerate(tiles):
                for c in range(KD):
                    ins = pe.transpose(ps[0:n, 2 * t + c // 4, (c % 4) * P:(c % 4 + 1) * P], aT[:, c, t0:t0 + n], ident[:])
                ins.then_inc(xn_done, 1)
            pe.wait_ge(memb_ready, 1)
            for t, (t0, n) in enumerate(tiles):
                for s in range(t + 1):
                    m = tiles[s][1]
                    lhs = upper[0:m, 0:n] if s == t else ones[0:m, 0:n]
                    mm(ps[0:n, 7, t * E:(t + 1) * E], lhs, memb[0:m, s, :], s == 0, s == t)
            for s, (_, m) in enumerate(tiles):
                ins = mm(ps[0:1, 7, NT * E:(NT + 1) * E], ones[0:m, 0:1], memb[0:m, s, :], s == 0, s == NT - 1)
            ins.then_inc(rank_done, 1)
            pe.wait_ge(xn_copied, NT)
            pe.wait_ge(cnt_ready, 1)

            def combine(n):
                pe.wait_ge(st_copied, n + 1)
                pe.wait_ge(yr_copied, n + 1)
                for c in range(KD):
                    if c >= 2:
                        pe.wait_ge(acc_added, n * KD + (c - 1))
                    mm(ps[:, 6 + c % 2, 0:T], yrow[:, c * P:(c + 1) * P], selT[:], True, True).then_inc(cb_done, 1)

            def expert(n, e, j):
                pe.wait_ge(sel_ready, n + 1)
                pe.wait_ge(st_copied, n + 1)
                for c in range(KD):
                    for t, (t0, m) in enumerate(tiles):
                        ins = mm(ps[:, 2, c * SLOTS:(c + 1) * SLOTS], tok[0:m, t, c * P:(c + 1) * P], sel[0:m, t, :],
                                 t == 0, t == NT - 1)
                ins.then_inc(xs_done, 1)
                pe.wait_ge(xs_copied, n + 1)
                for c in range(KD):
                    pe.wait_ge(u_loaded[c], n * 16 + 16)
                    for f in range(2 * KF):
                        ins = mm(ps[:, f // KF, (f % KF) * SLOTS:(f % KF + 1) * SLOTS],
                                 ring[:, c * UCOLS + f * P:c * UCOLS + (f + 1) * P], xsel[:, c, :],
                                 c == 0 and f % KF == 0, c == KD - 1)
                    ins.then_inc(u_used, 1)
                combine(n)
                for t, (t0, m) in enumerate(tiles):
                    ins = pe.transpose(ps[0:SLOTS, 2, t0:t0 + m], selg[0:m, t, :], ident[0:m, 0:m])
                ins.then_inc(st_done, 1)
                pe.wait_ge(hid_ready, n + 1)
                for c in range(KF // 2):
                    pe.wait_ge(u_loaded[KD + c], n * 16 + 16)
                    for k in range(2):
                        for f in range(KD):
                            w0 = (KD + c) * UCOLS + k * D + f * P
                            ins = mm(ps[:, 3, f * SLOTS:(f + 1) * SLOTS], ring[:, w0:w0 + P], hid[:, 2 * c + k, :],
                                     c + k + f == 0, 2 * c + k == KF - 1)
                    ins.then_inc(u_used, 1)
                pe.wait_ge(y_copied, n + 1)
                for f in range(KD):
                    o = ps[0:SLOTS, 4 + f // 4, (f % 4) * P:(f % 4 + 1) * P]
                    ins = mm(o, yT[:, f, :], ident[:], True, True) if f == 0 else pe.transpose(o, yT[:, f, :], ident[:])
                ins.then_inc(yr_done, 1)

            with pe.Fori(0, E) as e:
                expert(e, e, 0)
            n = overflow_blocks(pe, expert)
            combine(n)

            pe.wait_ge(h_ready, KD + 1)
            sums(2, acc)
            pe.wait_ge(norm_ready, 3 * KD)
            pe.wait_ge(pg_loaded, 16 * (KD // 2))
            for c in range(KD):
                b = c % 4
                if c >= 4:
                    pe.wait_ge(pg_used, c - 3)
                    pe.wait_ge(pg_sig, c - 3)
                for k in range(PLE // P):
                    mm(ps[:, 4 + b, 0:T], w_pp[:, k, c * P:(c + 1) * P], pT[:, k, :], k == 0,
                       k == PLE // P - 1)
                for k in range(KD):
                    ins = mm(ps[:, b, 0:T], ring[:, k * D + c * P:k * D + (c + 1) * P], aT[:, k, :], k == 0, k == KD - 1)
                ins.then_inc(pg_done, 1)
            pe.wait_ge(h_ready, KD + 2)
            sums(3, acc)
            pe.wait_ge(norm_ready, 4 * KD)
            for t, (t0, n) in enumerate(tiles):
                for c in range(KD):
                    ins = pe.transpose(ps[0:n, 2 * t + c // 4, (c % 4) * P:(c % 4 + 1) * P], aT[:, c, t0:t0 + n], ident[:])
                ins.then_inc(out_done, 1)

        @block.vector
        def _(dve):
            lk = Links(dve, chain)
            for c in range(1, KD, 2):
                dve.wait_ge(xT_done, c + 1)
                dve.tensor_copy(hT[:, c, :], ps[:, c, 0:T]).then_inc(xT_copied_v, 1)
            dve.wait_ge(vec_done, 1)
            dve.tensor_copy(vecT[:], ps[:, 0, 0:NV]).then_inc(vec_copied, 1)
            dve.wait_ge(vec_copied, 1)

            def apply_norm(k, g0):
                dve.wait_ge(rinv_ready, k + 1)
                for c in range(KD):
                    dve.scalar_tensor_tensor(aT[:, c, :], hT[:, c, :], vecT[:, g0 + c:g0 + c + 1], rinv[:],
                                             ALU.mult, ALU.mult).then_inc(norm_ready, 1)

            l0, l1 = vecT[:, V_LB:V_LB + HH], vecT[:, V_LB + HH:V_LB + 2 * HH]
            lk.add(dve.tensor_tensor(lbt[:, 0], l0, l1, ALU.max))
            lk.wait()
            lk.add(dve.tensor_tensor(lbt[:, 1], l0, lbt[:, 0], ALU.subtract))
            dve.tensor_tensor(lbt[:, 2], l1, lbt[:, 0], ALU.subtract).then_inc(lb_ready, 1)
            apply_norm(0, V_MIX)
            dve.wait_ge(gs_done, 1)
            for u in range(PAIRS):
                lk.add(dve.tensor_scalar(gs[:, 0, u, :], ps[:, 5 + u, 0:T], vecT[:, V_BGK + u:V_BGK + u + 1], None, ALU.add))
            lk.wait()
            dve.scalar_tensor_tensor(gs[:, 1], gs[:, 0], -1.0, gs[:, 0], ALU.mult, ALU.max).then_inc(gs_bias, 1)
            dve.wait_ge(gs_exp, 1)
            lk.add(dve.scalar_tensor_tensor(gs[:, 0], gs[:, 0], 0.0, gs[:, 2], ALU.min, ALU.subtract))
            lk.wait()
            lk.add(dve.tensor_scalar(lam[:, 0:PAIRS, :], gs[:, 0], 1.0 / GLA_NORMALIZER, None, ALU.mult))
            dve.wait_ge(lb_exp, 1)
            lk.add(dve.tensor_tensor(lbt[:, 3], lbt[:, 1], lbt[:, 2], ALU.add))
            lk.wait()
            lk.add(dve.reciprocal(lbt[:, 3], lbt[:, 3]))
            lk.wait()
            lk.add(dve.tensor_tensor(lbt[:, 4], lbt[:, 1], lbt[:, 3], ALU.mult))
            lk.wait()
            lk.add(dve.tensor_scalar(lbt[:, 5], lbt[:, 4], -1.0, 1.0, ALU.mult, ALU.add))
            lk.wait()
            dve.wait_ge(sig_ready, 2)
            dve.wait_ge(z_copied, 3 * G)
            q2, f2 = z[:, Z_Q2:Z_Q2 + HH, :], z[:, Z_F2:Z_F2 + HH, :]
            lk.add(dve.tensor_tensor(q2, q2, e_q[:, PAIRS:KU, :], ALU.mult))
            for h in range(HH):
                lk.add(dve.tensor_scalar(lam[:, PAIRS + h, :], e_k[:, PAIRS + h, :], lbt[:, 5, h:h + 1], lbt[:, 4, h:h + 1],
                                         ALU.mult, ALU.add))
            lk.wait()
            dve.tensor_scalar(f2, lam[:, PAIRS:KU, :], -1.0, 1.0, ALU.mult, ALU.add).then_inc(forget_ready, 1)
            dve.wait_ge(sig_ready, 3)
            i2 = z[:, Z_I2:Z_I2 + HH, :]
            dve.tensor_tensor(i2, i2, e_end[:, PAIRS:KU, :], ALU.mult).then_inc(v_ready, 1)
            dve.wait_ge(lnf_ready, 1)
            for u in range(KU):
                ins = dve.tensor_tensor_scan(cum[:, u, :], reset[:], lam[:, u, :], 0.0, ALU.mult, ALU.add)
            ins.then_inc(cum_ready, 1)
            dve.wait_ge(cum_ready, 1)

            def by_chunk(a):
                return ((a[:, :, 0:L].rearrange("p u (n c) -> p u n c", c=CHUNK), NCH, CHUNK),
                        (a[:, :, L:T].rearrange("p u (n c) -> p u n c", c=SL), SB, SL))

            for (o, n, c), (i, _, _) in zip(by_chunk(lam), by_chunk(cum)):
                ref = i[:, :, :, c // 2:c // 2 + 1].to_broadcast([P, KU, n, c])
                ins = dve.tensor_tensor(o, i, ref, ALU.subtract)
            ins.then_inc(d1_ready, 1)
            dve.wait_ge(e_ready, 1)
            lk.add(dve.tensor_copy(dec[:, :, 0:NCH], e_b[:, :, CHUNK - 1:L:CHUNK]))
            lk.add(dve.tensor_copy(dec[:, :, NCH:NCH + SB], e_b[:, :, L + SL - 1:T:SL]))
            dve.wait_ge(e_ready, 3)
            for (o, n, c), (i, _, _) in zip(by_chunk(lam), by_chunk(cum)):
                last = i[:, :, :, c - 1:c].to_broadcast([P, KU, n, c])
                ins = dve.tensor_tensor(o, last, i, ALU.subtract)
            ins.then_inc(d3_ready, 1)
            for half in range(2):
                r = slice(half * GK, (half + 1) * GK)
                for pad, ex in ((qr_pad, e_q), (qb_pad, e_b)):
                    lk.add(dve.scalar_tensor_tensor(pad[r, :, half, :], z[r, Z_Q1:Z_Q1 + PAIRS, :], float(GK) ** -0.5,
                                                    ex[r, 0:PAIRS, :], ALU.mult, ALU.mult))
            lk.wait()
            for ex in (e_q, e_b):
                lk.add(dve.tensor_tensor(ex[:, PAIRS:KU, :], q2, ex[:, PAIRS:KU, :], ALU.mult))
            dve.wait_ge(e_ready, 4)
            for ex in (e_k, e_end):
                lk.add(dve.tensor_tensor(ex[:, 0:PAIRS, :], z[:, Z_K1:Z_K1 + PAIRS, :], ex[:, 0:PAIRS, :], ALU.mult))
                ins = dve.tensor_tensor(ex[:, PAIRS:KU, :], f2, ex[:, PAIRS:KU, :], ALU.mult)
            ins.then_inc(qk_ready, 1)
            dve.wait_ge(bias_done, 1)
            lk.add(dve.tensor_copy(bguT[:].rearrange("p e c -> p (e c)"), ps[:, 4, :]))
            lk.add(dve.tensor_copy(bdnT[:].rearrange("p e c -> p (e c)"), ps[:, 5, 0:E * KD]))
            dve.tensor_copy(pT[:], ps[:, 6:8, 0:T]).then_inc(bias_copied, 1)
            for t, (t0, n) in enumerate(tiles):
                dve.wait_ge(vt_done, t + 1)
                dve.tensor_copy(tok[0:n, t, :], ps[0:n, 2 * t:2 * t + 2, :].rearrange("p b n -> p (b n)")).then_inc(v_copied, 1)
            dve.wait_ge(att_zeroed, 2)
            for t, (t0, n) in enumerate(tiles):
                dve.wait_ge(ke_done, t + 1)
                src = ps[:, 2 * t:2 * t + 2, :].rearrange("p b n -> p (b n)")[:, 0:KU * P]
                if t < TT:
                    for half in range(2):
                        r = slice(half * CHUNK, (half + 1) * CHUNK)
                        dve.tensor_copy(kend_tok[r, t, half, :], src[r])
                else:
                    dve.tensor_copy(kend_smp[0:S, :], src[0:S]).then_inc(ke_copied, 1)
            dve.wait_ge(consts_ready, 11)
            for h in range(HEADS):
                dve.wait_ge(att_done, h + 1)
                for t in range(TT):
                    dve.copy_predicated(att[:, h, t * P:(t + 1) * P], maski[:, 0:P], ps[:, h % 4, t * P:(t + 1) * P])
                dve.copy_predicated(att[0:S, h, L:T], maski[0:S, P:P + S], ps[0:S, h % 4, L:T]).then_inc(att_masked, 1)
            k = 0
            for u in range(KU):
                parts = [(slice(0, GK), 0), (slice(GK, P), P)] if u < PAIRS else [(slice(0, P), 0)]
                for n0 in range(0, NCH, 2):
                    dve.wait_ge(u_done, k + 1)
                    for n in (n0, n0 + 1):
                        if n:
                            lk.wait()
                        for r, v0 in parts:
                            src = ps[r, 4 + k % 4, (n - n0) * 2 * P + v0:(n - n0) * 2 * P + v0 + P]
                            if n == 0:
                                lk.add(dve.tensor_copy(s_hist[r, u, 0, :], src))
                            else:
                                lk.add(dve.scalar_tensor_tensor(s_hist[r, u, n, :], s_hist[r, u, n - 1, :], dec[r, u, n:n + 1],
                                                                src, ALU.mult, ALU.add))
                    lk.wait()
                    dve.nop().then_inc(s_copied_u, 1)
                    k += 1
            dve.nop().then_inc(s_ready, 1)
            dve.wait_ge(sig_ready, 5)
            g1 = z[:, Z_G1:Z_G1 + GH, :]
            lk.add(dve.tensor_tensor(g1, g1, acc[:, 0:GH, :], ALU.mult))
            def sample_state(h):
                u = h // 2 if h < GH else h - GH + PAIRS
                st = s0[:, u % 2]
                dve.wait_ge(o_done, 2 * u + 2 if h < GH else h + 1)
                if h >= GH or h % 2 == 0:
                    lk.add(dve.tensor_tensor(st, st, dec[:, u, NCH:NCH + SB].unsqueeze(2).to_broadcast([P, SB, P]), ALU.mult))
                    lk.wait()
                r = slice((h % 2) * GK, (h % 2 + 1) * GK) if h < GH else slice(0, P)
                dve.wait_ge(su_done, h + 1)
                b = 4 + 2 * (h % 2)
                src = ps[r, b:b + 2, :].rearrange("p b (s v) -> p (b s) v", v=P)
                dve.tensor_tensor(st[r], st[r], src, ALU.add).then_inc(su_used, 1)

            def head_norm(h):
                dve.wait_ge(orinv_ready, h + 1)
                dve.wait_ge(o_copied, h + 1)
                gn = vecT[:, V_GN + (h >= GH):V_GN + (h >= GH) + 1]
                lk.add(dve.scalar_tensor_tensor(o_raw[:, h, :], o_raw[:, h, :], gn, aT[:, h, :], ALU.mult, ALU.mult))
                lk.wait()
                dve.tensor_tensor(acc[:, h, :], o_raw[:, h, :], z[:, Z_G1 + h, :], ALU.mult).then_inc(o_ready, 1)

            for h in range(HEADS):
                if h % 2 == 1 or h >= GH:
                    if h < GH:
                        sample_state(h - 1)
                    sample_state(h)
            for h in range(HEADS):
                head_norm(h)
            for c in range(KD):
                dve.wait_ge(h_done, c + 1)
                dve.tensor_tensor(hT[:, c, :], hT[:, c, :], ps[:, 4 + c % 4, 0:T], ALU.add).then_inc(h_ready, 1)
            dve.wait_ge(h_ready, KD)
            apply_norm(1, V_FFN)
            dve.wait_ge(small_loaded, 16 * 4)
            dve.wait_ge(lg_done, 1)
            for t, (t0, n) in enumerate(tiles):
                lk.add(dve.tensor_tensor(logit[0:n, t, :], ps[0:n, 6, t * E:(t + 1) * E], b_rt[0:n, :], ALU.add))
            lk.wait()
            for t, (t0, n) in enumerate(tiles):
                lk.add(dve.max(top8[0:n, t, :], logit[0:n, t, :]))
            lk.wait()
            for t, (t0, n) in enumerate(tiles):
                lk.add(dve.max_index(idx8[0:n, t, :], top8[0:n, t, :], logit[0:n, t, :]))
            dve.tensor_tensor(pk[:], top8[:, :, 0:TOPK], top8[:, :, 0:1].to_broadcast([P, NT, TOPK]), ALU.subtract) \
                .then_inc(pk_ready, 1)
            lk.wait()
            lk.add(dve.tensor_scalar(idxf[:], idx8[:, :, 0:TOPK], 1.0, None, ALU.add))
            lk.wait()
            lk.add(dve.tensor_tensor(onehot[:].rearrange("p t k e -> p (t k) e"),
                                     iota1[:, 0:E].unsqueeze(1).to_broadcast([P, NT * TOPK, E]),
                                     idxf[:].rearrange("p t k -> p (t k)").unsqueeze(2).to_broadcast([P, NT * TOPK, E]), ALU.is_equal))
            lk.wait()
            dve.tensor_reduce(memb[:], onehot[:].rearrange("p t k e -> p t e k"), AX_X, ALU.add).then_inc(memb_ready, 1)
            dve.wait_ge(pk_exp, 1)
            lk.add(dve.tensor_reduce(psum_k[:, :, 0:1], pk[:], AX_X, ALU.add))
            lk.wait()
            lk.add(dve.reciprocal(psum_k[:, :, 1:2], psum_k[:, :, 0:1]))
            lk.wait()
            lk.add(dve.tensor_tensor(pk[:], pk[:], psum_k[:, :, 1:2].to_broadcast([P, NT, TOPK]), ALU.mult))
            lk.wait()
            lk.add(dve.tensor_tensor(gated[:].rearrange("p t k e -> p (t k) e"), onehot[:].rearrange("p t k e -> p (t k) e"),
                                     pk[:].rearrange("p t k -> p (t k)").unsqueeze(2).to_broadcast([P, NT * TOPK, E]), ALU.mult))
            lk.wait()
            lk.add(dve.tensor_reduce(gate_e[:], gated[:].rearrange("p t k e -> p t e k"), AX_X, ALU.add))
            dve.wait_ge(rank_done, 1)
            for t, (t0, n) in enumerate(tiles):
                lk.add(dve.scalar_tensor_tensor(rankp[0:n, t, :], ps[0:n, 7, t * E:(t + 1) * E], 1.0, memb[0:n, t, :],
                                                ALU.add, ALU.mult))
            lk.add(dve.tensor_copy(cnt_f[:, 0:E], ps[0:1, 7, NT * E:(NT + 1) * E]))
            lk.wait()
            lk.add(dve.tensor_reduce(cnt_f[:, E:E + 1], cnt_f[:, 0:E], AX_X, ALU.max))
            lk.wait()
            dve.tensor_copy(cnt_i[:], cnt_f[:]).then_inc(cnt_ready, 1)

            def add_combined(n):
                for c in range(KD):
                    dve.wait_ge(cb_done, n * KD + (c + 1))
                    dve.tensor_tensor(acc[:, c, :], acc[:, c, :], ps[:, 6 + c % 2, 0:T], ALU.add).then_inc(acc_added, 1)

            LINKS = 6

            def expert(n, e, j):
                bk = Links(dve, moe_chain, n * LINKS)
                io_ = iota1[:, 0:SLOTS] if isinstance(j, int) else iota1[:, bass.ds(j * SLOTS, SLOTS)]
                for (a, b, m) in ((0, TT, P), (TT, NT, S)):
                    bk.add(dve.tensor_tensor(sel[0:m, a:b, :], io_[0:m].unsqueeze(1).to_broadcast([m, b - a, SLOTS]),
                                             rankp[0:m, a:b, bass.ds(e, 1)].to_broadcast([m, b - a, SLOTS]), ALU.is_equal))
                bk.wait()
                dve.tensor_tensor(selg[0:P, 0:TT, :], sel[0:P, 0:TT, :], gate_e[0:P, 0:TT, bass.ds(e, 1)].to_broadcast([P, TT, SLOTS]),
                                  ALU.mult)
                dve.tensor_tensor(selg[0:S, TT:NT, :], sel[0:S, TT:NT, :],
                                  gate_e[0:S, TT:NT, bass.ds(e, 1)].to_broadcast([S, 1, SLOTS]), ALU.mult).then_inc(sel_ready, 1)
                dve.wait_ge(u_used, n * UNITS + KD)
                pg = ps[:, 0, :].rearrange("p (c s) -> p c s", s=SLOTS)
                pu = ps[:, 1, :].rearrange("p (c s) -> p c s", s=SLOTS)
                bk.add(dve.tensor_tensor(gbuf, pg, bguT[:, bass.ds(e, 1), 0:KF].rearrange("p a c -> p (a c)").unsqueeze(2)
                                         .to_broadcast([P, KF, SLOTS]), ALU.add))
                bk.wait()
                dve.tensor_scalar(gbuf, gbuf, SWIGLU_LIMIT, None, ALU.min).then_inc(gate_ready, 1)
                bk.add(dve.tensor_tensor(ubuf, pu, bguT[:, bass.ds(e, 1), KF:2 * KF].rearrange("p a c -> p (a c)").unsqueeze(2)
                                         .to_broadcast([P, KF, SLOTS]), ALU.add))
                bk.wait()
                bk.add(dve.tensor_scalar(ubuf, ubuf, -SWIGLU_LIMIT, SWIGLU_LIMIT, ALU.max, ALU.min))
                dve.wait_ge(sigm_ready, n + 1)
                dve.wait_ge(gate_ready, n + 1)
                bk.add(dve.tensor_tensor(sbuf, sbuf, gbuf, ALU.mult))
                bk.wait()
                dve.scalar_tensor_tensor(hid, ubuf, 1.0, sbuf, ALU.add, ALU.mult).then_inc(hid_ready, 1)
                add_combined(n)
                dve.wait_ge(u_used, n * UNITS + UNITS)
                dve.tensor_tensor(yT, ps[:, 3, :].rearrange("p (c s) -> p c s", s=SLOTS),
                                  bdnT[:, bass.ds(e, 1), :].rearrange("p a c -> p (a c)").unsqueeze(2).to_broadcast([P, KD, SLOTS]),
                                  ALU.add).then_inc(y_copied, 1)
                dve.wait_ge(st_done, n + 1)
                assert bk.n == LINKS

            dve.wait_ge(zero_ready, 1)
            dve.wait_ge(bias_copied, 1)
            with dve.Fori(0, E) as e:
                expert(e, e, 0)
            n = overflow_blocks(dve, expert)
            add_combined(n)
            dve.wait_ge(acc_added, n * KD + KD)
            dve.tensor_tensor(hT[:], hT[:], acc[:], ALU.add).then_inc(h_ready, 1)
            dve.wait_ge(h_ready, KD + 1)
            apply_norm(2, V_PLE)
            for c in range(KD):
                dve.wait_ge(pg_sig, c + 1)
                b = c % 4
                dve.tensor_tensor(acc[:, c, :], acc[:, c, :], ps[:, 4 + b, 0:T], ALU.mult).then_inc(pg_used, 1)
            dve.wait_ge(pg_used, KD)
            dve.tensor_tensor(hT[:], hT[:], acc[:], ALU.add).then_inc(h_ready, 1)
            dve.wait_ge(h_ready, KD + 2)
            apply_norm(3, V_FIN)


_INS = ["x_prompt", "x_sample", "p_prompt", "p_sample", "state_gla", "state_hgrn", "g_mix", "w_in", "w_gk2", "b_gk2",
        "gn_gla", "lb_logits", "gn_hgrn", "w_out", "g_ffn", "w_router", "b_router", "w_gu", "b_gu", "w_dn", "b_dn",
        "g_ple", "w_ple_gate", "w_ple_proj", "g_final"]


def kernel(**inputs):
    import numpy as np
    import concourse.bacc as bacc
    from concourse.bass_utils import run_bass_kernel_spmd

    nc = bacc.Bacc("TRN2", target_bir_lowering=False, num_devices=1)
    arrays, io = {}, {}
    for name in _INS:
        a = np.ascontiguousarray(inputs[name])
        arrays[f"in_{name}"] = a
        io[name] = nc.dram_tensor(f"in_{name}", a.shape, mybir.dt.from_np(a.dtype), kind="ExternalInput").ap()
    sg, sh = inputs["state_gla"].shape, inputs["state_hgrn"].shape
    nb = inputs["x_prompt"].shape[0]
    shapes = [inputs["x_prompt"].shape, inputs["x_sample"].shape, (sg[0], nb) + tuple(sg[2:]), (sh[0], nb) + tuple(sh[2:]), sg, sh]
    out = [nc.dram_tensor(f"out_{i}", tuple(s), F32, kind="ExternalOutput").ap() for i, s in enumerate(shapes)]
    build(nc, io, out)
    r = run_bass_kernel_spmd(nc, [arrays], core_ids=[0])
    return tuple(r.results[0][f"out_{i}"] for i in range(len(shapes)))
```

```python
from contextlib import ExitStack

import concourse.bass as bass
from concourse import mybir

F32 = mybir.dt.float32
I32 = mybir.dt.int32
U32 = mybir.dt.uint32
ALU = mybir.AluOpType
ACT = mybir.ActivationFunctionType
AX_X = mybir.AxisListType.X

P = 128
BANK = 512
EPS = 1e-6
SLOTS = 64
SWIGLU_LIMIT = 7.0
SWIGLU_ALPHA = 1.702
GLA_NORMALIZER = 16.0
CHUNK = 64


class Links:

    def __init__(self, eng, sem, base=0):
        self.eng, self.sem, self.base, self.n = eng, sem, base, 0

    def add(self, ins):
        self.n += 1
        ins.then_inc(self.sem, 1)

    def wait(self):
        self.eng.wait_ge(self.sem, self.base + self.n)


def build(nc, io, out):
    D = io["x_prompt"].shape[2]
    L = io["x_prompt"].shape[1]
    SB, SL = io["x_sample"].shape[:2]
    S = SB * SL
    T = L + S
    E = io["w_router"].shape[2]
    FF = io["w_dn"].shape[2]
    PLE = io["w_ple_proj"].shape[1]
    GH, GK, GV = io["state_gla"].shape[2:]
    HH, HK, HV = io["state_hgrn"].shape[2:]
    RANK = io["w_gk2"].shape[1]
    KD = D // P
    KF = FF // P
    TT = L // P
    NT = TT + 1
    NCH = L // CHUNK
    PAIRS = GH * GK // P
    HEADS = GH + HH
    KU = PAIRS + HH
    TOPK = 4
    BLOCKS = -(-T // SLOTS)
    assert GV == HV == HK == P and GK * 2 == P and L == TT * P and S <= 32 and BANK >= T

    tiles = [(t * P, P) for t in range(TT)] + [(L, S)]

    G = 4
    c_q1 = 0
    c_v1 = 2 * GH * GK
    c_g1 = c_v1 + GH * GV
    c_r1 = c_g1 + GH * GV
    c_q2 = c_r1 + RANK
    c_f2 = c_q2 + HH * HK
    c_i2 = c_f2 + HH * HK
    c_g2 = c_i2 + HH * HV
    group_cols = [c_q1, c_q2, c_f2, c_v1, c_i2, c_g1, c_g2]
    NG = len(group_cols)
    Z_Q1, Z_K1, Z_Q2, Z_F2, Z_V, Z_I2, Z_G1, Z_G2 = 0, 2, 4, 8, 12, 16, 20, 24
    NZ = NG * G
    WSLOTS = 4

    UNITS = KD + KF // 2
    UCOLS = 2 * FF
    assert 2 * FF == 2 * D

    with ExitStack() as ctx:
        def sb(name, shape, dt=F32):
            return ctx.enter_context(nc.sbuf_tensor(name, shape, dt))

        def sem(name):
            return ctx.enter_context(nc.semaphore(name))

        ring = sb("ring", [P, UNITS * UCOLS])
        at = [0]

        def carve(*dims):
            n = 1
            for d in dims:
                n *= d
            v = ring[:, at[0]:at[0] + n]
            at[0] += n
            if len(dims) == 1:
                return v
            names = "abcd"[:len(dims)]
            return v.rearrange("p (" + " ".join(names) + ") -> p " + " ".join(names),
                               **{k: d for k, d in zip(names, dims)})

        z = carve(NZ, T)
        decay_start = at[0]
        lam = carve(KU, T)
        cum = carve(KU, T)
        at[0] = decay_start
        kend_tok = carve(TT, 2, KU * P)
        kend_smp = carve(KU * P)
        e_q = carve(KU, T)
        e_k = carve(KU, T)
        e_end = carve(KU, T)
        e_b = carve(KU, T)
        qr_pad = carve(PAIRS, 2, T)
        qb_pad = carve(PAIRS, 2, T)
        hist_start = at[0]
        s_hist = carve(KU, NCH, P)
        assert at[0] <= UNITS * UCOLS
        at[0] = hist_start
        gs = carve(3, PAIRS, T)
        p_tok = carve(NT, PLE)
        assert at[0] <= hist_start + KU * NCH * P
        assert at[0] <= UNITS * UCOLS
        att = z[:, 0:HEADS, :]
        o_raw = z[:, Z_V:Z_V + HEADS, :]

        wst = sb("wst", [P, WSLOTS, KD, P])
        blk = wst[:].rearrange("p a b c -> p (a b c)")
        bc = KD * SLOTS
        xrow, xsel, gbuf, ubuf, sbuf, hid, hidT, yrow = (blk[:, i * bc:(i + 1) * bc] for i in range(8))
        assert 8 * bc <= WSLOTS * KD * P and KF == KD and bc == BANK == D // 2 == FF // 2
        tok = sb("tok", [P, NT, D])
        hT = sb("hT", [P, KD, T])
        aT = sb("aT", [P, KD, T])
        acc = sb("acc", [P, KD, T])
        s0 = sb("s0", [P, 2, SB, P])
        vmask = sb("vmask", [32, 2, SB, P])
        rinv = sb("rinv", [P, T])
        lnbuf = sb("lnbuf", [P, T])
        ident = sb("ident", [P, P])
        ones = sb("ones", [P, P])
        upper = sb("upper", [P, P])
        reset = sb("reset", [P, T])
        maskf = sb("maskf", [P, P + 32])
        maski = sb("maski", [P, P + 32], I32)
        b_dn = vmask[0:E, 0].rearrange("e b v -> e (b v)")
        seqmask = sb("seqmask", [32, SB])
        iota_i = ring[:, 0:BLOCKS * SLOTS].bitcast(I32)
        iota1 = sb("iota1", [P, BLOCKS * SLOTS])
        eps = sb("eps", [P, 1])
        NV = 4 * KD + PAIRS + 2 * HH + 2
        vec_rows = sb("vec_rows", [NV, P])
        vecT = sb("vecT", [P, NV])
        V_MIX, V_FFN, V_PLE, V_FIN, V_BGK = 0, KD, 2 * KD, 3 * KD, 4 * KD
        V_LB = V_BGK + PAIRS
        V_GN = V_LB + 2 * HH
        lbt = sb("lbt", [P, 6, HH])
        r1w = sb("r1w", [P, KD, RANK])
        r1T = sb("r1T", [RANK, T])
        gk2 = sb("gk2", [RANK, GH * GK])
        dec = sb("dec", [P, KU, NCH + SB])
        w_rt = sb("w_rt", [P, KD, E])
        b_rt = sb("b_rt", [P, E])
        bgu = sb("bgu", [P, 2 * FF])
        ehot = sb("ehot", [P, SLOTS])
        pT = sb("pT", [P, PLE // P, T])
        w_pp = sb("w_pp", [P, PLE // P, D])
        logit = sb("logit", [P, NT, E])
        top8 = sb("top8", [P, NT, 8])
        idx8 = sb("idx8", [P, NT, 8], U32)
        idxf = sb("idxf", [P, NT, TOPK])
        pk = sb("pk", [P, NT, TOPK])
        psum_k = sb("psum_k", [P, NT, 2])
        onehot = sb("onehot", [P, NT, TOPK, E])
        gated = sb("gated", [P, NT, TOPK, E])
        gate_e = sb("gate_e", [P, NT, E])
        memb = sb("memb", [P, NT, E])
        rankp = sb("rankp", [P, NT, E])
        cnt_f = sb("cnt_f", [1, E + 1])
        cnt_i = sb("cnt_i", [1, E + 1], I32)
        sel = sb("sel", [P, NT, SLOTS])
        selg = sb("selg", [P, NT, 2, SLOTS])
        selT = sb("selT", [P, T])
        gateT = sb("gateT", [E, T])

        ps = ctx.enter_context(nc.psum_tensor("ps", [P, 8, BANK], F32))

        x_loaded = sem("x_loaded")
        vec_loaded = sem("vec_loaded")
        small_loaded = sem("small_loaded")
        r1w_loaded = sem("r1w_loaded")
        ple_loaded = sem("ple_loaded")
        pool_link = sem("pool_link")
        consts_ready = sem("consts_ready")
        xT_done = sem("xT_done")
        xT_copied_a = sem("xT_copied_a")
        xT_copied_v = sem("xT_copied_v")
        vec_done = sem("vec_done")
        vec_copied = sem("vec_copied")
        pT_done = sem("pT_done")
        pT_copied = sem("pT_copied")
        bgu_loaded = sem("bgu_loaded")
        bdn_loaded = sem("bdn_loaded")
        gateT_done = sem("gateT_done")
        gateT_copied = sem("gateT_copied")
        bd_done = sem("bd_done")
        acc_ready = sem("acc_ready")
        sq_ready = sem("sq_ready")
        ss_ready = sem("ss_ready")
        act_link = sem("act_link")
        rinv_ready = sem("rinv_ready")
        norm_ready = sem("norm_ready")
        r1_done = sem("r1_done")
        r1_copied = sem("r1_copied")
        gs_done = sem("gs_done")
        gs_bias = sem("gs_bias")
        gs_exp = sem("gs_exp")
        w_loaded = [sem(f"w_loaded{i}") for i in range(WSLOTS)]
        z_done = sem("z_done")
        z_copied = sem("z_copied")
        sig_ready = sem("sig_ready")
        chain = sem("chain")
        forget_ready = sem("forget_ready")
        lnf_ready = sem("lnf_ready")
        d1_ready = sem("d1_ready")
        e_ready = sem("e_ready")
        d3_ready = sem("d3_ready")
        cum_ready = sem("cum_ready")
        qk_ready = sem("qk_ready")
        v_ready = sem("v_ready")
        vt_done = sem("vt_done")
        v_copied = sem("v_copied")
        ke_done = sem("ke_done")
        ke_copied = sem("ke_copied")
        att_zeroed = sem("att_zeroed")
        att_done = sem("att_done")
        att_masked = sem("att_masked")
        u_done = sem("u_done")
        s_ready = sem("s_ready")
        o_done = sem("o_done")
        o_copied = sem("o_copied")
        osq_ready = sem("osq_ready")
        oss_ready = sem("oss_ready")
        oln_ready = sem("oln_ready")
        orinv_ready = sem("orinv_ready")
        gates_ready = sem("gates_ready")
        o_ready = sem("o_ready")
        s0_loaded = [sem("s0_loaded0"), sem("s0_loaded1")]
        vm_ready = sem("vm_ready")
        su_done = sem("su_done")
        su_used = sem("su_used")
        s_copied_u = sem("s_copied_u")
        lb_ready = sem("lb_ready")
        lb_exp = sem("lb_exp")
        s0_stored = sem("s0_stored")
        sp_stored = sem("sp_stored")
        h_done = sem("h_done")
        h_ready = sem("h_ready")
        xn_done = sem("xn_done")
        xn_copied = sem("xn_copied")
        lg_done = sem("lg_done")
        pk_ready = sem("pk_ready")
        gate_done = sem("gate_done")
        pk_exp = sem("pk_exp")
        memb_ready = sem("memb_ready")
        rank_done = sem("rank_done")
        cnt_ready = sem("cnt_ready")
        p_done = sem("p_done")
        p_copied = sem("p_copied")
        u_loaded = [sem(f"u_loaded{i}") for i in range(UNITS)]
        u_used = sem("u_used")
        sel_ready = sem("sel_ready")
        selg_ready = sem("selg_ready")
        xs_done = sem("xs_done")
        xs_copied = sem("xs_copied")
        gate_ready = sem("gate_ready")
        sigm_ready = sem("sigm_ready")
        hid_ready = sem("hid_ready")
        xsT_done = sem("xsT_done")
        xsel_copied = sem("xsel_copied")
        hT_done = sem("hT_done")
        hT_copied = sem("hT_copied")
        yr_copied = sem("yr_copied")
        st_done = sem("st_done")
        st_copied = sem("st_copied")
        cb_done = sem("cb_done")
        acc_added = sem("acc_added")
        moe_chain = sem("moe_chain")
        pg_loaded = sem("pg_loaded")
        pg_done = sem("pg_done")
        pg_sig = sem("pg_sig")
        pg_used = sem("pg_used")
        out_done = sem("out_done")
        out_copied = sem("out_copied")
        out_stored = sem("out_stored")

        block = ctx.enter_context(nc.Block())

        CB_BANKS = (6, 6, 2, 6)

        def unit_src(e, c):
            if c < KD:
                return io["w_gu"][0, e, c * P:(c + 1) * P, :]
            c = 2 * (c - KD)
            return io["w_dn"][0, e, c * P:(c + 2) * P, :].rearrange("(c p) n -> p c n", p=P)

        def unit_dst(c):
            v = ring[:, c * UCOLS:(c + 1) * UCOLS]
            return v if c < KD else v.rearrange("p (c n) -> p c n", c=2)

        def overflow_blocks(eng, body):
            n = eng.alloc_register(f"blocks_{eng.engine.name}")
            eng.reg_mov(n, E)
            eng.wait_ge(cnt_ready, 1)
            most = eng.value_load(cnt_i[0:1, E:E + 1], min_val=0, max_val=T)
            with eng.If(most > SLOTS):
                with eng.Fori(0, E) as e:
                    c = eng.value_load(cnt_i[0:1, bass.ds(e, 1)], min_val=0, max_val=T)
                    with eng.Fori(1, BLOCKS) as j:
                        with eng.If(c > j * SLOTS):
                            body(eng.snap(n, min_val=E, max_val=E * BLOCKS), e, j)
                            eng.reg_add(n, n, 1)
            return eng.snap(n, min_val=E, max_val=E * BLOCKS)

        @block.sync
        def _(sp):
            cols = [(io["w_in"], c0 + j * P) for c0 in group_cols for j in range(G)]
            cols += [(io["w_out"], j * P) for j in range(KD)]

            def load_cols(i):
                w, c0 = cols[i]
                if i >= WSLOTS:
                    last = i - WSLOTS
                    if last < NZ:
                        sp.wait_ge(z_done, last + 1)
                    else:
                        sp.wait_ge(h_done, last - NZ + 1)
                sp.dma_start(wst[:, i % WSLOTS], w[0, :, c0:c0 + P].rearrange("(c p) n -> p c n", p=P)) \
                    .then_inc(w_loaded[i % WSLOTS], 16)

            def state_dram(gla, hgrn, u):
                if u < PAIRS:
                    return gla[0][:, 2 * u:2 * u + 2].rearrange("b h k v -> (h k) b v")
                return hgrn[0][:, u - PAIRS].rearrange("b k v -> k b v")

            def load_state(u):
                sp.dma_start(s0[:, u % 2], state_dram(io["state_gla"], io["state_hgrn"], u)).then_inc(s0_loaded[u % 2], 16)

            for i in range(NZ + WSLOTS):
                load_cols(i)
                if i == NZ // 2:
                    load_state(0)
                    load_state(1)
            sp.wait_ge(s_ready, 1)
            sp.dma_start(out[2][0, 0].rearrange("(u h) k v -> (h k) u v", h=2), s_hist[:, 0:PAIRS, NCH - 1, :]) \
                .then_inc(sp_stored, 16)
            sp.dma_start(out[3][0, 0].rearrange("h k v -> k h v"), s_hist[:, PAIRS:KU, NCH - 1, :]).then_inc(sp_stored, 16)
            for u in range(KU):
                sp.wait_ge(su_used, 2 * u + 2 if u < PAIRS else GH + u - PAIRS + 1)
                sp.dma_start(state_dram(out[4], out[5], u), s0[:, u % 2]).then_inc(s0_stored, 16)
                if u + 2 < KU:
                    sp.wait_ge(s0_stored, 16 * (u + 1))
                    load_state(u + 2)
            sp.wait_ge(su_done, HEADS)
            sp.dma_start(b_dn, io["b_dn"][0]).then_inc(bdn_loaded, 16)
            sp.wait_ge(o_ready, HEADS)
            sp.wait_ge(sp_stored, 16 * 2)
            for c in range(UNITS):
                if c < KD - WSLOTS:
                    load_cols(NZ + WSLOTS + c)
                sp.dma_start(unit_dst(c), unit_src(0, c)).then_inc(u_loaded[c], 16)

            def load_block(n, e, j):
                for c in range(UNITS):
                    sp.wait_ge(u_used, n * UNITS + (c + 1 - UNITS))
                    sp.dma_start(unit_dst(c), unit_src(e, c)).then_inc(u_loaded[c], 16)

            with sp.Fori(1, E) as e:
                load_block(e, e, 0)
            n = overflow_blocks(sp, load_block)
            for c in range(KD // 2):
                sp.wait_ge(u_used, n * UNITS + (c + 1 - UNITS))
                sp.dma_start(ring[:, c * UCOLS:(c + 1) * UCOLS].rearrange("p (c n) -> p c n", c=2),
                             io["w_ple_gate"][0, 2 * c * P:(2 * c + 2) * P, :].rearrange("(c p) n -> p c n", p=P)) \
                    .then_inc(pg_loaded, 16)
            sp.wait_ge(out_copied, NT)
            sp.dma_start(out[0][0].rearrange("(t p) d -> p t d", p=P), tok[:, 0:TT, :]).then_inc(out_stored, 16)
            sp.dma_start(out[1].rearrange("b l d -> (b l) d"), tok[0:S, TT, :]).then_inc(out_stored, 16)
            sp.wait_ge(out_stored, 32)
            sp.wait_ge(s0_stored, 16 * KU)

        @block.gpsimd
        def _(pool):
            lk = Links(pool, pool_link)
            lk.add(pool.memset(ident[:], 0.0))
            lk.add(pool.memset(ones[:], 1.0))
            lk.add(pool.memset(reset[:], 1.0))
            lk.add(pool.memset(maskf[:], 1.0))
            lk.add(pool.memset(seqmask[:], 1.0))
            lk.add(pool.memset(eps[:], EPS))
            lk.add(pool.memset(bgu[:], 0.0))
            lk.add(pool.iota(iota_i, pattern=[[1, BLOCKS * SLOTS]], base=1, channel_multiplier=0))
            lk.wait()
            pool.affine_select(out=ident[:], in_=ident[:], compare_op=ALU.not_equal, fill=1.0, base=0,
                               pattern=[[-1, P]], channel_multiplier=1).then_inc(consts_ready, 1)
            pool.dma_start(bgu[0:E, :], io["b_gu"][0]).then_inc(bgu_loaded, 16)
            pool.affine_select(out=upper[:], in_=ones[:], compare_op=ALU.is_gt, fill=0.0, base=0,
                               pattern=[[1, P]], channel_multiplier=-1).then_inc(consts_ready, 1)
            pool.memset(reset[:, 0:L].rearrange("p (n c) -> p n c", c=CHUNK)[:, :, 0:1], 0.0).then_inc(consts_ready, 1)
            pool.memset(reset[:, L:T].rearrange("p (n c) -> p n c", c=SL)[:, :, 0:1], 0.0).then_inc(consts_ready, 1)
            lk.add(pool.affine_select(out=maskf[:], in_=maskf[:], compare_op=ALU.is_ge, fill=0.0, base=0,
                                      pattern=[[1, P + 32]], channel_multiplier=-1))
            lk.wait()
            lk.add(pool.memset(maskf[0:CHUNK, CHUNK:P], 0.0))
            lk.add(pool.affine_select(out=maskf[0:32, P:P + 32], in_=ones[0:32, 0:32], compare_op=ALU.is_ge, fill=0.0,
                                      base=0, pattern=[[1, 32]], channel_multiplier=-1))
            lk.wait()
            lk.add(pool.affine_select(out=maskf[0:32, P:P + 32], in_=maskf[0:32, P:P + 32], compare_op=ALU.is_ge,
                                      fill=0.0, base=0, pattern=[[-SL, 32 // SL], [0, SL]], channel_multiplier=1))
            lk.add(pool.affine_select(out=seqmask[:], in_=seqmask[:], compare_op=ALU.is_ge, fill=0.0, base=0,
                                      pattern=[[-SL, SB]], channel_multiplier=1))
            lk.wait()
            pool.affine_select(out=seqmask[:], in_=seqmask[:], compare_op=ALU.is_ge, fill=0.0, base=SL - 1,
                               pattern=[[SL, SB]], channel_multiplier=-1).then_inc(consts_ready, 1)
            pool.tensor_copy(maski[:], maskf[:]).then_inc(consts_ready, 1)
            pool.tensor_copy(iota1[:], iota_i).then_inc(consts_ready, 1)
            pool.memset(qr_pad, 0.0).then_inc(consts_ready, 1)
            pool.memset(qb_pad, 0.0).then_inc(consts_ready, 1)
            pool.memset(idx8[:], 0).then_inc(consts_ready, 1)
            pool.memset(top8[:], 0.0).then_inc(consts_ready, 1)
            pool.memset(selT[:], 0.0).then_inc(st_copied, 1)
            pool.wait_ge(qk_ready, 1)
            pool.memset(att, 0.0).then_inc(att_zeroed, 1)
            pool.memset(kend_tok, 0.0).then_inc(att_zeroed, 1)
            for h in range(HEADS):
                if h == 0:
                    pool.wait_ge(v_copied, NT)
                if h >= 2:
                    pool.wait_ge(su_done, h - 1)
                pool.tensor_tensor(vmask[0:S, h % 2], tok[0:S, TT, h * P:(h + 1) * P].unsqueeze(1).to_broadcast([S, SB, P]),
                                   seqmask[0:S, :].unsqueeze(2).to_broadcast([S, SB, P]), ALU.mult).then_inc(vm_ready, 1)
            pool.wait_ge(h_done, KD)
            pool.memset(yrow, 0.0).then_inc(yr_copied, 1)

        @block.scalar
        def _(act):
            lk = Links(act, act_link)
            act.dma_start(tok[:, 0:TT, :], io["x_prompt"][0].rearrange("(t p) d -> p t d", p=P)).then_inc(x_loaded, 16)
            act.dma_start(tok[0:S, TT, :], io["x_sample"].rearrange("b l d -> (b l) d")).then_inc(x_loaded, 16)
            row = 0
            for name, n in (("g_mix", KD), ("g_ffn", KD), ("g_ple", KD), ("g_final", KD), ("b_gk2", PAIRS),
                            ("lb_logits", 2 * HH), ("gn_gla", 1), ("gn_hgrn", 1)):
                a = io[name]
                src = a.rearrange("(r p) -> r p", p=P) if len(a.shape) == 1 else a.rearrange("a (r p) -> (a r) p", p=P)
                act.dma_start(vec_rows[row:row + n, :], src).then_inc(vec_loaded, 16)
                row += n
            act.dma_start(r1w[:], io["w_in"][0, :, c_r1:c_r1 + RANK].rearrange("(c p) n -> p c n", p=P)).then_inc(r1w_loaded, 16)
            act.dma_start(gk2[:], io["w_gk2"][0]).then_inc(r1w_loaded, 16)
            act.dma_start(w_rt[:], io["w_router"][0].rearrange("(c p) n -> p c n", p=P)).then_inc(small_loaded, 16)
            act.dma_start(b_rt[:], io["b_router"][0:1, :].to_broadcast([P, E])).then_inc(small_loaded, 16)
            act.dma_start(p_tok[:, 0:TT, :], io["p_prompt"][0, 0].rearrange("(t p) d -> p t d", p=P)).then_inc(ple_loaded, 16)
            act.dma_start(p_tok[0:S, TT, :], io["p_sample"][0].rearrange("b l d -> (b l) d")).then_inc(ple_loaded, 16)
            act.dma_start(w_pp[:], io["w_ple_proj"][0].rearrange("(c p) n -> p c n", p=P)).then_inc(ple_loaded, 16)

            for c in range(0, KD, 2):
                act.wait_ge(xT_done, c + 1)
                act.copy(hT[:, c, :], ps[:, c, 0:T]).then_inc(xT_copied_a, 1)

            def inv_rms(k, src, sqbuf):
                act.activation(sqbuf, src, ACT.Square).then_inc(sq_ready, 1)
                act.wait_ge(ss_ready, k + 1)
                lk.add(act.activation(lnbuf[:], ps[:, 7, 0:T], ACT.Ln, bias=eps[:, 0:1], scale=1.0 / D))
                lk.wait()
                act.activation(rinv[:], lnbuf[:], ACT.Exp, scale=-0.5).then_inc(rinv_ready, 1)

            act.wait_ge(xT_copied_v, KD // 2)
            act.wait_ge(xT_copied_a, KD // 2)
            act.wait_ge(consts_ready, 11)
            inv_rms(0, hT[:], acc[:])

            act.wait_ge(lb_ready, 1)
            act.activation(lbt[:, 1:3], lbt[:, 1:3], ACT.Exp).then_inc(lb_exp, 1)
            act.wait_ge(r1_done, 1)
            act.copy(r1T[:], ps[0:RANK, 7, 0:T]).then_inc(r1_copied, 1)
            act.wait_ge(gs_bias, 1)
            lk.add(act.activation(gs[:, 2], gs[:, 1], ACT.Exp, scale=-1.0))
            lk.wait()
            act.activation(gs[:, 2], gs[:, 2], ACT.Ln, bias=ones[:, 0:1], scale=1.0).then_inc(gs_exp, 1)

            def copy_groups(g0, g1):
                with act.Fori(g0, g1) as g:
                    for j in range(G):
                        act.wait_ge(z_done, g * G + (j + 1))
                        act.copy(z[:, bass.ds(g * G + j, 1), :], ps[:, j:j + 1, 0:T]).then_inc(z_copied, 1)

            copy_groups(0, 3)
            act.wait_ge(z_copied, 3 * G)
            act.activation(e_q[:, 2:6, :], z[:, Z_Q2:Z_Q2 + G, :], ACT.Sigmoid).then_inc(sig_ready, 1)
            act.activation(e_k[:, 2:6, :], z[:, Z_F2:Z_F2 + G, :], ACT.Sigmoid).then_inc(sig_ready, 1)
            copy_groups(3, 5)
            act.wait_ge(z_copied, 5 * G)
            act.activation(e_end[:, 2:6, :], z[:, Z_I2:Z_I2 + G, :], ACT.Sigmoid).then_inc(sig_ready, 1)
            act.wait_ge(forget_ready, 1)
            act.activation(lam[:, PAIRS:KU, :], lam[:, PAIRS:KU, :], ACT.Ln).then_inc(lnf_ready, 1)
            act.wait_ge(cum_ready, 1)
            act.activation(e_b, cum, ACT.Exp).then_inc(e_ready, 1)
            act.wait_ge(d1_ready, 1)
            act.activation(e_q, lam, ACT.Exp).then_inc(e_ready, 1)
            act.activation(e_k, lam, ACT.Exp, scale=-1.0).then_inc(e_ready, 1)
            act.wait_ge(v_ready, 1)
            act.wait_ge(d3_ready, 1)
            act.activation(e_end, lam, ACT.Exp).then_inc(e_ready, 1)
            copy_groups(5, 7)
            act.wait_ge(z_copied, 7 * G)
            act.activation(acc[:, 0:G, :], z[:, Z_G1:Z_G1 + G, :], ACT.Sigmoid).then_inc(sig_ready, 1)
            act.activation(z[:, Z_G2:Z_G2 + G, :], z[:, Z_G2:Z_G2 + G, :], ACT.Sigmoid).then_inc(sig_ready, 1)

            def head_rinv(h):
                act.wait_ge(oss_ready, h + 1)
                if h:
                    act.wait_ge(orinv_ready, h)
                lk.add(act.activation(lnbuf[:], ps[:, 2 + h % 2, 0:T], ACT.Ln, bias=eps[:, 0:1], scale=1.0 / P))
                lk.wait()
                act.activation(aT[:, h, :], lnbuf[:], ACT.Exp, scale=-0.5).then_inc(orinv_ready, 1)

            for h in range(HEADS):
                act.wait_ge(o_done, h + 1)
                act.copy(o_raw[:, h, :], ps[:, h % 2, 0:T]).then_inc(o_copied, 1)
                act.activation(aT[:, h, :], ps[:, h % 2, 0:T], ACT.Square).then_inc(osq_ready, 1)
                if h >= 2:
                    head_rinv(h - 2)
            for h in range(HEADS - 2, HEADS):
                head_rinv(h)

            act.wait_ge(h_ready, KD)
            inv_rms(1, hT[:], tok[:, :, :].rearrange("p t d -> p (t d)")[:, 0:KD * T].rearrange("p (c t) -> p c t", t=T))
            act.wait_ge(ss_ready, 2)
            for t, (t0, n) in enumerate(tiles):
                act.wait_ge(xn_done, t + 1)
                act.copy(tok[0:n, t, :], ps[0:n, 2 * t:2 * t + 2, :].rearrange("p b n -> p (b n)")).then_inc(xn_copied, 1)
            act.wait_ge(pk_ready, 1)
            act.activation(pk[:], pk[:], ACT.Exp).then_inc(pk_exp, 1)

            act.wait_ge(gateT_done, 1)
            act.copy(gateT[:], ps[0:E, 6, 0:T]).then_inc(gateT_copied, 1)
            for c in range(KD):
                act.wait_ge(bd_done, c + 1)
                act.copy(acc[:, c, :], ps[:, c % 2, 0:T]).then_inc(acc_ready, 1)

            def expert(n, e, j):
                act.wait_ge(xs_done, n + 1)
                act.copy(xrow, ps[:, 2, :]).then_inc(xs_copied, 1)
                act.wait_ge(xsT_done, n + 1)
                act.copy(xsel, ps[:, 3, :]).then_inc(xsel_copied, 1)
                act.wait_ge(gate_ready, n + 1)
                act.activation(sbuf, gbuf, ACT.Sigmoid, scale=SWIGLU_ALPHA).then_inc(sigm_ready, 1)
                act.wait_ge(hT_done, n + 1)
                act.copy(hidT, ps[:, 4, :]).then_inc(hT_copied, 1)
                act.wait_ge(st_done, n + 1)
                act.copy(selT[:], ps[:, 4, 0:T]).then_inc(st_copied, 1)
                act.wait_ge(u_used, n * UNITS + UNITS)
                act.copy(yrow, ps[:, 5, :]).then_inc(yr_copied, 1)

            act.wait_ge(st_copied, 1)
            act.wait_ge(yr_copied, 1)
            with act.Fori(0, E) as e:
                expert(e, e, 0)
            overflow_blocks(act, expert)

            act.wait_ge(h_ready, KD + 1)
            inv_rms(2, hT[:], acc[:])
            for c in range(KD):
                act.wait_ge(pg_done, c + 1)
                act.activation(acc[:, c, :], ps[:, c % 4, 0:T], ACT.Sigmoid).then_inc(pg_sig, 1)
            act.wait_ge(h_ready, KD + 2)
            inv_rms(3, hT[:], acc[:])
            for t, (t0, n) in enumerate(tiles):
                act.wait_ge(out_done, t + 1)
                act.copy(tok[0:n, t, :], ps[0:n, 2 * t:2 * t + 2, :].rearrange("p b n -> p (b n)")).then_inc(out_copied, 1)

        @block.tensor
        def _(pe):
            def mm(o, lhsT, rhs, start, stop):
                return pe.matmul(o, lhsT, rhs, start=start, stop=stop, skip_group_check=True)

            pe.wait_ge(consts_ready, 2)
            pe.wait_ge(x_loaded, 32)
            for c in range(KD):
                for t, (t0, n) in enumerate(tiles):
                    ins = pe.transpose(ps[:, c, t0:t0 + n], tok[0:n, t, c * P:(c + 1) * P], ident[0:n, 0:n])
                ins.then_inc(xT_done, 1)
            pe.wait_ge(vec_loaded, 16 * 8)
            pe.wait_ge(xT_copied_a, 1)
            pe.transpose(ps[:, 0, 0:NV], vec_rows[:], ident[0:NV, 0:NV]).then_inc(vec_done, 1)

            def sums(k, sqbuf):
                pe.wait_ge(sq_ready, k + 1)
                for c in range(KD):
                    ins = mm(ps[:, 7, 0:T], ones[:], sqbuf[:, c, :], c == 0, c == KD - 1)
                ins.then_inc(ss_ready, 1)

            sums(0, acc)
            pe.wait_ge(r1w_loaded, 32)
            pe.wait_ge(norm_ready, KD)
            pe.wait_ge(rinv_ready, 1)
            for c in range(KD):
                ins = mm(ps[0:RANK, 7, 0:T], r1w[:, c, :], aT[:, c, :], c == 0, c == KD - 1)
            ins.then_inc(r1_done, 1)
            pe.wait_ge(r1_copied, 1)
            pe.wait_ge(xT_copied_v, KD // 2)
            for u in range(PAIRS):
                ins = mm(ps[:, 5 + u, 0:T], gk2[:, u * P:(u + 1) * P], r1T[:], True, True)
            ins.then_inc(gs_done, 1)
            pe.wait_ge(vec_copied, 1)
            def project(g, first=False):
                for j in range(G):
                    pe.wait_ge(w_loaded[j], 16 * (g + 1))
                    if not first:
                        pe.wait_ge(z_copied, g * G + (j + 1 - G))
                    for c in range(KD):
                        ins = mm(ps[:, j, 0:T], wst[:, j, c, :], aT[:, c, :], c == 0, c == KD - 1)
                    ins.then_inc(z_done, 1)

            project(0, first=True)
            with pe.Fori(1, NG) as g:
                project(g)
            pe.wait_ge(small_loaded, 16 * 2)
            pe.wait_ge(ple_loaded, 16 * 3)
            pe.wait_ge(gs_bias, 1)
            for c in range(PLE // P):
                for t, (t0, n) in enumerate(tiles):
                    ins = pe.transpose(ps[:, 6 + c, t0:t0 + n], p_tok[0:n, t, c * P:(c + 1) * P], ident[0:n, 0:n])
            ins.then_inc(pT_done, 1)
            pe.wait_ge(v_ready, 1)
            pe.wait_ge(z_copied, NZ)
            pe.wait_ge(pT_copied, 1)
            for t, (t0, n) in enumerate(tiles):
                for c in range(HEADS):
                    ins = pe.transpose(ps[0:n, 2 * t + c // 4, (c % 4) * P:(c % 4 + 1) * P], z[:, Z_V + c, t0:t0 + n], ident[:])
                ins.then_inc(vt_done, 1)
            pe.wait_ge(qk_ready, 1)
            for t, (t0, n) in enumerate(tiles):
                pe.wait_ge(v_copied, t + 1)
                for u in range(KU):
                    ins = pe.transpose(ps[0:n, 2 * t + u // 4, (u % 4) * P:(u % 4 + 1) * P], e_end[:, u, t0:t0 + n], ident[:])
                ins.then_inc(ke_done, 1)
            pe.wait_ge(ke_copied, 1)
            for h in range(HEADS):
                b = h % 4
                if h >= 4:
                    pe.wait_ge(att_masked, h - 3)
                u = h // 2 if h < GH else h - GH + PAIRS
                q = qr_pad[:, u, h % 2, :] if h < GH else e_q[:, u, :]
                for t, (t0, n) in enumerate(tiles):
                    ins = mm(ps[0:n, b, t0:t0 + n], e_k[:, u, t0:t0 + n], q[:, t0:t0 + n], True, True)
                ins.then_inc(att_done, 1)
            k = 0
            for u in range(KU):
                heads = 2 if u < PAIRS else 1
                v0 = 2 * u * P if u < PAIRS else (GH + u - PAIRS) * P
                for n0 in range(0, NCH, 2):
                    if k >= 4:
                        pe.wait_ge(s_copied_u, k - 3)
                    for n in (n0, n0 + 1):
                        ins = mm(ps[:, 4 + k % 4, (n - n0) * 2 * P:(n - n0) * 2 * P + heads * P],
                                 kend_tok[:, n // 2, n % 2, u * P:(u + 1) * P], tok[:, n // 2, v0:v0 + heads * P], True, True)
                    ins.then_inc(u_done, 1)
                    k += 1
            def head_sums(h):
                pe.wait_ge(osq_ready, h + 1)
                if h >= 2:
                    pe.wait_ge(orinv_ready, h - 1)
                mm(ps[:, 2 + h % 2, 0:T], ones[:], aT[:, h, :], True, True).then_inc(oss_ready, 1)

            pe.wait_ge(s_ready, 1)
            for h in range(HEADS):
                b = h % 2
                pe.wait_ge(att_masked, HEADS)
                if h >= 2:
                    pe.wait_ge(osq_ready, h - 1)
                    pe.wait_ge(o_copied, h - 1)
                u = h // 2 if h < GH else h - GH + PAIRS
                qb = qb_pad[:, u, h % 2, :] if h < GH else e_b[:, u, :]
                if h < GH and h % 2 == 0 or h >= GH:
                    pe.wait_ge(s0_loaded[u % 2], 16 * (u // 2 + 1))
                for t, (t0, n) in enumerate(tiles):
                    mm(ps[:, b, t0:t0 + n], tok[0:n, t, h * P:(h + 1) * P], att[0:n, h, t0:t0 + n], t == 0, False)
                for n in range(1, NCH):
                    mm(ps[:, b, n * CHUNK:(n + 1) * CHUNK], s_hist[:, u, n - 1, :], qb[:, n * CHUNK:(n + 1) * CHUNK], False, False)
                for s in range(SB):
                    c0 = L + s * SL
                    ins = mm(ps[:, b, c0:c0 + SL], s0[:, u % 2, s, :], qb[:, c0:c0 + SL], False, s == SB - 1)
                ins.then_inc(o_done, 1)
                pe.wait_ge(vm_ready, h + 1)
                if h >= 2:
                    pe.wait_ge(su_used, h - 1)
                for half in range(2):
                    ins = mm(ps[:, 4 + 2 * (h % 2) + half, :], kend_smp[0:S, u * P:(u + 1) * P],
                             vmask[0:S, h % 2, half * 4:half * 4 + 4, :].rearrange("p b v -> p (b v)"), True, True)
                ins.then_inc(su_done, 1)
                if h >= 1:
                    head_sums(h - 1)
            head_sums(HEADS - 1)
            for c in range(KD):
                i = NZ + c
                pe.wait_ge(w_loaded[i % WSLOTS], 16 * (i // WSLOTS + 1))
                if c == 0:
                    pe.wait_ge(o_ready, HEADS)
                    pe.wait_ge(su_used, HEADS)
                if c >= 4:
                    pe.wait_ge(h_ready, c - 3)
                for h in range(HEADS):
                    ins = mm(ps[:, 4 + c % 4, 0:T], wst[:, i % WSLOTS, h, :], acc[:, h, :], h == 0, h == HEADS - 1)
                ins.then_inc(h_done, 1)
            pe.wait_ge(h_ready, KD)
            sums(1, tok[:, :, :].rearrange("p t d -> p (t d)")[:, 0:KD * T].rearrange("p (c t) -> p c t", t=T))
            pe.wait_ge(norm_ready, 2 * KD)
            for t, (t0, n) in enumerate(tiles):
                for c in range(KD):
                    ins = mm(ps[0:n, 6, t * E:(t + 1) * E], aT[:, c, t0:t0 + n], w_rt[:, c, :], c == 0, c == KD - 1)
            ins.then_inc(lg_done, 1)
            for t, (t0, n) in enumerate(tiles):
                for c in range(KD):
                    ins = pe.transpose(ps[0:n, 2 * t + c // 4, (c % 4) * P:(c % 4 + 1) * P], aT[:, c, t0:t0 + n], ident[:])
                ins.then_inc(xn_done, 1)
            pe.wait_ge(memb_ready, 1)
            for t, (t0, n) in enumerate(tiles):
                for s in range(t + 1):
                    m = tiles[s][1]
                    lhs = upper[0:m, 0:n] if s == t else ones[0:m, 0:n]
                    mm(ps[0:n, 7, t * E:(t + 1) * E], lhs, memb[0:m, s, :], s == 0, s == t)
            for s, (_, m) in enumerate(tiles):
                ins = mm(ps[0:1, 7, NT * E:(NT + 1) * E], ones[0:m, 0:1], memb[0:m, s, :], s == 0, s == NT - 1)
            ins.then_inc(rank_done, 1)
            pe.wait_ge(xn_copied, NT)
            pe.wait_ge(cnt_ready, 1)

            pe.wait_ge(gate_done, 1)
            for t, (t0, n) in enumerate(tiles):
                ins = pe.transpose(ps[0:E, 6, t0:t0 + n], gate_e[0:n, t, :], ident[0:n, 0:n])
            ins.then_inc(gateT_done, 1)
            pe.wait_ge(gateT_copied, 1)
            pe.wait_ge(bdn_loaded, 16)
            for c in range(KD):
                if c >= 2:
                    pe.wait_ge(acc_ready, c - 1)
                mm(ps[:, c % 2, 0:T], b_dn[:, c * P:(c + 1) * P], gateT[:], True, True).then_inc(bd_done, 1)
            pe.wait_ge(acc_ready, KD)
            pe.wait_ge(bgu_loaded, 16)

            def combine(n, c):
                if c == 0:
                    pe.wait_ge(st_copied, n + 1)
                    pe.wait_ge(yr_copied, n + 1)
                elif c != 2:
                    pe.wait_ge(acc_added, n * (KD // 2) + (c + 1) // 2)
                for half in range(2):
                    r = slice(half * SLOTS, (half + 1) * SLOTS)
                    ins = mm(ps[:, CB_BANKS[c] + half, 0:T], yrow[r, c * P:(c + 1) * P], selT[r, :], True, True)
                ins.then_inc(cb_done, 1)

            def halves(bank, lhsT, rhs0, rhs1, start, stop):
                mm(ps[0:SLOTS, bank, :], lhsT, rhs0, start, stop)
                return mm(ps[SLOTS:P, bank, :], lhsT, rhs1, start, stop)

            def expert(n, e, j):
                pe.wait_ge(sel_ready, n + 1)
                for t, (t0, m) in enumerate(tiles):
                    ins = halves(2, sel[0:m, t, :], tok[0:m, t, 0:D // 2], tok[0:m, t, D // 2:D], t == 0, t == NT - 1)
                ins.then_inc(xs_done, 1)
                for b in range(2):
                    halves(b, ehot[:], bgu[:, b * FF:b * FF + BANK], bgu[:, b * FF + BANK:(b + 1) * FF], True, False)
                pe.wait_ge(xs_copied, n + 1)
                for c in range(KD // 2):
                    ins = pe.transpose(ps[:, 3, c * P:(c + 1) * P], xrow[:, c * P:(c + 1) * P], ident[:])
                ins.then_inc(xsT_done, 1)
                combine(n, 0)
                pe.wait_ge(xsel_copied, n + 1)
                for c in range(KD):
                    x0 = (c % (KD // 2)) * P + (c // (KD // 2)) * SLOTS
                    pe.wait_ge(u_loaded[c], n * 16 + 16)
                    for b in range(2):
                        w0 = c * UCOLS + b * FF
                        ins = halves(b, xsel[:, x0:x0 + SLOTS], ring[:, w0:w0 + BANK], ring[:, w0 + BANK:w0 + FF],
                                     False, c == KD - 1)
                    ins.then_inc(u_used, 1)
                combine(n, 1)
                combine(n, 2)
                pe.wait_ge(hid_ready, n + 1)
                for c in range(KF // 2):
                    ins = pe.transpose(ps[:, 4, c * P:(c + 1) * P], hid[:, c * P:(c + 1) * P], ident[:])
                ins.then_inc(hT_done, 1)
                pe.wait_ge(hT_copied, n + 1)
                for c in range(KF // 2):
                    pe.wait_ge(u_loaded[KD + c], n * 16 + 16)
                    for k in range(2):
                        kc = 2 * c + k
                        x0 = (kc % (KF // 2)) * P + (kc // (KF // 2)) * SLOTS
                        w0 = (KD + c) * UCOLS + k * D
                        ins = halves(5, hidT[:, x0:x0 + SLOTS], ring[:, w0:w0 + BANK], ring[:, w0 + BANK:w0 + D],
                                     kc == 0, kc == KF - 1)
                    ins.then_inc(u_used, 1)
                    if c == 0:
                        combine(n, 3)
                    if c == 1:
                        pe.wait_ge(selg_ready, n + 1)
                        for t, (t0, m) in enumerate(tiles):
                            ins = pe.transpose(ps[:, 4, t0:t0 + m], selg[0:m, t, :, :].rearrange("p a s -> p (a s)"),
                                               ident[0:m, 0:m])
                        ins.then_inc(st_done, 1)

            with pe.Fori(0, E) as e:
                expert(e, e, 0)
            n = overflow_blocks(pe, expert)
            pe.wait_ge(acc_added, n * (KD // 2))
            for c in range(KD // 2):
                combine(n, c)

            pe.wait_ge(h_ready, KD + 1)
            sums(2, acc)
            pe.wait_ge(norm_ready, 3 * KD)
            pe.wait_ge(pg_loaded, 16 * (KD // 2))
            for c in range(KD):
                b = c % 4
                if c >= 4:
                    pe.wait_ge(pg_used, c - 3)
                    pe.wait_ge(pg_sig, c - 3)
                for k in range(PLE // P):
                    mm(ps[:, 4 + b, 0:T], w_pp[:, k, c * P:(c + 1) * P], pT[:, k, :], k == 0,
                       k == PLE // P - 1)
                for k in range(KD):
                    ins = mm(ps[:, b, 0:T], ring[:, k * D + c * P:k * D + (c + 1) * P], aT[:, k, :], k == 0, k == KD - 1)
                ins.then_inc(pg_done, 1)
            pe.wait_ge(h_ready, KD + 2)
            sums(3, acc)
            pe.wait_ge(norm_ready, 4 * KD)
            for t, (t0, n) in enumerate(tiles):
                for c in range(KD):
                    ins = pe.transpose(ps[0:n, 2 * t + c // 4, (c % 4) * P:(c % 4 + 1) * P], aT[:, c, t0:t0 + n], ident[:])
                ins.then_inc(out_done, 1)

        @block.vector
        def _(dve):
            lk = Links(dve, chain)
            for c in range(1, KD, 2):
                dve.wait_ge(xT_done, c + 1)
                dve.tensor_copy(hT[:, c, :], ps[:, c, 0:T]).then_inc(xT_copied_v, 1)
            dve.wait_ge(vec_done, 1)
            dve.tensor_copy(vecT[:], ps[:, 0, 0:NV]).then_inc(vec_copied, 1)
            dve.wait_ge(vec_copied, 1)

            def apply_norm(k, g0):
                dve.wait_ge(rinv_ready, k + 1)
                for c in range(KD):
                    dve.scalar_tensor_tensor(aT[:, c, :], hT[:, c, :], vecT[:, g0 + c:g0 + c + 1], rinv[:],
                                             ALU.mult, ALU.mult).then_inc(norm_ready, 1)

            l0, l1 = vecT[:, V_LB:V_LB + HH], vecT[:, V_LB + HH:V_LB + 2 * HH]
            lk.add(dve.tensor_tensor(lbt[:, 0], l0, l1, ALU.max))
            lk.wait()
            lk.add(dve.tensor_tensor(lbt[:, 1], l0, lbt[:, 0], ALU.subtract))
            dve.tensor_tensor(lbt[:, 2], l1, lbt[:, 0], ALU.subtract).then_inc(lb_ready, 1)
            apply_norm(0, V_MIX)
            dve.wait_ge(gs_done, 1)
            for u in range(PAIRS):
                lk.add(dve.tensor_scalar(gs[:, 0, u, :], ps[:, 5 + u, 0:T], vecT[:, V_BGK + u:V_BGK + u + 1], None, ALU.add))
            lk.wait()
            dve.scalar_tensor_tensor(gs[:, 1], gs[:, 0], -1.0, gs[:, 0], ALU.mult, ALU.max).then_inc(gs_bias, 1)
            dve.wait_ge(gs_exp, 1)
            lk.add(dve.scalar_tensor_tensor(gs[:, 0], gs[:, 0], 0.0, gs[:, 2], ALU.min, ALU.subtract))
            lk.wait()
            lk.add(dve.tensor_scalar(lam[:, 0:PAIRS, :], gs[:, 0], 1.0 / GLA_NORMALIZER, None, ALU.mult))
            dve.wait_ge(lb_exp, 1)
            lk.add(dve.tensor_tensor(lbt[:, 3], lbt[:, 1], lbt[:, 2], ALU.add))
            lk.wait()
            lk.add(dve.reciprocal(lbt[:, 3], lbt[:, 3]))
            lk.wait()
            lk.add(dve.tensor_tensor(lbt[:, 4], lbt[:, 1], lbt[:, 3], ALU.mult))
            lk.wait()
            lk.add(dve.tensor_scalar(lbt[:, 5], lbt[:, 4], -1.0, 1.0, ALU.mult, ALU.add))
            lk.wait()
            dve.wait_ge(sig_ready, 2)
            dve.wait_ge(z_copied, 3 * G)
            q2, f2 = z[:, Z_Q2:Z_Q2 + HH, :], z[:, Z_F2:Z_F2 + HH, :]
            lk.add(dve.tensor_tensor(q2, q2, e_q[:, PAIRS:KU, :], ALU.mult))
            for h in range(HH):
                lk.add(dve.tensor_scalar(lam[:, PAIRS + h, :], e_k[:, PAIRS + h, :], lbt[:, 5, h:h + 1], lbt[:, 4, h:h + 1],
                                         ALU.mult, ALU.add))
            lk.wait()
            dve.tensor_scalar(f2, lam[:, PAIRS:KU, :], -1.0, 1.0, ALU.mult, ALU.add).then_inc(forget_ready, 1)
            dve.wait_ge(sig_ready, 3)
            i2 = z[:, Z_I2:Z_I2 + HH, :]
            dve.tensor_tensor(i2, i2, e_end[:, PAIRS:KU, :], ALU.mult).then_inc(v_ready, 1)
            dve.wait_ge(lnf_ready, 1)
            for u in range(KU):
                ins = dve.tensor_tensor_scan(cum[:, u, :], reset[:], lam[:, u, :], 0.0, ALU.mult, ALU.add)
            ins.then_inc(cum_ready, 1)
            dve.wait_ge(cum_ready, 1)

            def by_chunk(a):
                return ((a[:, :, 0:L].rearrange("p u (n c) -> p u n c", c=CHUNK), NCH, CHUNK),
                        (a[:, :, L:T].rearrange("p u (n c) -> p u n c", c=SL), SB, SL))

            for (o, n, c), (i, _, _) in zip(by_chunk(lam), by_chunk(cum)):
                ref = i[:, :, :, c // 2:c // 2 + 1].to_broadcast([P, KU, n, c])
                ins = dve.tensor_tensor(o, i, ref, ALU.subtract)
            ins.then_inc(d1_ready, 1)
            dve.wait_ge(e_ready, 1)
            lk.add(dve.tensor_copy(dec[:, :, 0:NCH], e_b[:, :, CHUNK - 1:L:CHUNK]))
            lk.add(dve.tensor_copy(dec[:, :, NCH:NCH + SB], e_b[:, :, L + SL - 1:T:SL]))
            dve.wait_ge(e_ready, 3)
            for (o, n, c), (i, _, _) in zip(by_chunk(lam), by_chunk(cum)):
                last = i[:, :, :, c - 1:c].to_broadcast([P, KU, n, c])
                ins = dve.tensor_tensor(o, last, i, ALU.subtract)
            ins.then_inc(d3_ready, 1)
            for half in range(2):
                r = slice(half * GK, (half + 1) * GK)
                for pad, ex in ((qr_pad, e_q), (qb_pad, e_b)):
                    lk.add(dve.scalar_tensor_tensor(pad[r, :, half, :], z[r, Z_Q1:Z_Q1 + PAIRS, :], float(GK) ** -0.5,
                                                    ex[r, 0:PAIRS, :], ALU.mult, ALU.mult))
            lk.wait()
            for ex in (e_q, e_b):
                lk.add(dve.tensor_tensor(ex[:, PAIRS:KU, :], q2, ex[:, PAIRS:KU, :], ALU.mult))
            dve.wait_ge(e_ready, 4)
            for ex in (e_k, e_end):
                lk.add(dve.tensor_tensor(ex[:, 0:PAIRS, :], z[:, Z_K1:Z_K1 + PAIRS, :], ex[:, 0:PAIRS, :], ALU.mult))
                ins = dve.tensor_tensor(ex[:, PAIRS:KU, :], f2, ex[:, PAIRS:KU, :], ALU.mult)
            ins.then_inc(qk_ready, 1)
            dve.wait_ge(pT_done, 1)
            dve.tensor_copy(pT[:], ps[:, 6:8, 0:T]).then_inc(pT_copied, 1)
            for t, (t0, n) in enumerate(tiles):
                dve.wait_ge(vt_done, t + 1)
                dve.tensor_copy(tok[0:n, t, :], ps[0:n, 2 * t:2 * t + 2, :].rearrange("p b n -> p (b n)")).then_inc(v_copied, 1)
            dve.wait_ge(att_zeroed, 2)
            for t, (t0, n) in enumerate(tiles):
                dve.wait_ge(ke_done, t + 1)
                src = ps[:, 2 * t:2 * t + 2, :].rearrange("p b n -> p (b n)")[:, 0:KU * P]
                if t < TT:
                    for half in range(2):
                        r = slice(half * CHUNK, (half + 1) * CHUNK)
                        dve.tensor_copy(kend_tok[r, t, half, :], src[r])
                else:
                    dve.tensor_copy(kend_smp[0:S, :], src[0:S]).then_inc(ke_copied, 1)
            dve.wait_ge(consts_ready, 11)
            for h in range(HEADS):
                dve.wait_ge(att_done, h + 1)
                for t in range(TT):
                    dve.copy_predicated(att[:, h, t * P:(t + 1) * P], maski[:, 0:P], ps[:, h % 4, t * P:(t + 1) * P])
                dve.copy_predicated(att[0:S, h, L:T], maski[0:S, P:P + S], ps[0:S, h % 4, L:T]).then_inc(att_masked, 1)
            k = 0
            for u in range(KU):
                parts = [(slice(0, GK), 0), (slice(GK, P), P)] if u < PAIRS else [(slice(0, P), 0)]
                for n0 in range(0, NCH, 2):
                    dve.wait_ge(u_done, k + 1)
                    for n in (n0, n0 + 1):
                        if n:
                            lk.wait()
                        for r, v0 in parts:
                            src = ps[r, 4 + k % 4, (n - n0) * 2 * P + v0:(n - n0) * 2 * P + v0 + P]
                            if n == 0:
                                lk.add(dve.tensor_copy(s_hist[r, u, 0, :], src))
                            else:
                                lk.add(dve.scalar_tensor_tensor(s_hist[r, u, n, :], s_hist[r, u, n - 1, :], dec[r, u, n:n + 1],
                                                                src, ALU.mult, ALU.add))
                    lk.wait()
                    dve.nop().then_inc(s_copied_u, 1)
                    k += 1
            dve.nop().then_inc(s_ready, 1)
            dve.wait_ge(sig_ready, 5)
            g1 = z[:, Z_G1:Z_G1 + GH, :]
            lk.add(dve.tensor_tensor(g1, g1, acc[:, 0:GH, :], ALU.mult))
            def sample_state(h):
                u = h // 2 if h < GH else h - GH + PAIRS
                st = s0[:, u % 2]
                dve.wait_ge(o_done, 2 * u + 2 if h < GH else h + 1)
                if h >= GH or h % 2 == 0:
                    lk.add(dve.tensor_tensor(st, st, dec[:, u, NCH:NCH + SB].unsqueeze(2).to_broadcast([P, SB, P]), ALU.mult))
                    lk.wait()
                r = slice((h % 2) * GK, (h % 2 + 1) * GK) if h < GH else slice(0, P)
                dve.wait_ge(su_done, h + 1)
                b = 4 + 2 * (h % 2)
                src = ps[r, b:b + 2, :].rearrange("p b (s v) -> p (b s) v", v=P)
                dve.tensor_tensor(st[r], st[r], src, ALU.add).then_inc(su_used, 1)

            def head_norm(h):
                dve.wait_ge(orinv_ready, h + 1)
                dve.wait_ge(o_copied, h + 1)
                gn = vecT[:, V_GN + (h >= GH):V_GN + (h >= GH) + 1]
                lk.add(dve.scalar_tensor_tensor(o_raw[:, h, :], o_raw[:, h, :], gn, aT[:, h, :], ALU.mult, ALU.mult))
                lk.wait()
                dve.tensor_tensor(acc[:, h, :], o_raw[:, h, :], z[:, Z_G1 + h, :], ALU.mult).then_inc(o_ready, 1)

            for h in range(HEADS):
                if h % 2 == 1 or h >= GH:
                    if h < GH:
                        sample_state(h - 1)
                    sample_state(h)
            for h in range(HEADS):
                head_norm(h)
            for c in range(KD):
                dve.wait_ge(h_done, c + 1)
                dve.tensor_tensor(hT[:, c, :], hT[:, c, :], ps[:, 4 + c % 4, 0:T], ALU.add).then_inc(h_ready, 1)
            dve.wait_ge(h_ready, KD)
            apply_norm(1, V_FFN)
            dve.wait_ge(small_loaded, 16 * 2)
            dve.wait_ge(lg_done, 1)
            for t, (t0, n) in enumerate(tiles):
                lk.add(dve.tensor_tensor(logit[0:n, t, :], ps[0:n, 6, t * E:(t + 1) * E], b_rt[0:n, :], ALU.add))
            lk.wait()
            for t, (t0, n) in enumerate(tiles):
                lk.add(dve.max(top8[0:n, t, :], logit[0:n, t, :]))
            lk.wait()
            for t, (t0, n) in enumerate(tiles):
                lk.add(dve.max_index(idx8[0:n, t, :], top8[0:n, t, :], logit[0:n, t, :]))
            dve.tensor_tensor(pk[:], top8[:, :, 0:TOPK], top8[:, :, 0:1].to_broadcast([P, NT, TOPK]), ALU.subtract) \
                .then_inc(pk_ready, 1)
            lk.wait()
            lk.add(dve.tensor_scalar(idxf[:], idx8[:, :, 0:TOPK], 1.0, None, ALU.add))
            lk.wait()
            lk.add(dve.tensor_tensor(onehot[:].rearrange("p t k e -> p (t k) e"),
                                     iota1[:, 0:E].unsqueeze(1).to_broadcast([P, NT * TOPK, E]),
                                     idxf[:].rearrange("p t k -> p (t k)").unsqueeze(2).to_broadcast([P, NT * TOPK, E]), ALU.is_equal))
            lk.wait()
            dve.tensor_reduce(memb[:], onehot[:].rearrange("p t k e -> p t e k"), AX_X, ALU.add).then_inc(memb_ready, 1)
            dve.wait_ge(pk_exp, 1)
            lk.add(dve.tensor_reduce(psum_k[:, :, 0:1], pk[:], AX_X, ALU.add))
            lk.wait()
            lk.add(dve.reciprocal(psum_k[:, :, 1:2], psum_k[:, :, 0:1]))
            lk.wait()
            lk.add(dve.tensor_tensor(pk[:], pk[:], psum_k[:, :, 1:2].to_broadcast([P, NT, TOPK]), ALU.mult))
            lk.wait()
            lk.add(dve.tensor_tensor(gated[:].rearrange("p t k e -> p (t k) e"), onehot[:].rearrange("p t k e -> p (t k) e"),
                                     pk[:].rearrange("p t k -> p (t k)").unsqueeze(2).to_broadcast([P, NT * TOPK, E]), ALU.mult))
            lk.wait()
            dve.tensor_reduce(gate_e[:], gated[:].rearrange("p t k e -> p t e k"), AX_X, ALU.add).then_inc(gate_done, 1)
            dve.wait_ge(rank_done, 1)
            for t, (t0, n) in enumerate(tiles):
                lk.add(dve.scalar_tensor_tensor(rankp[0:n, t, :], ps[0:n, 7, t * E:(t + 1) * E], 1.0, memb[0:n, t, :],
                                                ALU.add, ALU.mult))
            lk.add(dve.tensor_copy(cnt_f[:, 0:E], ps[0:1, 7, NT * E:(NT + 1) * E]))
            lk.wait()
            lk.add(dve.tensor_reduce(cnt_f[:, E:E + 1], cnt_f[:, 0:E], AX_X, ALU.max))
            lk.wait()
            dve.tensor_copy(cnt_i[:], cnt_f[:]).then_inc(cnt_ready, 1)

            def add_combined(n, c):
                b = CB_BANKS[c]
                dve.wait_ge(cb_done, n * (KD // 2) + (c + 1))
                a = acc[:, c:KD:KD // 2, :]
                dve.tensor_tensor(a, a, ps[:, b:b + 2, 0:T], ALU.add).then_inc(acc_added, 1)

            LINKS = 4

            def expert(n, e, j):
                bk = Links(dve, moe_chain, n * LINKS)
                slot = iota1[:, 0:SLOTS] if isinstance(j, int) else iota1[:, bass.ds(j * SLOTS, SLOTS)]
                parts = ((0, TT, P), (TT, NT, S))
                for a, b, m in parts:
                    bk.add(dve.tensor_tensor(sel[0:m, a:b, :], slot[0:m].unsqueeze(1).to_broadcast([m, b - a, SLOTS]),
                                             rankp[0:m, a:b, bass.ds(e, 1)].to_broadcast([m, b - a, SLOTS]), ALU.is_equal))
                bk.wait()
                dve.tensor_copy(ehot[:], ident[:, bass.ds(e, 1)].to_broadcast([P, SLOTS])).then_inc(sel_ready, 1)
                add_combined(n, 0)
                for a, b, m in parts:
                    ins = dve.tensor_tensor(selg[0:m, a:b], sel[0:m, a:b, :].unsqueeze(2).to_broadcast([m, b - a, 2, SLOTS]),
                                            gate_e[0:m, a:b, bass.ds(e, 1)].unsqueeze(2).to_broadcast([m, b - a, 2, SLOTS]),
                                            ALU.mult)
                ins.then_inc(selg_ready, 1)
                dve.wait_ge(u_used, n * UNITS + KD)
                dve.tensor_scalar(gbuf, ps[:, 0, :], SWIGLU_LIMIT, None, ALU.min).then_inc(gate_ready, 1)
                bk.add(dve.tensor_scalar(ubuf, ps[:, 1, :], -SWIGLU_LIMIT, SWIGLU_LIMIT, ALU.max, ALU.min))
                bk.wait()
                bk.add(dve.scalar_tensor_tensor(ubuf, ubuf, 1.0, gbuf, ALU.add, ALU.mult))
                bk.wait()
                dve.wait_ge(sigm_ready, n + 1)
                dve.tensor_tensor(hid, ubuf, sbuf, ALU.mult).then_inc(hid_ready, 1)
                for c in range(1, KD // 2):
                    add_combined(n, c)
                dve.wait_ge(selg_ready, n + 1)
                dve.wait_ge(acc_added, n * (KD // 2) + KD // 2)
                assert bk.n == LINKS

            dve.wait_ge(bgu_loaded, 16)
            dve.wait_ge(acc_ready, KD)
            with dve.Fori(0, E) as e:
                expert(e, e, 0)
            n = overflow_blocks(dve, expert)
            for c in range(KD // 2):
                add_combined(n, c)
            dve.wait_ge(acc_added, n * (KD // 2) + KD // 2)
            dve.tensor_tensor(hT[:], hT[:], acc[:], ALU.add).then_inc(h_ready, 1)
            dve.wait_ge(h_ready, KD + 1)
            apply_norm(2, V_PLE)
            for c in range(KD):
                dve.wait_ge(pg_sig, c + 1)
                b = c % 4
                dve.tensor_tensor(acc[:, c, :], acc[:, c, :], ps[:, 4 + b, 0:T], ALU.mult).then_inc(pg_used, 1)
            dve.wait_ge(pg_used, KD)
            dve.tensor_tensor(hT[:], hT[:], acc[:], ALU.add).then_inc(h_ready, 1)
            dve.wait_ge(h_ready, KD + 2)
            apply_norm(3, V_FIN)


_INS = ["x_prompt", "x_sample", "p_prompt", "p_sample", "state_gla", "state_hgrn", "g_mix", "w_in", "w_gk2", "b_gk2",
        "gn_gla", "lb_logits", "gn_hgrn", "w_out", "g_ffn", "w_router", "b_router", "w_gu", "b_gu", "w_dn", "b_dn",
        "g_ple", "w_ple_gate", "w_ple_proj", "g_final"]


def kernel(**inputs):
    import numpy as np
    import concourse.bacc as bacc
    from concourse.bass_utils import run_bass_kernel_spmd

    nc = bacc.Bacc("TRN2", target_bir_lowering=False, num_devices=1)
    arrays, io = {}, {}
    for name in _INS:
        a = np.ascontiguousarray(inputs[name])
        arrays[f"in_{name}"] = a
        io[name] = nc.dram_tensor(f"in_{name}", a.shape, mybir.dt.from_np(a.dtype), kind="ExternalInput").ap()
    sg, sh = inputs["state_gla"].shape, inputs["state_hgrn"].shape
    nb = inputs["x_prompt"].shape[0]
    shapes = [inputs["x_prompt"].shape, inputs["x_sample"].shape, (sg[0], nb) + tuple(sg[2:]), (sh[0], nb) + tuple(sh[2:]), sg, sh]
    out = [nc.dram_tensor(f"out_{i}", tuple(s), F32, kind="ExternalOutput").ap() for i, s in enumerate(shapes)]
    build(nc, io, out)
    r = run_bass_kernel_spmd(nc, [arrays], core_ids=[0])
    return tuple(r.results[0][f"out_{i}"] for i in range(len(shapes)))
```

```python
from contextlib import ExitStack

import concourse.bass as bass
from concourse import mybir

F32 = mybir.dt.float32
I32 = mybir.dt.int32
U32 = mybir.dt.uint32
ALU = mybir.AluOpType
ACT = mybir.ActivationFunctionType
AX_X = mybir.AxisListType.X

P = 128
BANK = 512
EPS = 1e-6
SLOTS = 64
SWIGLU_LIMIT = 7.0
SWIGLU_ALPHA = 1.702
GLA_NORMALIZER = 16.0
CHUNK = 64


class Links:

    def __init__(self, eng, sem, base=0):
        self.eng, self.sem, self.base, self.n = eng, sem, base, 0

    def add(self, ins):
        self.n += 1
        ins.then_inc(self.sem, 1)

    def wait(self):
        self.eng.wait_ge(self.sem, self.base + self.n)


def build(nc, io, out):
    D = io["x_prompt"].shape[2]
    L = io["x_prompt"].shape[1]
    SB, SL = io["x_sample"].shape[:2]
    S = SB * SL
    T = L + S
    E = io["w_router"].shape[2]
    FF = io["w_dn"].shape[2]
    PLE = io["w_ple_proj"].shape[1]
    GH, GK, GV = io["state_gla"].shape[2:]
    HH, HK, HV = io["state_hgrn"].shape[2:]
    RANK = io["w_gk2"].shape[1]
    KD = D // P
    KF = FF // P
    TT = L // P
    NT = TT + 1
    NCH = L // CHUNK
    PAIRS = GH * GK // P
    HEADS = GH + HH
    KU = PAIRS + HH
    TOPK = 4
    BLOCKS = -(-T // SLOTS)
    assert GV == HV == HK == P and GK * 2 == P and L == TT * P and S == 32 and BANK >= T
    assert TT == 2 and HEADS == KD == SB == 8

    tiles = [(t * P, P) for t in range(TT)] + [(L, S)]

    G = 4
    c_q1 = 0
    c_v1 = 2 * GH * GK
    c_g1 = c_v1 + GH * GV
    c_r1 = c_g1 + GH * GV
    c_q2 = c_r1 + RANK
    c_f2 = c_q2 + HH * HK
    c_i2 = c_f2 + HH * HK
    c_g2 = c_i2 + HH * HV
    group_cols = [c_q1, c_q2, c_f2, c_v1, c_i2, c_g1, c_g2]
    NG = len(group_cols)
    Z_Q1, Z_K1, Z_Q2, Z_F2, Z_V, Z_I2, Z_G1, Z_G2 = 0, 2, 4, 8, 12, 16, 20, 24
    NZ = NG * G
    WSLOTS = 4

    UNITS = KD + KF // 2
    UCOLS = 2 * FF
    assert 2 * FF == 2 * D

    with ExitStack() as ctx:
        def sb(name, shape, dt=F32):
            return ctx.enter_context(nc.sbuf_tensor(name, shape, dt))

        def sem(name):
            return ctx.enter_context(nc.semaphore(name))

        ring = sb("ring", [P, UNITS * UCOLS])
        at = [0]

        def carve(*dims):
            n = 1
            for d in dims:
                n *= d
            v = ring[:, at[0]:at[0] + n]
            at[0] += n
            if len(dims) == 1:
                return v
            names = "abcd"[:len(dims)]
            return v.rearrange("p (" + " ".join(names) + ") -> p " + " ".join(names),
                               **{k: d for k, d in zip(names, dims)})

        z = carve(NZ, T)
        decay_start = at[0]
        lam = carve(KU, T)
        cum = carve(KU, T)
        at[0] = decay_start
        kend_tok = carve(TT, 2, KU * P)
        kend_smp = carve(KU * P)
        e_start = at[0]
        e_q = carve(KU, T)
        e_k = carve(KU, T)
        e_end = carve(KU, T)
        e_b = carve(KU, T)
        qr_pad = carve(PAIRS, 2, T)
        qb_pad = carve(PAIRS, 2, T)
        hist_start = at[0]
        s_hist = carve(KU, NCH, P)
        assert at[0] <= UNITS * UCOLS
        at[0] = hist_start
        gs = carve(3, PAIRS, T)
        p_tok = carve(NT, PLE)
        assert at[0] <= hist_start + KU * NCH * P
        assert at[0] <= UNITS * UCOLS
        assert HEADS * T <= TT * 2 * KU * P
        osq = ring[:, decay_start:decay_start + HEADS * T].rearrange("p (h t) -> p h t", t=T)
        att = z[:, 0:HEADS, :]
        o_raw = z[:, Z_V:Z_V + HEADS, :]

        wst = sb("wst", [P, WSLOTS, KD, P])
        blk = wst[:].rearrange("p a b c -> p (a b c)")
        bc = KD * SLOTS
        xrow, xsel, gbuf, ubuf, sbuf, hid, hidT, yrow = (blk[:, i * bc:(i + 1) * bc] for i in range(8))
        assert 8 * bc <= WSLOTS * KD * P and KF == KD and bc == BANK == D // 2 == FF // 2
        tok = sb("tok", [P, NT, D])
        hT = sb("hT", [P, KD, T])
        aT = sb("aT", [P, KD, T])
        acc = sb("acc", [P, KD, T])
        s0 = sb("s0", [P, 2, SB, P])
        assert (KU - 2) * SB * P <= 3 * KU * T
        late = ring[:, e_start:e_start + (KU - 2) * SB * P].rearrange("p (u b v) -> p u b v", u=KU - 2, b=SB)
        states = [s0[:, u] if u < 2 else late[:, u - 2] for u in range(KU)]
        smp_tmp = acc[:, GH:KD, :].rearrange("p c t -> p (c t)")[:, 0:SB * P].rearrange("p (b v) -> p b v", b=SB)
        smp = sb("smp", [P, 2, P])
        smask = sb("smask", [P, SB])
        squares = tok[:].rearrange("p t d -> p (t d)")[:, 0:KD * T].rearrange("p (c t) -> p c t", t=T)
        pgt = blk[:, 0:2 * T].rearrange("p (i t) -> p i t", t=T)
        fin = blk[:, 2 * T:(2 + KD) * T].rearrange("p (c t) -> p c t", t=T)
        vmask = sb("vmask", [32, 2, SB, P])
        after_v = vmask[0:E, 1].rearrange("e b v -> e (b v)")
        lgs = after_v[:, 0:T]
        gateT = after_v[:, T:2 * T]
        rcol = sb("rcol", [P, NT])
        rinv = sb("rinv", [P, T])
        lnbuf = sb("lnbuf", [P, T])
        w_pp_chunk = lnbuf[:, 0:PLE].rearrange("p (k n) -> p k n", k=PLE // P)
        b_dn_chunk = rinv[0:E, 0:P]
        ident = sb("ident", [P, P])
        ones = sb("ones", [P, P])
        upper = sb("upper", [P, P])
        reset = sb("reset", [P, T])
        maskf = sb("maskf", [P, P + 32])
        maski = sb("maski", [P, P + 32], I32)
        b_dn = vmask[0:E, 0].rearrange("e b v -> e (b v)")
        seqmask = sb("seqmask", [32, SB])
        iota_i = ring[:, 0:BLOCKS * SLOTS].bitcast(I32)
        iota1 = sb("iota1", [P, BLOCKS * SLOTS])
        eps = sb("eps", [P, 1])
        NV = 4 * KD + PAIRS + 2 * HH + 2
        vec_rows = sb("vec_rows", [NV, P])
        vecT = sb("vecT", [P, NV])
        V_MIX, V_FFN, V_PLE, V_FIN, V_BGK = 0, KD, 2 * KD, 3 * KD, 4 * KD
        V_LB = V_BGK + PAIRS
        V_GN = V_LB + 2 * HH
        lbt = sb("lbt", [P, 6, HH])
        r1w = sb("r1w", [P, KD, RANK])
        r1T = sb("r1T", [RANK, T])
        gk2 = sb("gk2", [RANK, GH * GK])
        dec = sb("dec", [P, KU, NCH + SB])
        w_rt = sb("w_rt", [P, KD, E])
        b_rt = sb("b_rt", [P, E])
        bgu = sb("bgu", [P, 2 * FF])
        ehot = sb("ehot", [P, SLOTS])
        pT = sb("pT", [P, PLE // P, T])
        w_pp = sb("w_pp", [P, PLE // P, D])
        logit = sb("logit", [P, NT, E])
        top8 = sb("top8", [P, NT, 8])
        idx8 = sb("idx8", [P, NT, 8], U32)
        idxf = sb("idxf", [P, NT, TOPK])
        pk = sb("pk", [P, NT, TOPK])
        psum_k = sb("psum_k", [P, NT, 2])
        onehot = sb("onehot", [P, NT, TOPK, E])
        gated = sb("gated", [P, NT, TOPK, E])
        gate_e = sb("gate_e", [P, NT, E])
        memb = sb("memb", [P, NT, E])
        rankp = sb("rankp", [P, NT, E])
        cnt_f = sb("cnt_f", [1, E + 1])
        cnt_i = sb("cnt_i", [1, E + 1], I32)
        sel = sb("sel", [P, NT, SLOTS])
        selg = sb("selg", [P, NT, 2, SLOTS])
        selT = sb("selT", [P, T])

        ps = ctx.enter_context(nc.psum_tensor("ps", [P, 8, BANK], F32))

        x_loaded = sem("x_loaded")
        vec_loaded = sem("vec_loaded")
        small_loaded = sem("small_loaded")
        r1w_loaded = sem("r1w_loaded")
        ple_loaded = sem("ple_loaded")
        pool_link = sem("pool_link")
        consts_ready = sem("consts_ready")
        xT_done = sem("xT_done")
        xT_copied_a = sem("xT_copied_a")
        xT_copied_v = sem("xT_copied_v")
        vec_done = sem("vec_done")
        vec_copied = sem("vec_copied")
        pT_done = sem("pT_done")
        pT_copied = sem("pT_copied")
        bgu_loaded = sem("bgu_loaded")
        bdn_loaded = sem("bdn_loaded")
        gateT_done = sem("gateT_done")
        gateT_copied = sem("gateT_copied")
        bd_done = sem("bd_done")
        sq_ready = sem("sq_ready")
        ss_ready = sem("ss_ready")
        act_link = sem("act_link")
        rinv_ready = sem("rinv_ready")
        norm_ready = sem("norm_ready")
        r1_done = sem("r1_done")
        r1_copied = sem("r1_copied")
        gs_done = sem("gs_done")
        gs_bias = sem("gs_bias")
        gs_exp = sem("gs_exp")
        w_loaded = [sem(f"w_loaded{i}") for i in range(WSLOTS)]
        z_done = sem("z_done")
        z_copied = sem("z_copied")
        sig_ready = sem("sig_ready")
        chain = sem("chain")
        forget_ready = sem("forget_ready")
        lnf_ready = sem("lnf_ready")
        d1_ready = sem("d1_ready")
        e_ready = sem("e_ready")
        d3_ready = sem("d3_ready")
        cum_ready = sem("cum_ready")
        qk_ready = sem("qk_ready")
        v_ready = sem("v_ready")
        vt_done = sem("vt_done")
        v_copied = sem("v_copied")
        ke_done = sem("ke_done")
        ke_copied = sem("ke_copied")
        att_zeroed = sem("att_zeroed")
        att_done = sem("att_done")
        att_masked = sem("att_masked")
        u_done = sem("u_done")
        s_ready = sem("s_ready")
        o_done = sem("o_done")
        o_copied = sem("o_copied")
        osq_ready = sem("osq_ready")
        oss_ready = sem("oss_ready")
        orinv_ready = sem("orinv_ready")
        o_ready = sem("o_ready")
        state_loaded = [sem(f"state_loaded{u}") for u in range(KU)]
        smask_loaded = sem("smask_loaded")
        si_done = sem("si_done")
        smp_ready = sem("smp_ready")
        vm_ready = sem("vm_ready")
        su_done = sem("su_done")
        su_used = sem("su_used")
        s_copied_u = sem("s_copied_u")
        lb_ready = sem("lb_ready")
        lb_exp = sem("lb_exp")
        s0_stored = sem("s0_stored")
        sp_stored = sem("sp_stored")
        h_done = sem("h_done")
        h_ready = sem("h_ready")
        lgs_ready = sem("lgs_ready")
        rc_done = sem("rc_done")
        rc_copied = sem("rc_copied")
        wx_ready = sem("wx_ready")
        pp_done = sem("pp_done")
        pp_copied = sem("pp_copied")
        xg0_ready = sem("xg0_ready")
        xg_ready = sem("xg_ready")
        pg_scaled = sem("pg_scaled")
        h3_ready = sem("h3_ready")
        fin_ready = sem("fin_ready")
        xn_done = sem("xn_done")
        xn_copied = sem("xn_copied")
        lg_done = sem("lg_done")
        pk_ready = sem("pk_ready")
        gate_done = sem("gate_done")
        pk_exp = sem("pk_exp")
        memb_ready = sem("memb_ready")
        rank_done = sem("rank_done")
        cnt_ready = sem("cnt_ready")
        u_loaded = [sem(f"u_loaded{i}") for i in range(UNITS)]
        u_used = sem("u_used")
        sel_ready = sem("sel_ready")
        selg_ready = sem("selg_ready")
        xs_done = sem("xs_done")
        xs_copied = sem("xs_copied")
        gate_ready = sem("gate_ready")
        sigm_ready = sem("sigm_ready")
        hid_ready = sem("hid_ready")
        xsT_done = sem("xsT_done")
        xsel_copied = sem("xsel_copied")
        hT_done = sem("hT_done")
        hT_copied = sem("hT_copied")
        yr_copied = sem("yr_copied")
        st_done = sem("st_done")
        st_copied = sem("st_copied")
        cb_done = sem("cb_done")
        rows_added = sem("rows_added")
        moe_chain = sem("moe_chain")
        pg_loaded = sem("pg_loaded")
        pg_done = sem("pg_done")
        pg_sig = sem("pg_sig")
        out_copied = [sem(f"out_copied{t}") for t in range(NT)]
        out_stored = sem("out_stored")

        block = ctx.enter_context(nc.Block())

        EARLY = 2
        early_loaded = [sem(f"early_loaded{c}") for c in range(EARLY)]
        early = (s0[:].rearrange("p i b v -> p (i b v)"), aT[:].rearrange("p c t -> p (c t)")[:, 0:UCOLS])
        LOOP_G = 5
        LATE = LOOP_G * G
        LATE_HEADS = (0, 2, 3, 5)
        SQ_LAST = 1 + KD + KD // 2
        SUM_BANK = (7, 0, 5, 5)
        CB_BANKS, CB_LAST = (6, 6, 2, 0), (6, 6, 2, 6)

        def unit_src(e, c):
            if c < KD:
                return io["w_gu"][0, e, c * P:(c + 1) * P, :]
            c = 2 * (c - KD)
            return io["w_dn"][0, e, c * P:(c + 2) * P, :].rearrange("(c p) n -> p c n", p=P)

        def unit_dst(c):
            v = ring[:, c * UCOLS:(c + 1) * UCOLS]
            return v if c < KD else v.rearrange("p (c n) -> p c n", c=2)

        def overflow_blocks(eng, body):
            n = eng.alloc_register(f"blocks_{eng.engine.name}")
            eng.reg_mov(n, E)
            eng.wait_ge(cnt_ready, 1)
            most = eng.value_load(cnt_i[0:1, E:E + 1], min_val=0, max_val=T)
            with eng.If(most > SLOTS):
                with eng.Fori(0, E) as e:
                    c = eng.value_load(cnt_i[0:1, bass.ds(e, 1)], min_val=0, max_val=T)
                    with eng.Fori(1, BLOCKS) as j:
                        with eng.If(c > j * SLOTS):
                            body(eng.snap(n, min_val=E, max_val=E * BLOCKS), e, j)
                            eng.reg_add(n, n, 1)
            return eng.snap(n, min_val=E, max_val=E * BLOCKS)

        @block.sync
        def _(sp):
            cols = [(io["w_in"], c0 + j * P) for c0 in group_cols for j in range(G)]
            cols += [(io["w_out"], j * P) for j in range(KD)]

            def load_cols(i):
                w, c0 = cols[i]
                if i >= WSLOTS:
                    last = i - WSLOTS
                    if last < NZ:
                        sp.wait_ge(z_done, last + 1)
                    else:
                        sp.wait_ge(h_done, last - NZ + 1)
                sp.dma_start(wst[:, i % WSLOTS], w[0, :, c0:c0 + P].rearrange("(c p) n -> p c n", p=P)) \
                    .then_inc(w_loaded[i % WSLOTS], 16)

            def state_dram(gla, hgrn, u):
                if u < PAIRS:
                    return gla[0][:, 2 * u:2 * u + 2].rearrange("b h k v -> (h k) b v")
                return hgrn[0][:, u - PAIRS].rearrange("b k v -> k b v")

            def load_state(u):
                sp.dma_start(states[u], state_dram(io["state_gla"], io["state_hgrn"], u)).then_inc(state_loaded[u], 16)

            for i in range(LATE + G):
                load_cols(i)
                if i == NZ // 2:
                    for u in range(2):
                        load_state(u)
            sp.wait_ge(att_done, HEADS)
            for u in range(2, KU):
                load_state(u)
            for i in range(LATE + G, NZ):
                load_cols(i)
            sp.wait_ge(s_ready, 1)
            sp.dma_start(out[2][0, 0].rearrange("(u h) k v -> (h k) u v", h=2), s_hist[:, 0:PAIRS, NCH - 1, :]) \
                .then_inc(sp_stored, 16)
            sp.dma_start(out[3][0, 0].rearrange("h k v -> k h v"), s_hist[:, PAIRS:KU, NCH - 1, :]).then_inc(sp_stored, 16)
            for h in range(HEADS):
                if h in LATE_HEADS:
                    load_cols(NZ + LATE_HEADS.index(h))
                if h >= GH or h % 2 == 1:
                    u = h // 2 if h < GH else h - GH + PAIRS
                    sp.wait_ge(su_used, h + 1)
                    sp.dma_start(state_dram(out[4], out[5], u), states[u]).then_inc(s0_stored, 16)
            sp.wait_ge(su_done, HEADS)
            sp.dma_start(b_dn, io["b_dn"][0]).then_inc(bdn_loaded, 16)
            sp.wait_ge(o_ready, HEADS)
            sp.wait_ge(sp_stored, 16 * 2)
            sp.wait_ge(s0_stored, 16 * KU)
            for c in range(UNITS):
                if c < KD - WSLOTS:
                    load_cols(NZ + WSLOTS + c)
                sp.dma_start(unit_dst(c), unit_src(0, c)).then_inc(u_loaded[c], 16)

            sp.wait_ge(xn_done, NT)
            for c in range(EARLY):
                sp.dma_start(early[c], unit_src(E - 1, c)).then_inc(early_loaded[c], 16)

            def load_block(n, e, j, first=0):
                for c in range(first, UNITS):
                    sp.wait_ge(u_used, n * UNITS + (c + 1 - UNITS))
                    sp.dma_start(unit_dst(c), unit_src(e, c)).then_inc(u_loaded[c], 16)

            with sp.Fori(1, E - 1) as e:
                load_block(e, e, 0)
            load_block(E - 1, E - 1, 0, first=EARLY)
            n = overflow_blocks(sp, load_block)
            for c in range(KD // 2):
                sp.wait_ge(u_used, n * UNITS + (c + 1 - UNITS))
                sp.dma_start(ring[:, c * UCOLS:(c + 1) * UCOLS].rearrange("p (c n) -> p c n", c=2),
                             io["w_ple_gate"][0, 2 * c * P:(2 * c + 2) * P, :].rearrange("(c p) n -> p c n", p=P)) \
                    .then_inc(pg_loaded, 16)
            for t in range(TT):
                sp.wait_ge(out_copied[t], 1)
                sp.dma_start(out[0][0, t * P:(t + 1) * P, :], tok[:, t, :]).then_inc(out_stored, 16)
            sp.wait_ge(out_copied[TT], 2)
            sp.dma_start(out[1].rearrange("b l d -> (b l) d"), tok[0:S, TT, :]).then_inc(out_stored, 16)
            sp.wait_ge(out_stored, 16 * NT)

        @block.gpsimd
        def _(pool):
            lk = Links(pool, pool_link)
            lk.add(pool.memset(ident[:], 0.0))
            lk.add(pool.memset(ones[:], 1.0))
            lk.add(pool.memset(reset[:], 1.0))
            lk.add(pool.memset(maskf[:], 1.0))
            lk.add(pool.memset(seqmask[:], 1.0))
            lk.add(pool.memset(eps[:], EPS))
            lk.add(pool.memset(bgu[:], 0.0))
            lk.add(pool.iota(iota_i, pattern=[[1, BLOCKS * SLOTS]], base=1, channel_multiplier=0))
            lk.wait()
            pool.affine_select(out=ident[:], in_=ident[:], compare_op=ALU.not_equal, fill=1.0, base=0,
                               pattern=[[-1, P]], channel_multiplier=1).then_inc(consts_ready, 1)
            pool.dma_start(bgu[0:E, :], io["b_gu"][0]).then_inc(bgu_loaded, 16)
            pool.affine_select(out=upper[:], in_=ones[:], compare_op=ALU.is_gt, fill=0.0, base=0,
                               pattern=[[1, P]], channel_multiplier=-1).then_inc(consts_ready, 1)
            pool.memset(reset[:, 0:L].rearrange("p (n c) -> p n c", c=CHUNK)[:, :, 0:1], 0.0).then_inc(consts_ready, 1)
            pool.memset(reset[:, L:T].rearrange("p (n c) -> p n c", c=SL)[:, :, 0:1], 0.0).then_inc(consts_ready, 1)
            lk.add(pool.affine_select(out=maskf[:], in_=maskf[:], compare_op=ALU.is_ge, fill=0.0, base=0,
                                      pattern=[[1, P + 32]], channel_multiplier=-1))
            lk.wait()
            lk.add(pool.memset(maskf[0:CHUNK, CHUNK:P], 0.0))
            lk.add(pool.affine_select(out=maskf[0:32, P:P + 32], in_=ones[0:32, 0:32], compare_op=ALU.is_ge, fill=0.0,
                                      base=0, pattern=[[1, 32]], channel_multiplier=-1))
            lk.wait()
            lk.add(pool.affine_select(out=maskf[0:32, P:P + 32], in_=maskf[0:32, P:P + 32], compare_op=ALU.is_ge,
                                      fill=0.0, base=0, pattern=[[-SL, 32 // SL], [0, SL]], channel_multiplier=1))
            lk.add(pool.affine_select(out=seqmask[:], in_=seqmask[:], compare_op=ALU.is_ge, fill=0.0, base=0,
                                      pattern=[[-SL, SB]], channel_multiplier=1))
            lk.wait()
            pool.affine_select(out=seqmask[:], in_=seqmask[:], compare_op=ALU.is_ge, fill=0.0, base=SL - 1,
                               pattern=[[SL, SB]], channel_multiplier=-1).then_inc(consts_ready, 1)
            pool.wait_ge(consts_ready, 5)
            for j in range(4):
                pool.dma_start(smask[j * S:(j + 1) * S, :], seqmask[:]).then_inc(smask_loaded, 16)
            pool.tensor_copy(maski[:], maskf[:]).then_inc(consts_ready, 1)
            pool.tensor_copy(iota1[:], iota_i).then_inc(consts_ready, 1)
            pool.memset(qr_pad, 0.0).then_inc(consts_ready, 1)
            pool.memset(qb_pad, 0.0).then_inc(consts_ready, 1)
            pool.memset(idx8[:], 0).then_inc(consts_ready, 1)
            pool.memset(top8[:], 0.0).then_inc(consts_ready, 1)
            pool.memset(selT[:], 0.0).then_inc(st_copied, 1)
            pool.wait_ge(qk_ready, 1)
            pool.memset(att, 0.0).then_inc(att_zeroed, 1)
            pool.memset(kend_tok, 0.0).then_inc(att_zeroed, 1)
            for h in range(HEADS):
                if h == 0:
                    pool.wait_ge(v_copied, NT)
                if h >= 2:
                    pool.wait_ge(su_done, h - 1)
                pool.tensor_tensor(vmask[0:S, h % 2], tok[0:S, TT, h * P:(h + 1) * P].unsqueeze(1).to_broadcast([S, SB, P]),
                                   seqmask[0:S, :].unsqueeze(2).to_broadcast([S, SB, P]), ALU.mult).then_inc(vm_ready, 1)
            pool.wait_ge(h_done, KD)
            pool.memset(yrow, 0.0).then_inc(yr_copied, 1)
            pool.wait_ge(rc_done, 1)
            pool.wait_ge(lgs_ready, 1)
            pool.wait_ge(ple_loaded, 16 * 3)
            pool.wait_ge(bdn_loaded, 16)
            with pool.Fori(0, KD) as n:
                pool.tensor_copy(w_pp_chunk, w_pp[:, :, bass.ds(n * P, P)]).then_inc(wx_ready, 1)
                pool.tensor_copy(b_dn_chunk, b_dn[:, bass.ds(n * P, P)]).then_inc(wx_ready, 1)
                pool.wait_ge(pp_done, n + 1)
                pool.wait_ge(bd_done, n + 1)

        @block.scalar
        def _(act):
            lk = Links(act, act_link)
            act.dma_start(tok[:, 0:TT, :], io["x_prompt"][0].rearrange("(t p) d -> p t d", p=P)).then_inc(x_loaded, 16)
            act.dma_start(tok[0:S, TT, :], io["x_sample"].rearrange("b l d -> (b l) d")).then_inc(x_loaded, 16)
            row = 0
            for name, n in (("g_mix", KD), ("g_ffn", KD), ("g_ple", KD), ("g_final", KD), ("b_gk2", PAIRS),
                            ("lb_logits", 2 * HH), ("gn_gla", 1), ("gn_hgrn", 1)):
                a = io[name]
                src = a.rearrange("(r p) -> r p", p=P) if len(a.shape) == 1 else a.rearrange("a (r p) -> (a r) p", p=P)
                act.dma_start(vec_rows[row:row + n, :], src).then_inc(vec_loaded, 16)
                row += n
            act.dma_start(r1w[:], io["w_in"][0, :, c_r1:c_r1 + RANK].rearrange("(c p) n -> p c n", p=P)).then_inc(r1w_loaded, 16)
            act.dma_start(gk2[:], io["w_gk2"][0]).then_inc(r1w_loaded, 16)
            act.dma_start(w_rt[:], io["w_router"][0].rearrange("(c p) n -> p c n", p=P)).then_inc(small_loaded, 16)
            act.dma_start(b_rt[:], io["b_router"][0:1, :].to_broadcast([P, E])).then_inc(small_loaded, 16)
            act.dma_start(p_tok[:, 0:TT, :], io["p_prompt"][0, 0].rearrange("(t p) d -> p t d", p=P)).then_inc(ple_loaded, 16)
            act.dma_start(p_tok[0:S, TT, :], io["p_sample"][0].rearrange("b l d -> (b l) d")).then_inc(ple_loaded, 16)
            act.dma_start(w_pp[:], io["w_ple_proj"][0].rearrange("(c p) n -> p c n", p=P)).then_inc(ple_loaded, 16)

            for c in range(0, KD, 2):
                act.wait_ge(xT_done, c + 1)
                act.copy(hT[:, c, :], ps[:, c, 0:T]).then_inc(xT_copied_a, 1)

            def inv_rms(k):
                act.wait_ge(ss_ready, k + 1)
                to, src = (slice(0, E), slice(E, 2 * E)) if k == 1 else (slice(0, P), slice(0, P))
                lk.add(act.activation(lnbuf[to], ps[src, SUM_BANK[k], 0:T], ACT.Ln, bias=eps[src, 0:1], scale=1.0 / D))
                lk.wait()
                act.activation(rinv[to], lnbuf[to], ACT.Exp, scale=-0.5).then_inc(rinv_ready, 1)

            act.wait_ge(xT_copied_v, KD // 2)
            act.wait_ge(xT_copied_a, KD // 2)
            act.activation(squares, hT[:], ACT.Square).then_inc(sq_ready, 1)
            act.wait_ge(consts_ready, 11)
            inv_rms(0)

            act.wait_ge(lb_ready, 1)
            act.activation(lbt[:, 1:3], lbt[:, 1:3], ACT.Exp).then_inc(lb_exp, 1)
            act.wait_ge(r1_done, 1)
            act.copy(r1T[:], ps[0:RANK, 7, 0:T]).then_inc(r1_copied, 1)
            act.wait_ge(gs_bias, 1)
            lk.add(act.activation(gs[:, 2], gs[:, 1], ACT.Exp, scale=-1.0))
            lk.wait()
            act.activation(gs[:, 2], gs[:, 2], ACT.Ln, bias=ones[:, 0:1], scale=1.0).then_inc(gs_exp, 1)

            def copy_groups(g0, g1):
                with act.Fori(g0, g1) as g:
                    for j in range(G):
                        act.wait_ge(z_done, g * G + (j + 1))
                        act.copy(z[:, bass.ds(g * G + j, 1), :], ps[:, j:j + 1, 0:T]).then_inc(z_copied, 1)

            act.wait_ge(z_copied, G)
            copy_groups(1, 3)
            act.wait_ge(z_copied, 3 * G)
            act.activation(e_q[:, 2:6, :], z[:, Z_Q2:Z_Q2 + G, :], ACT.Sigmoid).then_inc(sig_ready, 1)
            act.activation(e_k[:, 2:6, :], z[:, Z_F2:Z_F2 + G, :], ACT.Sigmoid).then_inc(sig_ready, 1)
            act.wait_ge(forget_ready, 1)
            act.activation(lam[:, PAIRS:KU, :], lam[:, PAIRS:KU, :], ACT.Ln).then_inc(lnf_ready, 1)
            act.wait_ge(cum_ready, 1)
            act.activation(e_b, cum, ACT.Exp).then_inc(e_ready, 1)
            act.wait_ge(d1_ready, 1)
            act.activation(e_q, lam, ACT.Exp).then_inc(e_ready, 1)
            act.activation(e_k, lam, ACT.Exp, scale=-1.0).then_inc(e_ready, 1)
            copy_groups(3, 4)
            act.wait_ge(d3_ready, 1)
            act.activation(e_end, lam, ACT.Exp).then_inc(e_ready, 1)
            copy_groups(4, 5)
            act.wait_ge(z_copied, LATE)
            act.activation(acc[:, 0:G, :], z[:, Z_I2:Z_I2 + G, :], ACT.Sigmoid).then_inc(sig_ready, 1)

            def copy_late(i, bank):
                act.wait_ge(z_done, LATE + i + 1)
                act.copy(z[:, LATE + i, :], ps[:, bank, 0:T]).then_inc(z_copied, 1)

            for i in range(G):
                copy_late(i, (6, 7, 0, 1)[i])
            act.wait_ge(z_copied, LATE + G)
            act.wait_ge(v_ready, 1)
            act.activation(acc[:, 0:G, :], z[:, Z_G1:Z_G1 + G, :], ACT.Sigmoid).then_inc(sig_ready, 1)

            def heads_rinv(i):
                act.wait_ge(oss_ready, 4 * (i + 1))
                a = osq[:, 4 * i:4 * (i + 1), :]
                lk.add(act.activation(a, ps[:, 0:4, 0:T], ACT.Ln, bias=eps[:, 0:1], scale=1.0 / P))
                lk.wait()
                act.activation(a, a, ACT.Exp, scale=-0.5).then_inc(orinv_ready, 1)

            for h in range(HEADS):
                act.wait_ge(o_done, h + 1)
                act.copy(o_raw[:, h, :], ps[:, 4, 0:T]).then_inc(o_copied, 1)
                act.activation(osq[:, h, :], ps[:, 4, 0:T], ACT.Square).then_inc(osq_ready, 1)
                if h in LATE_HEADS:
                    copy_late(G + LATE_HEADS.index(h), 5)
                if h == LATE_HEADS[-1]:
                    act.wait_ge(z_copied, NZ)
                    act.activation(z[:, Z_G2:Z_G2 + G, :], z[:, Z_G2:Z_G2 + G, :], ACT.Sigmoid).then_inc(sig_ready, 1)
                if h % 4 == 0 and h:
                    heads_rinv(h // 4 - 1)
            heads_rinv(HEADS // 4 - 1)

            for c in range(KD):
                act.wait_ge(h_ready, c + 1)
                act.activation(squares[:, c, :], hT[:, c, :], ACT.Square).then_inc(sq_ready, 1)
            inv_rms(1)
            act.wait_ge(rc_done, 1)
            act.copy(rcol[:, 0:TT], ps[:, 1, 0:TT * P:P]).then_inc(rc_copied, 1)
            act.copy(rcol[0:S, TT:NT], ps[0:S, 1, TT * P:TT * P + 1]).then_inc(rc_copied, 1)
            act.wait_ge(rc_copied, 2)
            for t, (t0, n) in enumerate(tiles):
                act.wait_ge(xn_done, t + 1)
                act.activation(tok[0:n, t, :], ps[0:n, 2 + 2 * t:4 + 2 * t, :].rearrange("p b n -> p (b n)"), ACT.Copy,
                               scale=rcol[0:n, t:t + 1]).then_inc(xn_copied, 1)
            act.wait_ge(pk_ready, 1)
            act.activation(pk[:], pk[:], ACT.Exp).then_inc(pk_exp, 1)
            act.wait_ge(gateT_done, 1)
            act.copy(gateT, ps[0:E, 0, 0:T]).then_inc(gateT_copied, 1)

            def expert(n, e, j, extra=False):
                act.wait_ge(xs_done, n + 1)
                act.copy(xrow, ps[:, 2, :]).then_inc(xs_copied, 1)
                act.wait_ge(xsT_done, n + 1)
                act.copy(xsel, ps[:, 3, :]).then_inc(xsel_copied, 1)
                act.wait_ge(gate_ready, n + 1)
                act.activation(sbuf, gbuf, ACT.Sigmoid, scale=SWIGLU_ALPHA).then_inc(sigm_ready, 1)
                act.wait_ge(hT_done, n + 1)
                act.copy(hidT, ps[:, 4, :]).then_inc(hT_copied, 1)
                if extra:
                    act.wait_ge(pp_done, n + 1)
                    act.copy(acc[:, bass.ds(n, 1), :], ps[:, 6:7, 0:T]).then_inc(pp_copied, 1)
                act.wait_ge(st_done, n + 1)
                act.copy(selT[:], ps[:, 4, 0:T]).then_inc(st_copied, 1)
                act.wait_ge(u_used, n * UNITS + UNITS)
                act.copy(yrow, ps[:, 5, :]).then_inc(yr_copied, 1)

            act.wait_ge(st_copied, 1)
            act.wait_ge(yr_copied, 1)
            with act.Fori(0, KD) as e:
                expert(e, e, 0, extra=True)
            with act.Fori(KD, E) as e:
                expert(e, e, 0)
            n = overflow_blocks(act, expert)

            for c in range(KD // 2):
                act.wait_ge(rows_added, n * (KD // 2) + (c + 1))
                act.activation(squares[:, c:KD:KD // 2, :], hT[:, c:KD:KD // 2, :], ACT.Square).then_inc(sq_ready, 1)
            inv_rms(2)
            for c in range(KD):
                act.wait_ge(pg_scaled, c + 1)
                act.activation(pgt[:, c % 2], pgt[:, c % 2], ACT.Sigmoid).then_inc(pg_sig, 1)
                if c:
                    act.wait_ge(h3_ready, c)
                    act.activation(squares[:, c - 1, :], hT[:, c - 1, :], ACT.Square).then_inc(sq_ready, 1)
            act.wait_ge(h3_ready, KD)
            act.activation(squares[:, KD - 1, :], hT[:, KD - 1, :], ACT.Square).then_inc(sq_ready, 1)
            inv_rms(3)
            act.wait_ge(rc_done, 2)
            act.copy(rcol[:, 0:TT], ps[:, 1, 0:TT * P:P]).then_inc(rc_copied, 1)
            act.copy(rcol[0:S, TT:NT], ps[0:S, 1, TT * P:TT * P + 1]).then_inc(rc_copied, 1)
            act.wait_ge(rc_copied, 4)
            act.activation(tok[:, 0, :], ps[:, 6:8, :].rearrange("p b n -> p (b n)"), ACT.Copy, scale=rcol[:, 0:1]) \
                .then_inc(out_copied[0], 1)
            act.activation(tok[0:S, TT, 0:BANK], ps[0:S, 4, :], ACT.Copy, scale=rcol[0:S, TT:NT]).then_inc(out_copied[TT], 1)

        @block.tensor
        def _(pe):
            def mm(o, lhsT, rhs, start, stop):
                return pe.matmul(o, lhsT, rhs, start=start, stop=stop, skip_group_check=True)

            pe.wait_ge(consts_ready, 2)
            pe.wait_ge(x_loaded, 32)
            for c in range(KD):
                for t, (t0, n) in enumerate(tiles):
                    ins = pe.transpose(ps[:, c, t0:t0 + n], tok[0:n, t, c * P:(c + 1) * P], ident[0:n, 0:n])
                ins.then_inc(xT_done, 1)
            pe.wait_ge(vec_loaded, 16 * 8)
            pe.wait_ge(xT_copied_v, 1)
            pe.transpose(ps[:, 1, 0:NV], vec_rows[:], ident[0:NV, 0:NV]).then_inc(vec_done, 1)

            def project_chunk(j, a):
                for c in range(KD):
                    if a is acc and j == 0:
                        pe.wait_ge(xg0_ready, c + 1)
                    ins = mm(ps[:, j, 0:T], wst[:, j, c, :], a[:, c, :], c == 0, c == KD - 1)
                ins.then_inc(z_done, 1)

            pe.wait_ge(xT_copied_a, KD // 2)
            pe.wait_ge(xT_copied_v, KD // 2)
            for j in range(G):
                pe.wait_ge(w_loaded[j], 16)
                project_chunk(j, acc)
                if j == 0:
                    pe.wait_ge(sq_ready, 1)
                    for c in range(KD):
                        ins = mm(ps[:, SUM_BANK[0], 0:T], ones[:], squares[:, c, :], c == 0, c == KD - 1)
                    ins.then_inc(ss_ready, 1)
                if j == G - 2:
                    pe.wait_ge(r1w_loaded, 32)
                    pe.wait_ge(norm_ready, KD)
                    pe.wait_ge(rinv_ready, 1)
                    for c in range(KD):
                        ins = mm(ps[0:RANK, 7, 0:T], r1w[:, c, :], aT[:, c, :], c == 0, c == KD - 1)
                    ins.then_inc(r1_done, 1)
            pe.wait_ge(r1_copied, 1)
            for u in range(PAIRS):
                ins = mm(ps[:, 5 + u, 0:T], gk2[:, u * P:(u + 1) * P], r1T[:], True, True)
            ins.then_inc(gs_done, 1)
            with pe.Fori(1, LOOP_G) as g:
                for j in range(G):
                    pe.wait_ge(w_loaded[j], 16 * (g + 1))
                    pe.wait_ge(z_copied, g * G + (j + 1 - G))
                    project_chunk(j, aT)
            pe.wait_ge(small_loaded, 16 * 2)
            pe.wait_ge(ple_loaded, 16 * 3)
            pe.wait_ge(gs_bias, 1)
            for c in range(PLE // P):
                for t, (t0, n) in enumerate(tiles):
                    ins = pe.transpose(ps[:, 6 + c, t0:t0 + n], p_tok[0:n, t, c * P:(c + 1) * P], ident[0:n, 0:n])
            ins.then_inc(pT_done, 1)
            def project_late(i, bank):
                pe.wait_ge(w_loaded[i % G], 16 * (LOOP_G + i // G + 1))
                for c in range(KD):
                    ins = mm(ps[:, bank, 0:T], wst[:, i % G, c, :], aT[:, c, :], c == 0, c == KD - 1)
                ins.then_inc(z_done, 1)

            pe.wait_ge(qk_ready, 1)
            pe.wait_ge(z_copied, LATE)
            for t, (t0, n) in enumerate(tiles):
                for u in range(KU):
                    ins = pe.transpose(ps[0:n, 2 * t + u // 4, (u % 4) * P:(u % 4 + 1) * P], e_end[:, u, t0:t0 + n], ident[:])
                ins.then_inc(ke_done, 1)
            pe.wait_ge(pT_copied, 1)
            project_late(0, 6)
            pe.wait_ge(v_ready, 1)
            for t, (t0, n) in enumerate(tiles):
                pe.wait_ge(ke_copied, t + 1)
                for c in range(HEADS):
                    ins = pe.transpose(ps[0:n, 2 * t + c // 4, (c % 4) * P:(c % 4 + 1) * P], z[:, Z_V + c, t0:t0 + n], ident[:])
                ins.then_inc(vt_done, 1)
            project_late(1, 7)
            pe.wait_ge(v_copied, NT)
            for h in range(HEADS):
                b = h % 4
                if h >= 4:
                    pe.wait_ge(att_masked, h - 3)
                u = h // 2 if h < GH else h - GH + PAIRS
                q = qr_pad[:, u, h % 2, :] if h < GH else e_q[:, u, :]
                for t, (t0, n) in enumerate(tiles):
                    ins = mm(ps[0:n, b, t0:t0 + n], e_k[:, u, t0:t0 + n], q[:, t0:t0 + n], True, True)
                ins.then_inc(att_done, 1)
            pe.wait_ge(z_copied, LATE + 2)
            k = 0
            for u in range(KU):
                if u == 3:
                    pe.wait_ge(att_masked, HEADS)
                    project_late(2, 0)
                if u == 5:
                    project_late(3, 1)
                heads = 2 if u < PAIRS else 1
                v0 = 2 * u * P if u < PAIRS else (GH + u - PAIRS) * P
                for n0 in range(0, NCH, 2):
                    if k >= 4:
                        pe.wait_ge(s_copied_u, k - 3)
                    for n in (n0, n0 + 1):
                        ins = mm(ps[:, 4 + k % 4, (n - n0) * 2 * P:(n - n0) * 2 * P + heads * P],
                                 kend_tok[:, n // 2, n % 2, u * P:(u + 1) * P], tok[:, n // 2, v0:v0 + heads * P], True, True)
                    ins.then_inc(u_done, 1)
                    k += 1
            def unit(h):
                return h // 2 if h < GH else h - GH + PAIRS

            def q_decayed(h):
                return qb_pad[:, unit(h), h % 2, :] if h < GH else e_b[:, unit(h), :]

            pe.wait_ge(z_copied, LATE + G)
            for i in range(2):
                for h in range(4 * i, 4 * i + 4):
                    pe.wait_ge(state_loaded[unit(h)], 16)
                for half in range(2):
                    for j in range(4):
                        h = 4 * i + j
                        ins = mm(ps[j * S:(j + 1) * S, 2 * i + half, :], q_decayed(h)[:, L:T],
                                 states[unit(h)].rearrange("p b v -> p (b v)")[:, half * BANK:(half + 1) * BANK], True, True)
                ins.then_inc(si_done, 1)

            def head_sums(h):
                pe.wait_ge(osq_ready, h + 1)
                if h == 0:
                    pe.wait_ge(smp_ready, 2)
                if h == 4:
                    pe.wait_ge(orinv_ready, 1)
                mm(ps[:, h % 4, 0:T], ones[:], osq[:, h, :], True, True).then_inc(oss_ready, 1)

            pe.wait_ge(s_ready, 1)
            for h in range(HEADS):
                b = 4
                if h:
                    pe.wait_ge(osq_ready, h)
                    pe.wait_ge(o_copied, h)
                u, qb = unit(h), q_decayed(h)
                for t, (t0, n) in enumerate(tiles):
                    mm(ps[:, b, t0:t0 + n], tok[0:n, t, h * P:(h + 1) * P], att[0:n, h, t0:t0 + n], t == 0, False)
                for n in range(1, NCH):
                    mm(ps[:, b, n * CHUNK:(n + 1) * CHUNK], s_hist[:, u, n - 1, :], qb[:, n * CHUNK:(n + 1) * CHUNK], False, False)
                if h % 4 == 0:
                    pe.wait_ge(smp_ready, h // 4 + 1)
                mm(ps[:, b, L:T], smp[:, h // 4, :], ident[:, (h % 4) * S:(h % 4 + 1) * S], False, True).then_inc(o_done, 1)
                pe.wait_ge(vm_ready, h + 1)
                if h:
                    pe.wait_ge(su_used, h)
                for half in range(2):
                    ins = mm(ps[:, 6 + half, :], kend_smp[0:S, u * P:(u + 1) * P],
                             vmask[0:S, h % 2, half * 4:half * 4 + 4, :].rearrange("p b v -> p (b v)"), True, True)
                ins.then_inc(su_done, 1)
                if h in LATE_HEADS:
                    i = G + LATE_HEADS.index(h)
                    if i > G:
                        pe.wait_ge(z_copied, LATE + i)
                    project_late(i, 5)
                if h >= 1:
                    head_sums(h - 1)
            head_sums(HEADS - 1)

            def stream_chunk(c):
                pe.wait_ge(sq_ready, 1 + c + 1)
                pe.wait_ge(xg_ready, c + 1)
                ins = mm(ps[E:2 * E, SUM_BANK[1], 0:T], ones[:, 0:E], squares[:, c, :], c == 0, c == KD - 1)
                if c == KD - 1:
                    ins.then_inc(ss_ready, 1)
                ins = mm(ps[0:E, 1, 0:T], w_rt[:, c, :], aT[:, c, :], c == 0, c == KD - 1)
                if c == KD - 1:
                    ins.then_inc(lg_done, 1)

            def project_out(c, h0, h1):
                for h in range(h0, h1):
                    ins = mm(ps[:, 4 + c % 4, 0:T], wst[:, (NZ + c) % WSLOTS, h, :], acc[:, h, :], h == 0, h == HEADS - 1)
                return ins

            pe.wait_ge(o_ready, HEADS // 2)
            pe.wait_ge(osq_ready, HEADS)
            pe.wait_ge(o_copied, HEADS)
            for c in range(4):
                if c == 2:
                    pe.wait_ge(su_used, HEADS)
                pe.wait_ge(w_loaded[(NZ + c) % WSLOTS], 16 * (NG + 1))
                project_out(c, 0, HEADS // 2)
            pe.wait_ge(o_ready, HEADS)
            pe.wait_ge(orinv_ready, 2)
            for c in range(4):
                project_out(c, HEADS // 2, HEADS).then_inc(h_done, 1)
            for c in range(4, KD):
                pe.wait_ge(w_loaded[(NZ + c) % WSLOTS], 16 * (NG + 2))
                pe.wait_ge(h_ready, c - 3)
                project_out(c, 0, HEADS).then_inc(h_done, 1)
                stream_chunk(c - 4)
            for c in range(KD - 4, KD):
                stream_chunk(c)
            pe.wait_ge(h_ready, KD)
            for t, (t0, n) in enumerate(tiles):
                for c in range(KD):
                    ins = pe.transpose(ps[0:n, 2 + 2 * t + c // 4, (c % 4) * P:(c % 4 + 1) * P], aT[:, c, t0:t0 + n], ident[:])
                ins.then_inc(xn_done, 1)
            pe.wait_ge(lgs_ready, 1)
            for t, (t0, n) in enumerate(tiles):
                ins = pe.transpose(ps[0:n, 0, t * E:(t + 1) * E], lgs[:, t0:t0 + n], ident[0:E, 0:E])
            ins.then_inc(lg_done, 1)

            def rinv_columns(bank):
                for t, (t0, n) in enumerate(tiles):
                    ins = pe.transpose(ps[0:n, bank, t * P:t * P + E], rinv[0:E, t0:t0 + n], ident[0:E, 0:E])
                ins.then_inc(rc_done, 1)

            rinv_columns(1)
            pe.wait_ge(memb_ready, 1)
            pe.wait_ge(rc_copied, 2)
            for t, (t0, n) in enumerate(tiles):
                for s in range(t + 1):
                    m = tiles[s][1]
                    lhs = upper[0:m, 0:n] if s == t else ones[0:m, 0:n]
                    mm(ps[0:n, 1, t * E:(t + 1) * E], lhs, memb[0:m, s, :], s == 0, s == t)
            for s, (_, m) in enumerate(tiles):
                ins = mm(ps[0:1, 1, NT * E:(NT + 1) * E], ones[0:m, 0:1], memb[0:m, s, :], s == 0, s == NT - 1)
            ins.then_inc(rank_done, 1)
            pe.wait_ge(gate_done, 1)
            for t, (t0, n) in enumerate(tiles):
                ins = pe.transpose(ps[0:E, 0, t0:t0 + n], gate_e[0:n, t, :], ident[0:n, 0:n])
            ins.then_inc(gateT_done, 1)
            pe.wait_ge(gateT_copied, 1)
            pe.wait_ge(cnt_ready, 1)
            pe.wait_ge(xn_copied, NT)
            pe.wait_ge(bdn_loaded, 16)
            pe.wait_ge(bgu_loaded, 16)

            def combine(n, c, banks=CB_BANKS):
                if c == 0:
                    pe.wait_ge(st_copied, n + 1)
                    pe.wait_ge(yr_copied, n + 1)
                elif banks[c] == 6:
                    pe.wait_ge(rows_added, n * (KD // 2) + (c + 1) // 2)
                for half in range(2):
                    r = slice(half * SLOTS, (half + 1) * SLOTS)
                    ins = mm(ps[:, banks[c] + half, 0:T], yrow[r, c * P:(c + 1) * P], selT[r, :], True, True)
                ins.then_inc(cb_done, 1)

            def halves(bank, lhsT, rhs0, rhs1, start, stop):
                mm(ps[0:SLOTS, bank, :], lhsT, rhs0, start, stop)
                return mm(ps[SLOTS:P, bank, :], lhsT, rhs1, start, stop)

            def expert(n, e, j, extra=False, last=False):
                pe.wait_ge(sel_ready, n + 1)
                for t, (t0, m) in enumerate(tiles):
                    ins = halves(2, sel[0:m, t, :], tok[0:m, t, 0:D // 2], tok[0:m, t, D // 2:D], t == 0, t == NT - 1)
                ins.then_inc(xs_done, 1)
                for b in range(2):
                    halves(b, ehot[:], bgu[:, b * FF:b * FF + BANK], bgu[:, b * FF + BANK:(b + 1) * FF], True, False)
                pe.wait_ge(xs_copied, n + 1)
                for c in range(KD // 2):
                    ins = pe.transpose(ps[:, 3, c * P:(c + 1) * P], xrow[:, c * P:(c + 1) * P], ident[:])
                ins.then_inc(xsT_done, 1)
                combine(n, 0)
                pe.wait_ge(xsel_copied, n + 1)
                for c in range(KD):
                    x0 = (c % (KD // 2)) * P + (c // (KD // 2)) * SLOTS
                    w, at_w = ring, c * UCOLS
                    if c >= EARLY:
                        pe.wait_ge(u_loaded[c], n * 16 + 16)
                    elif last:
                        pe.wait_ge(early_loaded[c], 16)
                        w, at_w = early[c], 0
                    else:
                        pe.wait_ge(u_loaded[c], n * 16 + 16 if isinstance(j, int) else n * 16)
                    for b in range(2):
                        w0 = at_w + b * FF
                        ins = halves(b, xsel[:, x0:x0 + SLOTS], w[:, w0:w0 + BANK], w[:, w0 + BANK:w0 + FF],
                                     False, c == KD - 1)
                    ins.then_inc(u_used, 1)
                combine(n, 1)
                combine(n, 2)
                pe.wait_ge(hid_ready, n + 1)
                for c in range(KF // 2):
                    ins = pe.transpose(ps[:, 4, c * P:(c + 1) * P], hid[:, c * P:(c + 1) * P], ident[:])
                ins.then_inc(hT_done, 1)
                combine(n, 3)
                if extra:
                    pe.wait_ge(wx_ready, 2 * n + 2)
                    pe.wait_ge(rows_added, n * (KD // 2) + 2)
                    for k in range(PLE // P):
                        ins = mm(ps[:, 6, 0:T], w_pp_chunk[:, k, :], pT[:, k, :], k == 0, k == PLE // P - 1)
                    ins.then_inc(pp_done, 1)
                    mm(ps[:, 7, 0:T], b_dn_chunk, gateT, True, True).then_inc(bd_done, 1)
                pe.wait_ge(hT_copied, n + 1)
                for c in range(KF // 2):
                    pe.wait_ge(u_loaded[KD + c], n * 16 + 16)
                    for k in range(2):
                        kc = 2 * c + k
                        x0 = (kc % (KF // 2)) * P + (kc // (KF // 2)) * SLOTS
                        w0 = (KD + c) * UCOLS + k * D
                        ins = halves(5, hidT[:, x0:x0 + SLOTS], ring[:, w0:w0 + BANK], ring[:, w0 + BANK:w0 + D],
                                     kc == 0, kc == KF - 1)
                    ins.then_inc(u_used, 1)
                    if c == 1:
                        pe.wait_ge(selg_ready, n + 1)
                        for t, (t0, m) in enumerate(tiles):
                            ins = pe.transpose(ps[:, 4, t0:t0 + m], selg[0:m, t, :, :].rearrange("p a s -> p (a s)"),
                                               ident[0:m, 0:m])
                        ins.then_inc(st_done, 1)
                if extra:
                    pe.wait_ge(pp_copied, n + 1)
                    pe.wait_ge(h_ready, n + (KD + 1))

            with pe.Fori(0, KD) as e:
                expert(e, e, 0, extra=True)
            with pe.Fori(KD, E - 1) as e:
                expert(e, e, 0)
            expert(E - 1, E - 1, 0, last=True)
            n = overflow_blocks(pe, expert)
            pe.wait_ge(rows_added, n * (KD // 2))
            for c in range(KD // 2):
                combine(n, c, CB_LAST)

            def final_chunk(c):
                if c == 0:
                    pe.wait_ge(rinv_ready, 3)
                pe.wait_ge(sq_ready, SQ_LAST + c + 1)
                ins = mm(ps[:, SUM_BANK[3], 0:T], ones[:], squares[:, c, :], c == 0, c == KD - 1)
                if c == KD - 1:
                    ins.then_inc(ss_ready, 1)
                pe.wait_ge(fin_ready, c + 1)
                for t, (t0, n) in enumerate(tiles):
                    if t < TT or c < KD // 2:
                        b = (6, 2, 4)[t] + c // 4
                        pe.transpose(ps[0:n, b, (c % 4) * P:(c % 4 + 1) * P], fin[:, c, t0:t0 + n], ident[:])

            pe.wait_ge(pg_loaded, 16 * (KD // 2))
            for c in range(KD):
                if c >= 2:
                    pe.wait_ge(pg_scaled, c - 1)
                for i in range(KD):
                    k = i // 2 + (i % 2) * (KD // 2)
                    if c == 0:
                        pe.wait_ge(xg_ready, KD + i + 1)
                    ins = mm(ps[:, c % 2, 0:T], ring[:, k * D + c * P:k * D + (c + 1) * P], aT[:, k, :], i == 0, i == KD - 1)
                ins.then_inc(pg_done, 1)
                if c == 0:
                    pe.wait_ge(sq_ready, SQ_LAST)
                    for k in range(KD):
                        ins = mm(ps[:, SUM_BANK[2], 0:T], ones[:], squares[:, k, :], k == 0, k == KD - 1)
                    ins.then_inc(ss_ready, 1)
                if c >= 2:
                    final_chunk(c - 2)
            for c in range(KD - 2, KD):
                final_chunk(c)
            pe.wait_ge(pg_scaled, KD)
            for c in range(KD // 2, KD):
                pe.transpose(ps[0:S, 0, (c % 4) * P:(c % 4 + 1) * P], fin[:, c, L:T], ident[:])
            pe.wait_ge(rinv_ready, 4)
            rinv_columns(1)

        @block.vector
        def _(dve):
            lk = Links(dve, chain)
            for c in range(1, KD, 2):
                dve.wait_ge(xT_done, c + 1)
                dve.tensor_copy(hT[:, c, :], ps[:, c, 0:T]).then_inc(xT_copied_v, 1)
            dve.wait_ge(vec_done, 1)
            dve.tensor_copy(vecT[:], ps[:, 1, 0:NV]).then_inc(vec_copied, 1)
            dve.wait_ge(vec_copied, 1)

            for c in range(KD):
                if c % 2 == 0:
                    dve.wait_ge(xT_copied_a, c // 2 + 1)
                else:
                    dve.wait_ge(xT_copied_v, c // 2 + 1)
                dve.tensor_scalar(acc[:, c, :], hT[:, c, :], vecT[:, V_MIX + c:V_MIX + c + 1], None, ALU.mult).then_inc(xg0_ready, 1)

            l0, l1 = vecT[:, V_LB:V_LB + HH], vecT[:, V_LB + HH:V_LB + 2 * HH]
            lk.add(dve.tensor_tensor(lbt[:, 0], l0, l1, ALU.max))
            lk.wait()
            lk.add(dve.tensor_tensor(lbt[:, 1], l0, lbt[:, 0], ALU.subtract))
            dve.tensor_tensor(lbt[:, 2], l1, lbt[:, 0], ALU.subtract).then_inc(lb_ready, 1)
            dve.wait_ge(xg0_ready, KD)
            dve.wait_ge(rinv_ready, 1)
            for c in range(KD):
                dve.tensor_tensor(aT[:, c, :], acc[:, c, :], rinv[:], ALU.mult).then_inc(norm_ready, 1)
            for j in range(G):
                dve.wait_ge(z_done, j + 1)
                dve.tensor_tensor(z[:, j, :], ps[:, j, 0:T], rinv[:], ALU.mult).then_inc(z_copied, 1)
            dve.wait_ge(gs_done, 1)
            for u in range(PAIRS):
                lk.add(dve.tensor_scalar(gs[:, 0, u, :], ps[:, 5 + u, 0:T], vecT[:, V_BGK + u:V_BGK + u + 1], None, ALU.add))
            lk.wait()
            dve.scalar_tensor_tensor(gs[:, 1], gs[:, 0], -1.0, gs[:, 0], ALU.mult, ALU.max).then_inc(gs_bias, 1)
            dve.wait_ge(gs_exp, 1)
            lk.add(dve.scalar_tensor_tensor(gs[:, 0], gs[:, 0], 0.0, gs[:, 2], ALU.min, ALU.subtract))
            lk.wait()
            lk.add(dve.tensor_scalar(lam[:, 0:PAIRS, :], gs[:, 0], 1.0 / GLA_NORMALIZER, None, ALU.mult))
            dve.wait_ge(lb_exp, 1)
            lk.add(dve.tensor_tensor(lbt[:, 3], lbt[:, 1], lbt[:, 2], ALU.add))
            lk.wait()
            lk.add(dve.reciprocal(lbt[:, 3], lbt[:, 3]))
            lk.wait()
            lk.add(dve.tensor_tensor(lbt[:, 4], lbt[:, 1], lbt[:, 3], ALU.mult))
            lk.wait()
            lk.add(dve.tensor_scalar(lbt[:, 5], lbt[:, 4], -1.0, 1.0, ALU.mult, ALU.add))
            lk.wait()
            dve.wait_ge(sig_ready, 2)
            dve.wait_ge(z_copied, 3 * G)
            q2, f2 = z[:, Z_Q2:Z_Q2 + HH, :], z[:, Z_F2:Z_F2 + HH, :]
            lk.add(dve.tensor_tensor(q2, q2, e_q[:, PAIRS:KU, :], ALU.mult))
            for h in range(HH):
                lk.add(dve.tensor_scalar(lam[:, PAIRS + h, :], e_k[:, PAIRS + h, :], lbt[:, 5, h:h + 1], lbt[:, 4, h:h + 1],
                                         ALU.mult, ALU.add))
            lk.wait()
            dve.tensor_scalar(f2, lam[:, PAIRS:KU, :], -1.0, 1.0, ALU.mult, ALU.add).then_inc(forget_ready, 1)
            dve.wait_ge(lnf_ready, 1)
            for u in range(KU):
                ins = dve.tensor_tensor_scan(cum[:, u, :], reset[:], lam[:, u, :], 0.0, ALU.mult, ALU.add)
            ins.then_inc(cum_ready, 1)
            dve.wait_ge(cum_ready, 1)

            def by_chunk(a):
                return ((a[:, :, 0:L].rearrange("p u (n c) -> p u n c", c=CHUNK), NCH, CHUNK),
                        (a[:, :, L:T].rearrange("p u (n c) -> p u n c", c=SL), SB, SL))

            for (o, n, c), (i, _, _) in zip(by_chunk(lam), by_chunk(cum)):
                ref = i[:, :, :, c // 2:c // 2 + 1].to_broadcast([P, KU, n, c])
                ins = dve.tensor_tensor(o, i, ref, ALU.subtract)
            ins.then_inc(d1_ready, 1)
            dve.wait_ge(e_ready, 1)
            lk.add(dve.tensor_copy(dec[:, :, 0:NCH], e_b[:, :, CHUNK - 1:L:CHUNK]))
            lk.add(dve.tensor_copy(dec[:, :, NCH:NCH + SB], e_b[:, :, L + SL - 1:T:SL]))
            dve.wait_ge(e_ready, 3)
            for (o, n, c), (i, _, _) in zip(by_chunk(lam), by_chunk(cum)):
                last = i[:, :, :, c - 1:c].to_broadcast([P, KU, n, c])
                ins = dve.tensor_tensor(o, last, i, ALU.subtract)
            ins.then_inc(d3_ready, 1)
            for half in range(2):
                r = slice(half * GK, (half + 1) * GK)
                for pad, ex in ((qr_pad, e_q), (qb_pad, e_b)):
                    lk.add(dve.scalar_tensor_tensor(pad[r, :, half, :], z[r, Z_Q1:Z_Q1 + PAIRS, :], float(GK) ** -0.5,
                                                    ex[r, 0:PAIRS, :], ALU.mult, ALU.mult))
            lk.wait()
            for ex in (e_q, e_b):
                lk.add(dve.tensor_tensor(ex[:, PAIRS:KU, :], q2, ex[:, PAIRS:KU, :], ALU.mult))
            dve.wait_ge(e_ready, 4)
            for ex in (e_k, e_end):
                lk.add(dve.tensor_tensor(ex[:, 0:PAIRS, :], z[:, Z_K1:Z_K1 + PAIRS, :], ex[:, 0:PAIRS, :], ALU.mult))
                ins = dve.tensor_tensor(ex[:, PAIRS:KU, :], f2, ex[:, PAIRS:KU, :], ALU.mult)
            ins.then_inc(qk_ready, 1)
            dve.wait_ge(pT_done, 1)
            dve.tensor_copy(pT[:], ps[:, 6:8, 0:T]).then_inc(pT_copied, 1)
            dve.wait_ge(att_zeroed, 2)
            for t, (t0, n) in enumerate(tiles):
                dve.wait_ge(ke_done, t + 1)
                src = ps[:, 2 * t:2 * t + 2, :].rearrange("p b n -> p (b n)")[:, 0:KU * P]
                if t < TT:
                    for half in range(2):
                        r = slice(half * CHUNK, (half + 1) * CHUNK)
                        ins = dve.tensor_copy(kend_tok[r, t, half, :], src[r])
                else:
                    ins = dve.tensor_copy(kend_smp[0:S, :], src[0:S])
                ins.then_inc(ke_copied, 1)
                if t == 0:
                    dve.wait_ge(sig_ready, 3)
                    dve.wait_ge(z_copied, LATE)
                    i2 = z[:, Z_I2:Z_I2 + HH, :]
                    dve.tensor_tensor(i2, i2, acc[:, 0:G, :], ALU.mult).then_inc(v_ready, 1)
            for t, (t0, n) in enumerate(tiles):
                dve.wait_ge(vt_done, t + 1)
                dve.tensor_copy(tok[0:n, t, :], ps[0:n, 2 * t:2 * t + 2, :].rearrange("p b n -> p (b n)")).then_inc(v_copied, 1)
            dve.wait_ge(consts_ready, 11)
            for h in range(HEADS):
                dve.wait_ge(att_done, h + 1)
                for t in range(TT):
                    dve.copy_predicated(att[:, h, t * P:(t + 1) * P], maski[:, 0:P], ps[:, h % 4, t * P:(t + 1) * P])
                dve.copy_predicated(att[0:S, h, L:T], maski[0:S, P:P + S], ps[0:S, h % 4, L:T]).then_inc(att_masked, 1)
            k = 0
            for u in range(KU):
                parts = [(slice(0, GK), 0), (slice(GK, P), P)] if u < PAIRS else [(slice(0, P), 0)]
                for n0 in range(0, NCH, 2):
                    dve.wait_ge(u_done, k + 1)
                    for n in (n0, n0 + 1):
                        if n:
                            lk.wait()
                        for r, v0 in parts:
                            src = ps[r, 4 + k % 4, (n - n0) * 2 * P + v0:(n - n0) * 2 * P + v0 + P]
                            if n == 0:
                                lk.add(dve.tensor_copy(s_hist[r, u, 0, :], src))
                            else:
                                lk.add(dve.scalar_tensor_tensor(s_hist[r, u, n, :], s_hist[r, u, n - 1, :], dec[r, u, n:n + 1],
                                                                src, ALU.mult, ALU.add))
                    lk.wait()
                    dve.nop().then_inc(s_copied_u, 1)
                    k += 1
            dve.nop().then_inc(s_ready, 1)
            dve.wait_ge(smask_loaded, 16 * 4)
            for i in range(2):
                dve.wait_ge(si_done, i + 1)
                lk.wait()
                lk.add(dve.tensor_tensor(smp_tmp, ps[:, 2 * i:2 * i + 2, :].rearrange("p b (s v) -> p (b s) v", v=P),
                                         smask[:].unsqueeze(2).to_broadcast([P, SB, P]), ALU.mult))
                lk.wait()
                dve.tensor_reduce(smp[:, i, :], smp_tmp.rearrange("p b v -> p v b"), AX_X, ALU.add).then_inc(smp_ready, 1)
                dve.wait_ge(smp_ready, i + 1)

            def sample_state(h):
                u = h // 2 if h < GH else h - GH + PAIRS
                st = states[u]
                if h >= GH or h % 2 == 0:
                    lk.add(dve.tensor_tensor(st, st, dec[:, u, NCH:NCH + SB].unsqueeze(2).to_broadcast([P, SB, P]), ALU.mult))
                    lk.wait()
                r = slice((h % 2) * GK, (h % 2 + 1) * GK) if h < GH else slice(0, P)
                dve.wait_ge(su_done, h + 1)
                src = ps[r, 6:8, :].rearrange("p b (s v) -> p (b s) v", v=P)
                dve.tensor_tensor(st[r], st[r], src, ALU.add).then_inc(su_used, 1)

            def head_norm(h):
                dve.wait_ge(orinv_ready, h // 4 + 1)
                gn = vecT[:, V_GN + (h >= GH):V_GN + (h >= GH) + 1]
                lk.add(dve.scalar_tensor_tensor(o_raw[:, h, :], o_raw[:, h, :], gn, osq[:, h, :], ALU.mult, ALU.mult))
                lk.wait()
                dve.tensor_tensor(acc[:, h, :], o_raw[:, h, :], z[:, Z_G1 + h, :], ALU.mult).then_inc(o_ready, 1)

            for h in range(HEADS):
                sample_state(h)
                if h == GH - 1:
                    dve.wait_ge(sig_ready, 4)
                    g1 = z[:, Z_G1:Z_G1 + GH, :]
                    lk.add(dve.tensor_tensor(g1, g1, acc[:, 0:GH, :], ALU.mult))
                    lk.wait()
                if h >= HEADS - 3 and h < HEADS - 1:
                    head_norm(2 * (h - HEADS + 3))
                    head_norm(2 * (h - HEADS + 3) + 1)
            dve.wait_ge(sig_ready, 5)
            for h in range(HEADS // 2, HEADS):
                head_norm(h)
            dve.wait_ge(o_ready, HEADS)
            for c in range(KD):
                dve.wait_ge(h_done, c + 1)
                dve.tensor_tensor(hT[:, c, :], hT[:, c, :], ps[:, 4 + c % 4, 0:T], ALU.add).then_inc(h_ready, 1)
                dve.wait_ge(h_ready, c + 1)
                dve.tensor_scalar(aT[:, c, :], hT[:, c, :], vecT[:, V_FFN + c:V_FFN + c + 1], None, ALU.mult).then_inc(xg_ready, 1)
            dve.wait_ge(lg_done, 1)
            dve.wait_ge(rinv_ready, 2)
            dve.tensor_tensor(lgs, ps[0:E, 1, 0:T], rinv[0:E, :], ALU.mult).then_inc(lgs_ready, 1)
            dve.wait_ge(small_loaded, 16 * 2)
            dve.wait_ge(lg_done, 2)
            for t, (t0, n) in enumerate(tiles):
                lk.add(dve.tensor_tensor(logit[0:n, t, :], ps[0:n, 0, t * E:(t + 1) * E], b_rt[0:n, :], ALU.add))
            lk.wait()
            for t, (t0, n) in enumerate(tiles):
                lk.add(dve.max(top8[0:n, t, :], logit[0:n, t, :]))
            lk.wait()
            for t, (t0, n) in enumerate(tiles):
                lk.add(dve.max_index(idx8[0:n, t, :], top8[0:n, t, :], logit[0:n, t, :]))
            dve.tensor_tensor(pk[:], top8[:, :, 0:TOPK], top8[:, :, 0:1].to_broadcast([P, NT, TOPK]), ALU.subtract) \
                .then_inc(pk_ready, 1)
            lk.wait()
            lk.add(dve.tensor_scalar(idxf[:], idx8[:, :, 0:TOPK], 1.0, None, ALU.add))
            lk.wait()
            lk.add(dve.tensor_tensor(onehot[:].rearrange("p t k e -> p (t k) e"),
                                     iota1[:, 0:E].unsqueeze(1).to_broadcast([P, NT * TOPK, E]),
                                     idxf[:].rearrange("p t k -> p (t k)").unsqueeze(2).to_broadcast([P, NT * TOPK, E]), ALU.is_equal))
            lk.wait()
            dve.tensor_reduce(memb[:], onehot[:].rearrange("p t k e -> p t e k"), AX_X, ALU.add).then_inc(memb_ready, 1)
            dve.wait_ge(pk_exp, 1)
            lk.add(dve.tensor_reduce(psum_k[:, :, 0:1], pk[:], AX_X, ALU.add))
            lk.wait()
            lk.add(dve.reciprocal(psum_k[:, :, 1:2], psum_k[:, :, 0:1]))
            lk.wait()
            lk.add(dve.tensor_tensor(pk[:], pk[:], psum_k[:, :, 1:2].to_broadcast([P, NT, TOPK]), ALU.mult))
            lk.wait()
            lk.add(dve.tensor_tensor(gated[:].rearrange("p t k e -> p (t k) e"), onehot[:].rearrange("p t k e -> p (t k) e"),
                                     pk[:].rearrange("p t k -> p (t k)").unsqueeze(2).to_broadcast([P, NT * TOPK, E]), ALU.mult))
            lk.wait()
            dve.tensor_reduce(gate_e[:], gated[:].rearrange("p t k e -> p t e k"), AX_X, ALU.add).then_inc(gate_done, 1)
            dve.wait_ge(rank_done, 1)
            for t, (t0, n) in enumerate(tiles):
                lk.add(dve.scalar_tensor_tensor(rankp[0:n, t, :], ps[0:n, 1, t * E:(t + 1) * E], 1.0, memb[0:n, t, :],
                                                ALU.add, ALU.mult))
            lk.add(dve.tensor_copy(cnt_f[:, 0:E], ps[0:1, 1, NT * E:(NT + 1) * E]))
            lk.wait()
            lk.add(dve.tensor_reduce(cnt_f[:, E:E + 1], cnt_f[:, 0:E], AX_X, ALU.max))
            lk.wait()
            dve.tensor_copy(cnt_i[:], cnt_f[:]).then_inc(cnt_ready, 1)

            def add_combined(n, c, banks=CB_BANKS):
                b = banks[c]
                dve.wait_ge(cb_done, n * (KD // 2) + (c + 1))
                a = hT[:, c:KD:KD // 2, :]
                dve.tensor_tensor(a, a, ps[:, b:b + 2, 0:T], ALU.add).then_inc(rows_added, 1)

            LINKS = 4

            def expert(n, e, j, extra=False):
                bk = Links(dve, moe_chain, n * LINKS)
                slot = iota1[:, 0:SLOTS] if isinstance(j, int) else iota1[:, bass.ds(j * SLOTS, SLOTS)]
                parts = ((0, TT, P), (TT, NT, S))
                for a, b, m in parts:
                    bk.add(dve.tensor_tensor(sel[0:m, a:b, :], slot[0:m].unsqueeze(1).to_broadcast([m, b - a, SLOTS]),
                                             rankp[0:m, a:b, bass.ds(e, 1)].to_broadcast([m, b - a, SLOTS]), ALU.is_equal))
                bk.wait()
                dve.tensor_copy(ehot[:], ident[:, bass.ds(e, 1)].to_broadcast([P, SLOTS])).then_inc(sel_ready, 1)
                add_combined(n, 0)
                for a, b, m in parts:
                    ins = dve.tensor_tensor(selg[0:m, a:b], sel[0:m, a:b, :].unsqueeze(2).to_broadcast([m, b - a, 2, SLOTS]),
                                            gate_e[0:m, a:b, bass.ds(e, 1)].unsqueeze(2).to_broadcast([m, b - a, 2, SLOTS]),
                                            ALU.mult)
                ins.then_inc(selg_ready, 1)
                dve.wait_ge(u_used, n * UNITS + KD)
                dve.tensor_scalar(gbuf, ps[:, 0, :], SWIGLU_LIMIT, None, ALU.min).then_inc(gate_ready, 1)
                bk.add(dve.tensor_scalar(ubuf, ps[:, 1, :], -SWIGLU_LIMIT, SWIGLU_LIMIT, ALU.max, ALU.min))
                bk.wait()
                bk.add(dve.scalar_tensor_tensor(ubuf, ubuf, 1.0, gbuf, ALU.add, ALU.mult))
                bk.wait()
                dve.wait_ge(sigm_ready, n + 1)
                dve.tensor_tensor(hid, ubuf, sbuf, ALU.mult).then_inc(hid_ready, 1)
                for c in range(1, KD // 2):
                    add_combined(n, c)
                dve.wait_ge(selg_ready, n + 1)
                dve.wait_ge(rows_added, n * (KD // 2) + KD // 2)
                if extra:
                    dve.wait_ge(bd_done, n + 1)
                    a = hT[:, bass.ds(n, 1), :]
                    dve.tensor_tensor(a, a, ps[:, 7:8, 0:T], ALU.add).then_inc(h_ready, 1)
                    dve.wait_ge(h_ready, n + (KD + 1))
                assert bk.n == LINKS

            dve.wait_ge(bgu_loaded, 16)
            with dve.Fori(0, KD) as e:
                expert(e, e, 0, extra=True)
            with dve.Fori(KD, E) as e:
                expert(e, e, 0)
            n = overflow_blocks(dve, expert)
            for c in range(KD // 2):
                add_combined(n, c, CB_LAST)
                dve.wait_ge(rows_added, n * (KD // 2) + (c + 1))
                for k in (c, c + KD // 2):
                    dve.tensor_scalar(aT[:, k, :], hT[:, k, :], vecT[:, V_PLE + k:V_PLE + k + 1], None, ALU.mult) \
                        .then_inc(xg_ready, 1)

            def finish(c):
                dve.wait_ge(pg_sig, c + 1)
                lk.add(dve.tensor_tensor(pgt[:, c % 2], pgt[:, c % 2], acc[:, c, :], ALU.mult))
                lk.wait()
                dve.tensor_tensor(hT[:, c, :], hT[:, c, :], pgt[:, c % 2], ALU.add).then_inc(h3_ready, 1)
                dve.wait_ge(h3_ready, c + 1)
                dve.tensor_scalar(fin[:, c, :], hT[:, c, :], vecT[:, V_FIN + c:V_FIN + c + 1], None, ALU.mult) \
                    .then_inc(fin_ready, 1)

            dve.wait_ge(rinv_ready, 3)
            for c in range(KD):
                dve.wait_ge(pg_done, c + 1)
                dve.tensor_tensor(pgt[:, c % 2], ps[:, c % 2, 0:T], rinv[:], ALU.mult).then_inc(pg_scaled, 1)
                if c:
                    finish(c - 1)
            finish(KD - 1)
            dve.wait_ge(rc_copied, 4)
            dve.tensor_scalar(tok[:, 1, :], ps[:, 2:4, :].rearrange("p b n -> p (b n)"), rcol[:, 1:2], None, ALU.mult) \
                .then_inc(out_copied[1], 1)
            dve.tensor_scalar(tok[0:S, TT, BANK:D], ps[0:S, 0, :], rcol[0:S, TT:NT], None, ALU.mult).then_inc(out_copied[TT], 1)


_INS = ["x_prompt", "x_sample", "p_prompt", "p_sample", "state_gla", "state_hgrn", "g_mix", "w_in", "w_gk2", "b_gk2",
        "gn_gla", "lb_logits", "gn_hgrn", "w_out", "g_ffn", "w_router", "b_router", "w_gu", "b_gu", "w_dn", "b_dn",
        "g_ple", "w_ple_gate", "w_ple_proj", "g_final"]


def kernel(**inputs):
    import numpy as np
    import concourse.bacc as bacc
    from concourse.bass_utils import run_bass_kernel_spmd

    nc = bacc.Bacc("TRN2", target_bir_lowering=False, num_devices=1)
    arrays, io = {}, {}
    for name in _INS:
        a = np.ascontiguousarray(inputs[name])
        arrays[f"in_{name}"] = a
        io[name] = nc.dram_tensor(f"in_{name}", a.shape, mybir.dt.from_np(a.dtype), kind="ExternalInput").ap()
    sg, sh = inputs["state_gla"].shape, inputs["state_hgrn"].shape
    nb = inputs["x_prompt"].shape[0]
    shapes = [inputs["x_prompt"].shape, inputs["x_sample"].shape, (sg[0], nb) + tuple(sg[2:]), (sh[0], nb) + tuple(sh[2:]), sg, sh]
    out = [nc.dram_tensor(f"out_{i}", tuple(s), F32, kind="ExternalOutput").ap() for i, s in enumerate(shapes)]
    build(nc, io, out)
    r = run_bass_kernel_spmd(nc, [arrays], core_ids=[0])
    return tuple(r.results[0][f"out_{i}"] for i in range(len(shapes)))
```
